# Optimizing a Trainium2 kernel written in Bass

```python
import math
import jax
import jax.numpy as jnp
from jax import lax
import numpy as np
import jax, jax.numpy as jnp

D_MODEL = 1024
BATCH = 1
SEQ = 256
DEPTH = 1

N_MOD = 6
EPS = 1e-6
GM_CHUNK = 128
GM_HEAD = 128
GM_GROUPS = D_MODEL // GM_HEAD
GM_WIDTH = GM_GROUPS * GM_HEAD
SSM_INNER = 2 * D_MODEL
SSM_HEAD_DIM = 64
SSM_HEADS = SSM_INNER // SSM_HEAD_DIM
SSM_GROUPS = 8
SSM_STATE = 128
SSM_CONV = 4
SSM_CHUNK = 128
CONV_DIM = SSM_INNER + 2 * SSM_GROUPS * SSM_STATE
D_FF = 4 * D_MODEL
IN_SIZES = (GM_WIDTH, GM_WIDTH, SSM_INNER, CONV_DIM, SSM_HEADS, D_MODEL, D_MODEL)
IN_WIDTH = sum(IN_SIZES)


def _split_offsets(sizes):
    offs, acc = [], 0
    for s in sizes[:-1]:
        acc += s
        offs.append(acc)
    return offs

def rms_norm(x, w=None):
    xf = x.astype(jnp.float32)
    y = xf * lax.rsqrt(jnp.mean(jnp.square(xf), axis=-1, keepdims=True) + EPS)
    if w is not None:
        y = y * w.astype(jnp.float32)
    return y.astype(x.dtype)

def gated_group_rms_norm(y, z, w, groups):
    g = y.astype(jnp.float32) * jax.nn.silu(z.astype(jnp.float32))
    gs = g.reshape(*g.shape[:-1], groups, -1)
    gs = gs * lax.rsqrt(jnp.mean(jnp.square(gs), axis=-1, keepdims=True) + EPS)
    return (gs.reshape(g.shape) * w.astype(jnp.float32)).astype(y.dtype)

def sgu_branch(u, v, norm_w, ws, bs):
    b, s, _ = v.shape
    u = jax.nn.gelu(u)
    v = rms_norm(jax.nn.gelu(v), norm_w)
    vc = v.reshape(b, s // GM_CHUNK, GM_CHUNK, GM_GROUPS, GM_HEAD)
    causal = jnp.tril(jnp.ones((GM_CHUNK, GM_CHUNK), dtype=bool))
    ws_c = jnp.where(causal[None], ws, jnp.zeros_like(ws))
    sv = jnp.einsum('gij,bnjgd->bnigd', ws_c, vc) + bs.T[None, None, :, :, None]
    return u * sv.reshape(b, s, GM_WIDTH)

def ssd_scan(xs, dt, A, Bm, Cm):
    b, s, h, p = xs.shape
    g, n = Bm.shape[-2], Bm.shape[-1]
    hpg = h // g
    q = SSM_CHUNK
    nc = s // q

    def to_chunks(t):
        return jnp.swapaxes(t.reshape(b, nc, q, *t.shape[2:]), 0, 1)

    xdt = (xs.astype(jnp.float32) * dt[..., None]).reshape(b, s, g, hpg, p)
    a = (dt * A).reshape(b, s, g, hpg)
    causal = jnp.tril(jnp.ones((q, q), dtype=bool))

    def step(state, inp):
        x_c, a_c, B_c, C_c = inp
        cum = jnp.cumsum(a_c, axis=1)
        cum_t = jnp.moveaxis(cum, 1, -1)
        seg = cum_t[..., :, None] - cum_t[..., None, :]
        decay = jnp.exp(jnp.where(causal, seg, -jnp.inf))
        cb = jnp.einsum('bign,bjgn->bgij', C_c, B_c)
        y_intra = jnp.einsum('bgij,bghij,bjghp->bighp', cb, decay, x_c)
        y_inter = jnp.einsum('bign,bghpn->bighp', C_c, state) * jnp.exp(cum)[..., None]
        last = cum[:, -1]
        w_end = jnp.exp(last[:, None] - cum)
        new_state = state * jnp.exp(last)[..., None, None] + jnp.einsum(
            'bjgn,bjgh,bjghp->bghpn', B_c, w_end, x_c)
        return new_state, y_intra + y_inter

    state0 = jnp.zeros((b, g, hpg, p, n), jnp.float32)
    _, ys = lax.scan(step, state0, (to_chunks(xdt), to_chunks(a),
                                    to_chunks(Bm.astype(jnp.float32)),
                                    to_chunks(Cm.astype(jnp.float32))))
    return jnp.swapaxes(ys, 0, 1).reshape(b, s, h, p)

def ssd_branch(z, xbc, dt_raw, conv_w, conv_b, dt_bias, a_log, d_skip, norm_w):
    b, s, _ = xbc.shape
    xbc = lax.conv_general_dilated(
        xbc, conv_w[:, None, :], window_strides=(1,), padding=[(SSM_CONV - 1, 0)],
        dimension_numbers=('NWC', 'WIO', 'NWC'), feature_group_count=CONV_DIM) + conv_b
    xbc = jax.nn.silu(xbc)
    gn = SSM_GROUPS * SSM_STATE
    xs = xbc[..., :SSM_INNER].reshape(b, s, SSM_HEADS, SSM_HEAD_DIM)
    Bm = xbc[..., SSM_INNER:SSM_INNER + gn].reshape(b, s, SSM_GROUPS, SSM_STATE)
    Cm = xbc[..., SSM_INNER + gn:].reshape(b, s, SSM_GROUPS, SSM_STATE)
    dt = jax.nn.softplus(dt_raw.astype(jnp.float32) + dt_bias.astype(jnp.float32))
    A = -jnp.exp(a_log.astype(jnp.float32))
    y = ssd_scan(xs, dt, A, Bm, Cm)
    y = y + xs.astype(jnp.float32) * d_skip.astype(jnp.float32)[:, None]
    y = y.reshape(b, s, SSM_INNER).astype(z.dtype)
    return gated_group_rms_norm(y, z, norm_w, SSM_GROUPS)

def first_inputs(seed: int = 0) -> dict:
    key = jax.random.key(seed)
    ks = jax.random.split(key, 22)
    f = jnp.float32
    L = DEPTH

    def nrm(k, shape, fan_in):
        return jax.random.normal(k, shape, f) * (fan_in ** -0.5)

    x = jax.random.normal(ks[0], (BATCH, SEQ, D_MODEL), f)
    c = jax.random.normal(ks[1], (BATCH, D_MODEL), f)
    w_mod = 0.5 * nrm(ks[2], (L, D_MODEL, N_MOD * D_MODEL), D_MODEL)
    b_mod = 0.01 * jax.random.normal(ks[3], (L, N_MOD * D_MODEL), f)
    w_in = nrm(ks[4], (L, D_MODEL, IN_WIDTH), D_MODEL)
    gm_norm_w = 1.0 + 0.05 * jax.random.normal(ks[5], (L, GM_WIDTH), f)
    gm_ws = nrm(ks[6], (L, GM_GROUPS, GM_CHUNK, GM_CHUNK), GM_CHUNK)
    gm_bs = 1.0 + 0.1 * jax.random.normal(ks[7], (L, GM_GROUPS, GM_CHUNK), f)
    conv_w = nrm(ks[8], (L, SSM_CONV, CONV_DIM), SSM_CONV)
    conv_b = 0.01 * jax.random.normal(ks[9], (L, CONV_DIM), f)
    dt0 = jnp.exp(jax.random.uniform(ks[10], (L, SSM_HEADS), f,
                                     minval=math.log(1e-3), maxval=math.log(1e-1)))
    dt_bias = dt0 + jnp.log(-jnp.expm1(-dt0))
    a_log = jnp.log(jax.random.uniform(ks[11], (L, SSM_HEADS), f, minval=1.0, maxval=16.0))
    d_skip = 1.0 + 0.1 * jax.random.normal(ks[12], (L, SSM_HEADS), f)
    ssm_norm_w = 1.0 + 0.05 * jax.random.normal(ks[13], (L, SSM_INNER), f)
    w_branch_gm = nrm(ks[14], (L, GM_WIDTH, D_MODEL), GM_WIDTH)
    w_branch_ssm = nrm(ks[15], (L, SSM_INNER, D_MODEL), SSM_INNER)
    w_out = nrm(ks[16], (L, D_MODEL, D_MODEL), D_MODEL)
    w_ff1 = nrm(ks[17], (L, D_MODEL, D_FF), D_MODEL)
    w_ff2 = nrm(ks[18], (L, D_FF, D_MODEL), D_FF)
    final_norm_w = 1.0 + 0.05 * jax.random.normal(ks[19], (D_MODEL,), f)
    return {'x': x, 'c': c, 'w_mod': w_mod, 'b_mod': b_mod, 'w_in': w_in,
            'gm_norm_w': gm_norm_w, 'gm_ws': gm_ws, 'gm_bs': gm_bs,
            'conv_w': conv_w, 'conv_b': conv_b, 'dt_bias': dt_bias, 'a_log': a_log,
            'd_skip': d_skip, 'ssm_norm_w': ssm_norm_w, 'w_branch_gm': w_branch_gm,
            'w_branch_ssm': w_branch_ssm, 'w_out': w_out, 'w_ff1': w_ff1,
            'w_ff2': w_ff2, 'final_norm_w': final_norm_w}

def first_block(x, c, w_mod, b_mod, w_in, gm_norm_w, gm_ws, gm_bs, conv_w, conv_b,
              dt_bias, a_log, d_skip, ssm_norm_w, w_branch_gm, w_branch_ssm, w_out,
              w_ff1, w_ff2, final_norm_w):
    c_act = jax.nn.silu(c)
    offs = _split_offsets(IN_SIZES)
    for l in range(DEPTH):
        mod = (c_act @ w_mod[l] + b_mod[l])[:, None, :]
        sh1, sc1, g1, sh2, sc2, g2 = jnp.split(mod, N_MOD, axis=-1)
        h = rms_norm(x) * (1.0 + sc1) + sh1
        proj = h @ w_in[l]
        u, v, z, xbc, dt_raw, gate_a, gate_b = jnp.split(proj, offs, axis=-1)
        y_a = sgu_branch(u, v, gm_norm_w[l], gm_ws[l], gm_bs[l])
        y_b = ssd_branch(z, xbc, dt_raw, conv_w[l], conv_b[l], dt_bias[l], a_log[l],
                         d_skip[l], ssm_norm_w[l])
        mixed = (jax.nn.sigmoid(gate_a) * (y_a @ w_branch_gm[l])
                 + jax.nn.sigmoid(gate_b) * (y_b @ w_branch_ssm[l]))
        x = x + g1 * (mixed @ w_out[l])
        h2 = rms_norm(x) * (1.0 + sc2) + sh2
        x = x + g2 * (jnp.square(jax.nn.relu(h2 @ w_ff1[l])) @ w_ff2[l])
    return rms_norm(x, final_norm_w)


MOBA_HEAD_DIM = 64
MOBA_HEADS = (D_MODEL // 2) // MOBA_HEAD_DIM
MOBA_WIDTH = MOBA_HEADS * MOBA_HEAD_DIM
MOBA_BLOCK = 256
MOBA_TOPK = 3
Q_BLOCK = 128
GLA_HEADS = 4
GLA_VAL_DIM = (D_MODEL // 2) // GLA_HEADS
GLA_KEY_DIM = GLA_VAL_DIM // 2
GLA_VWIDTH = GLA_HEADS * GLA_VAL_DIM
GLA_KWIDTH = GLA_HEADS * GLA_KEY_DIM
GLA_GATE_RANK = 16
GLA_GATE_TAU = 16.0
GLA_CHUNK = 64
MIX_WIDTH = MOBA_WIDTH + GLA_VWIDTH
IN_COLS = 3 * MOBA_WIDTH + 2 * GLA_KWIDTH + 2 * GLA_VWIDTH + GLA_GATE_RANK
D_FF_2 = 256 * ((8 * D_MODEL // 3 + 255) // 256)
CONV_WIDTH = 3
ROPE_THETA = 10000.0


def rms_norm_2(x, g):
    xf = x.astype(jnp.float32)
    y = xf * lax.rsqrt(jnp.mean(xf * xf, axis=-1, keepdims=True) + EPS)
    return (y * g.astype(jnp.float32)).astype(x.dtype)

def rope(t, pos):
    hd = t.shape[-1]
    inv_freq = 1.0 / (ROPE_THETA ** (jnp.arange(0, hd, 2, dtype=jnp.float32) / hd))
    ang = pos.astype(jnp.float32)[:, None] * inv_freq[None, :]
    cos = jnp.cos(ang).astype(t.dtype)
    sin = jnp.sin(ang).astype(t.dtype)
    t1, t2 = t[..., : hd // 2], t[..., hd // 2:]
    return jnp.concatenate([t1 * cos - t2 * sin, t2 * cos + t1 * sin], axis=-1)

def moba_attention(q, k, v):
    B, H, S, hd = q.shape
    nb = -(-S // MOBA_BLOCK)
    n_sel = min(MOBA_TOPK, nb)
    pad = nb * MOBA_BLOCK - S
    padw = ((0, 0), (0, 0), (0, pad), (0, 0))
    kp = jnp.pad(k, padw).reshape(B, H, nb, MOBA_BLOCK, hd)
    vp = jnp.pad(v, padw).reshape(B, H, nb, MOBA_BLOCK, hd)
    k_mean = jnp.mean(kp, axis=3)
    q = q * (hd ** -0.5)
    n_qb = S // Q_BLOCK
    gather = jax.vmap(jax.vmap(lambda blocks, idx: blocks[idx]))
    block_ids = jnp.arange(nb)

    def one_query_block(c):
        q0 = c * Q_BLOCK
        qc = lax.dynamic_slice_in_dim(q, q0, Q_BLOCK, axis=2)
        own = q0 // MOBA_BLOCK
        qpos = q0 + jnp.arange(Q_BLOCK)
        gate = jnp.einsum('bhqd,bhnd->bhqn', qc, k_mean).astype(jnp.float32)
        gate = jnp.where((block_ids < own)[None, None, None, :], gate, -jnp.inf)
        top_s, top_i = lax.top_k(gate, n_sel)
        valid = top_s > -jnp.inf
        kg = gather(kp, top_i)
        vg = gather(vp, top_i)
        s_sel = jnp.einsum('bhqd,bhqnkd->bhqnk', qc, kg).astype(jnp.float32)
        s_sel = jnp.where(valid[..., None], s_sel, -jnp.inf)
        s_sel = s_sel.reshape(B, H, Q_BLOCK, n_sel * MOBA_BLOCK)
        k_own = lax.dynamic_index_in_dim(kp, own, axis=2, keepdims=False)
        v_own = lax.dynamic_index_in_dim(vp, own, axis=2, keepdims=False)
        kpos = own * MOBA_BLOCK + jnp.arange(MOBA_BLOCK)
        s_own = jnp.einsum('bhqd,bhkd->bhqk', qc, k_own).astype(jnp.float32)
        s_own = jnp.where(qpos[:, None] >= kpos[None, :], s_own, -jnp.inf)
        p = jax.nn.softmax(jnp.concatenate([s_sel, s_own], axis=-1), axis=-1).astype(v.dtype)
        p_sel = p[..., : n_sel * MOBA_BLOCK].reshape(B, H, Q_BLOCK, n_sel, MOBA_BLOCK)
        p_own = p[..., n_sel * MOBA_BLOCK:]
        return (jnp.einsum('bhqnk,bhqnkd->bhqd', p_sel, vg)
                + jnp.einsum('bhqk,bhkd->bhqd', p_own, v_own))

    out = lax.map(one_query_block, jnp.arange(n_qb))
    return out.transpose(1, 2, 0, 3, 4).reshape(B, H, S, hd)

def gla_attention(q, k, v, log_a):
    B, H, S, dk = q.shape
    dv = v.shape[-1]
    C = GLA_CHUNK
    nc = S // C
    f32 = jnp.float32

    def to_chunks(t):
        return t.astype(f32).reshape(B, H, nc, C, t.shape[-1]).transpose(2, 0, 1, 3, 4)

    qc = to_chunks(q * (dk ** -0.5))
    kc, vc = to_chunks(k), to_chunks(v)
    G = jnp.cumsum(to_chunks(log_a), axis=3)
    causal = jnp.tril(jnp.ones((C, C), dtype=bool))

    def step(state, inp):
        q_, k_, v_, G_ = inp
        diff = G_[:, :, :, None, :] - G_[:, :, None, :, :]
        decay = jnp.exp(jnp.where(causal[None, None, :, :, None], diff, -jnp.inf))
        A = jnp.einsum('bhtd,bhsd,bhtsd->bhts', q_, k_, decay)
        o = (jnp.einsum('bhts,bhsv->bhtv', A, v_)
             + jnp.einsum('bhtd,bhdv->bhtv', q_ * jnp.exp(G_), state))
        G_last = G_[:, :, -1:, :]
        state = (jnp.exp(G_last)[:, :, 0, :, None] * state
                 + jnp.einsum('bhsd,bhsv->bhdv', k_ * jnp.exp(G_last - G_), v_))
        return state, o

    state0 = jnp.zeros((B, H, dk, dv), f32)
    _, o = lax.scan(step, state0, (qc, kc, vc, G))
    return o.transpose(1, 2, 0, 3, 4).reshape(B, H, S, dv)

def causal_dwconv(h, w, b):
    S = h.shape[1]
    hp = jnp.pad(h, ((0, 0), (CONV_WIDTH - 1, 0), (0, 0)))
    return sum(w[j] * hp[:, j:j + S] for j in range(CONV_WIDTH)) + b

def split_heads(t, n_heads):
    B, S, W = t.shape
    return t.reshape(B, S, n_heads, W // n_heads).transpose(0, 2, 1, 3)

def merge_heads(t):
    B, H, S, d = t.shape
    return t.transpose(0, 2, 1, 3).reshape(B, S, H * d)

def second_inputs(seed: int = 0) -> dict:
    key = jax.random.key(seed)
    ks = jax.random.split(key, 16)
    f32 = jnp.float32
    D, L = D_MODEL, DEPTH
    nrm = lambda k, shape, fan: jax.random.normal(k, shape, f32) * (fan ** -0.5)
    return {
        "x": jax.random.normal(ks[0], (BATCH, SEQ, D), f32),
        "attn_norm_g": 1.0 + 0.02 * jax.random.normal(ks[1], (L, D), f32),
        "w_in": nrm(ks[2], (L, D, IN_COLS), D),
        "w_gate_up": nrm(ks[3], (L, GLA_GATE_RANK, GLA_KWIDTH), GLA_GATE_RANK),
        "b_gate": 0.1 * jax.random.normal(ks[4], (L, GLA_KWIDTH), f32),
        "gla_norm_g": 1.0 + 0.02 * jax.random.normal(ks[5], (L, GLA_HEADS, GLA_VAL_DIM), f32),
        "w_out": nrm(ks[6], (L, MIX_WIDTH, D), MIX_WIDTH),
        "ffn_norm_g": 1.0 + 0.02 * jax.random.normal(ks[7], (L, D), f32),
        "w_ffn_up": nrm(ks[8], (L, D, 2 * D_FF_2), D),
        "conv_w": nrm(ks[9], (L, CONV_WIDTH, 2 * D_FF_2), CONV_WIDTH),
        "conv_b": 0.02 * jax.random.normal(ks[10], (L, 2 * D_FF_2), f32),
        "w_ffn_down": nrm(ks[11], (L, D_FF_2, D), D_FF_2),
        "final_norm_g": 1.0 + 0.02 * jax.random.normal(ks[12], (D,), f32),
    }

def second_block(x, attn_norm_g, w_in, w_gate_up, b_gate, gla_norm_g, w_out,
              ffn_norm_g, w_ffn_up, conv_w, conv_b, w_ffn_down, final_norm_g):
    B, S, _ = x.shape
    pos = jnp.arange(S)
    o_mq = 0
    o_mk = o_mq + MOBA_WIDTH
    o_mv = o_mk + MOBA_WIDTH
    o_gq = o_mv + MOBA_WIDTH
    o_gk = o_gq + GLA_KWIDTH
    o_gv = o_gk + GLA_KWIDTH
    o_gr = o_gv + GLA_VWIDTH
    o_gg = o_gr + GLA_VWIDTH
    for l in range(DEPTH):
        xn = rms_norm_2(x, attn_norm_g[l])
        proj = xn @ w_in[l]
        mq = rope(split_heads(proj[..., o_mq:o_mk], MOBA_HEADS), pos)
        mk = rope(split_heads(proj[..., o_mk:o_mv], MOBA_HEADS), pos)
        mv = split_heads(proj[..., o_mv:o_gq], MOBA_HEADS)
        y_moba = merge_heads(moba_attention(mq, mk, mv))
        gq = split_heads(proj[..., o_gq:o_gk], GLA_HEADS)
        gk = split_heads(proj[..., o_gk:o_gv], GLA_HEADS)
        gv = split_heads(proj[..., o_gv:o_gr], GLA_HEADS)
        gr = proj[..., o_gr:o_gg]
        gate_lr = proj[..., o_gg:]
        log_a = jax.nn.log_sigmoid((gate_lr @ w_gate_up[l] + b_gate[l]).astype(jnp.float32)) / GLA_GATE_TAU
        og = gla_attention(gq, gk, gv, split_heads(log_a, GLA_HEADS))
        og = og * lax.rsqrt(jnp.mean(og * og, axis=-1, keepdims=True) + EPS)
        og = og * gla_norm_g[l].astype(jnp.float32)[None, :, None, :]
        y_gla = merge_heads(og).astype(x.dtype) * jax.nn.silu(gr)
        x = x + jnp.concatenate([y_moba, y_gla], axis=-1) @ w_out[l]
        hn = rms_norm_2(x, ffn_norm_g[l])
        h = causal_dwconv(hn @ w_ffn_up[l], conv_w[l], conv_b[l])
        h_gate, h_val = h[..., :D_FF_2], h[..., D_FF_2:]
        x = x + (jax.nn.silu(h_gate) * h_val) @ w_ffn_down[l]
    return rms_norm_2(x, final_norm_g)


def setup_inputs(seed=0):
    out = dict(first_inputs(seed))
    for name, value in second_inputs(seed + 1).items():
        if name != "x":
            out[name + "_2"] = value
    return out


def reference(
    x, c, w_mod, b_mod, w_in, gm_norm_w, gm_ws, gm_bs, conv_w, conv_b, dt_bias, a_log, d_skip,
    ssm_norm_w, w_branch_gm, w_branch_ssm, w_out, w_ff1, w_ff2, final_norm_w, attn_norm_g_2,
    w_in_2, w_gate_up_2, b_gate_2, gla_norm_g_2, w_out_2, ffn_norm_g_2, w_ffn_up_2, conv_w_2,
    conv_b_2, w_ffn_down_2, final_norm_g_2,
):
    x = first_block(
        x, c, w_mod, b_mod, w_in, gm_norm_w, gm_ws, gm_bs, conv_w, conv_b, dt_bias, a_log,
        d_skip, ssm_norm_w, w_branch_gm, w_branch_ssm, w_out, w_ff1, w_ff2, final_norm_w,
    )
    return second_block(
        x, attn_norm_g_2, w_in_2, w_gate_up_2, b_gate_2, gla_norm_g_2, w_out_2, ffn_norm_g_2,
        w_ffn_up_2, conv_w_2, conv_b_2, w_ffn_down_2, final_norm_g_2,
    )


_drawn_inputs = setup_inputs


def setup_inputs(seed=0):
    import zlib

    import numpy as np

    out = dict(_drawn_inputs(seed))
    spreads = {}
    factors = {'gm_norm_w': 8.0,
     'gm_bs': 3.605,
     'conv_b': 8.0,
     'd_skip': 5.008,
     'ssm_norm_w': 4.883,
     'attn_norm_g_2': 3.033,
     'b_gate_2': 2.853,
     'gla_norm_g_2': 6.55,
     'ffn_norm_g_2': 3.97,
     'conv_b_2': 4.075,
     'final_norm_g_2': 2.848}
    for name, (base, spread) in spreads.items():
        noise = np.random.default_rng([zlib.crc32(name.encode()), seed]).standard_normal(out[name].shape)
        drawn = base * np.exp(spread * noise) if base else spread * noise
        out[name] = jnp.asarray(drawn.astype(out[name].dtype))
    for name, factor in factors.items():
        out[name] = (out[name] * factor).astype(out[name].dtype)
    return out
```

```python
from contextlib import ExitStack, contextmanager

import concourse.bass as bass
from concourse import mybir

ALU = mybir.AluOpType
ACT = mybir.ActivationFunctionType
AX_X = mybir.AxisListType.X
F32 = mybir.dt.float32
F32R = mybir.dt.float32r
U32 = mybir.dt.uint32

P = 128
T = 256
TT = T // P
D = 1024
KT = D // P
EPS = 1e-6
NT = 4
SLOTS = 4
GROUPS_SGU = 8
HEADS = 32
SSD_GROUPS = 8
HPG = HEADS // SSD_GROUPS
FF_TILES = 32
GLU_TILES = 22
GLA_HEADS = 4
MOBA_HEADS = 8
LEVELS = [1, 2, 4, 8, 16, 32, 64]
NEG = -3.0e38

_WIDTHS = [("b_mod", 48), ("conv_w", 32 * 4), ("conv_b", 32), ("gm_norm_w", 8), ("ssm_norm_w", 16), ("d_skip", 16),
           ("final_norm_w", 8), ("c", 8), ("attn_g", 8), ("b_gate", 2), ("gla_g", 4), ("ffn_g", 8),
           ("fconv_w", 44 * 3), ("fconv_b", 44), ("final_g", 8), ("dt_bias", 32), ("a_log", 32)]
COL, NCOLS = {}, 0
for _name, _w in _WIDTHS:
    COL[_name] = NCOLS
    NCOLS += _w

STAGES = [("v", 2, 1), ("u", 2, 1), ("xbc", 8, 1), ("zg", 8, 1), ("gm", 2, 1), ("ssm", 2, 2), ("out", 2, 1),
          ("ff1", 8, 1), ("ff2", 2, 4), ("in2", 6, 1), ("out2", 2, 1), ("up", 11, 1), ("down", 2, 3)]
GROUP, _g = {}, 0
for _name, _c, _n in STAGES:
    GROUP[_name] = _g
    _g += _c * _n
MOD_FIRST = 4
N_SPLIT = _g
N_RAW = _g + 12
EVAC_XBC, EVAC_ZG, EVAC_FF1, EVAC_IN2, EVAC_UP = 4, 12, 20, 28, 34
DVE_OUT, DVE_FF2, DVE_OUT2, DVE_DOWN = 4, 6, 8, 10
N_READY = 6
UNITS = 6


def landed_group(g):
    if g < GROUP["zg"]:
        return MOD_FIRST + g
    if g < GROUP["gm"]:
        return MOD_FIRST + GROUP["zg"] + 2 * (g - GROUP["zg"])
    return MOD_FIRST + 8 + g


class Steps:

    def __init__(self, eng, sem):
        self.eng, self.sem, self.base, self.n = eng, sem, 0, 0

    def __call__(self, ins):
        self.n += 1
        ins.then_inc(self.sem, 1)
        self.eng.wait_ge(self.sem, self.base + self.n)

    @contextmanager
    def loop(self, trips, per):
        start = self.n
        with self.eng.Fori(0, trips) as i:
            self.base, self.n = i * per + start, 0
            yield i
            assert self.n == per, self.n
        self.base, self.n = 0, start + trips * per


def spread(ap, axis, n):
    ap = ap.unsqueeze(axis)
    shape = list(ap.shape)
    shape[axis] = n
    return ap.broadcast_to(shape)


def two_blocks(nc, panels, x_t, cols_d, square_d, ws_t, bs_rows, wdt_d, wglr_d, wgu_d, rope_d, levels_d, neg_d, out):
    with ExitStack() as ctx:
        def at(name, kb, shape, dt=F32):
            return nc.alloc_sbuf_tensor_at(name, [P] + shape, dt, offset=16896 + int(kb * 1024))

        def sem(name):
            return ctx.enter_context(nc.semaphore(name))

        raw = at("raw", 0, [SLOTS, 1024])
        w_hi = at("w_hi", 16, [SLOTS, 1024], F32R)
        w_lo = at("w_lo", 32, [SLOTS, 1024], F32R)
        xres = at("xres", 48, [KT, T])
        act_hi = at("act_hi", 56, [KT, T], F32R)
        act_lo = at("act_lo", 64, [KT, T], F32R)
        xbc = at("xbc", 72, [32, T])
        zg = at("zg", 104, [32, T])
        u_sb = at("u_sb", 136, [KT, T])
        v_sb = at("v_sb", 144, [TT, D])
        ya_hi = at("ya_hi", 144, [KT, T], F32R)
        ya_lo = at("ya_lo", 152, [KT, T], F32R)
        yb_hi = at("yb_hi", 104, [16, T], F32R)
        yb_lo = at("yb_lo", 88, [16, T], F32R)
        group_rs = at("group_rs", 136, [8, T])
        conv_acc = at("conv_acc", 152, [2, NT, T])
        conv_in = at("conv_in", 160, [2, NT, T + 3])
        stg = at("stg", 136, [2, 4, T])
        a_upto = at("a_upto", 160, [2, HPG, P])
        decay = at("decay", 164, [2, HPG, P])
        xdt = at("xdt", 168, [2, T])
        c_in = at("c_in", 172, [HPG, P])
        state = at("state", 174, [T])
        xw = at("xw", 175, [T])
        b_tok = at("b_tok", 201, [P])
        cbm = at("cbm", 201.5, [2, P])
        tmp_a = at("tmp_a", 160, [KT, T])
        tmp_b = at("tmp_b", 168, [KT, T])
        ff_hi = at("ff_hi", 72, [FF_TILES, T], F32R)
        ff_lo = at("ff_lo", 104, [FF_TILES, T], F32R)
        relu_sb = at("relu_sb", 136, [2, NT * T])
        sq_sb = at("sq_sb", 144, [2, NT * T])
        q_sb = at("q_sb", 72, [4, T])
        k_sb = at("k_sb", 76, [4, T])
        mv_sb = at("mv_sb", 80, [TT, 512])
        gqk = at("gqk", 84, [4, T])
        gv_sb = at("gv_sb", 88, [TT, 512])
        gr_sb = at("gr_sb", 92, [4, T])
        gd = at("gd", 96, [2, 2 * T])
        gx = at("gx", 100, [2, 2 * T])
        scores_t = at("scores_t", 104, [3, GLA_HEADS, P])
        glog = at("glog", 110, [2, T])
        glr_sb = nc.alloc_sbuf_tensor_at("glr_sb", [16, T], F32, offset=16896 + 112 * 1024)
        gt = at("gt", 113, [3, 2, T])
        og = at("og", 119, [GLA_HEADS, T])
        og2 = at("og2", 123, [GLA_HEADS, T])
        rope_t = at("rope_t", 127, [2, NT, T])
        mix_hi = at("mix_hi", 136, [KT, T], F32R)
        mix_lo = at("mix_lo", 144, [KT, T], F32R)
        prob = at("prob", 152, [6, 512])
        prob_t = at("prob_t", 164, [6, 512])
        glu_hi = at("glu_hi", 72, [GLU_TILES, T], F32R)
        glu_lo = at("glu_lo", 94, [GLU_TILES, T], F32R)
        fconv_in = at("fconv_in", 116, [2, NT, T + 2])
        fconv_acc = at("fconv_acc", 125, [2, NT, T])
        glu_sb = at("glu_sb", 133, [2, 2, T])
        cols = at("cols", 176, [NCOLS])
        square = at("square", 178.25, [4, P])
        ones = at("ones", 180.25, [P])
        avg_d = at("avg_d", 180.75, [P])
        avg_g = at("avg_g", 181.25, [P])
        avg_v = at("avg_v", 181.75, [P])
        modc = at("modc", 182.25, [48])
        silu_c = at("silu_c", 182.5, [8])
        eps = at("eps", 182.625, [1])
        zero8 = at("zero8", 182.6875, [8])
        wst = at("wst", 183, [GROUPS_SGU, P])
        bs_sb = at("bs_sb", 187, [GROUPS_SGU, P])
        rope_sb = at("rope_sb", 183, [2, T])
        level_sb = at("level_sb", 185, [8, P])
        neg_sb = at("neg_sb", 189, [3, P])
        wgu = nc.alloc_sbuf_tensor_at("wgu", [16, 2 * P], F32, offset=16896 + int(190.5 * 1024))
        wdt = at("wdt", 191.5, [KT, HEADS])
        wdt_hi = at("wdt_hi", 192.5, [KT, HEADS], F32R)
        wdt_lo = at("wdt_lo", 193.5, [KT, HEADS], F32R)
        wglr = at("wglr", 191.5, [KT, 16])
        wglr_hi = at("wglr_hi", 192.5, [KT, 16], F32R)
        wglr_lo = at("wglr_lo", 193.5, [KT, 16], F32R)
        dts = at("dts", 194.5, [8, TT, HEADS])
        dt_sb, a_sb, wend = dts[:, 0], dts[:, 1], dts[:, 2, 0]
        mod_acc = at("mod_acc", 196.5, [2, 512])
        rt_sb = at("rt_sb", 202.5, [T])
        rs_sb = at("rs_sb", 203.5, [T])
        conv_t = at("conv_t", 169, [NT, T])
        small = at("small", 204.5, [96])
        exp_a = at("exp_a", 205, [HEADS])
        junk = at("junk", 205.25, [16])
        taps_sb = at("taps_sb", 205.5, [20])
        upto, after, ident, turn = (square[:, i, :] for i in range(4))

        proj_ps = ctx.enter_context(nc.psum_tensor("proj_ps", [P, 2, NT * T], F32))
        aux = ctx.enter_context(nc.psum_tensor("aux", [P, 4, 512], F32))

        landed = [sem(f"landed_{s}") for s in range(SLOTS)]
        hi_done = sem("hi_done")
        taken = sem("taken")
        used = sem("used")
        evac_act = sem("evac_act")
        evac_dve = sem("evac_dve")
        names = {
            "SP or GpSimd or ACT loads": "x_in early_in late_in",
            "an engine's own steps": "act_step dve_step pool_step",
            "memsets and first conversions": "ready padded c_ready wdt_hi_ok wdt_ok ws_masked exp_a_ok",
            "modulation": "mod_mm mod_done",
            "RMS norms": "sq_done ms_mm rt_done rs_done nrm_t nrm_hi nrm_lo mid_ok",
            "SGU": "v_ss v_rt v_ready sgu_mm sgu_y sgu_hi sgu_done",
            "dt": "dt_mm dt_abs dt_exp dt_u dt_ln dt_ok wend_mm wend_ok",
            "convolution": "conv_pool conv_done xbc_done",
            "SSD": "stg_ok upto_ok xw_ok cin_ok t_mm cb_mm seg_mm cum_mm st_mm y_mm xdt_ok cbm_ok m_ok y_ok "
                   "btok_ok decay_ok ecum_ok state_ok",
            "gated group norm": "silu_z sig_ok g_ok g2_ok gsum_mm grt_ok yb_f yb_h yb_ok",
            "mixers' sum": "mix_f mix_h mix_ok",
            "first MLP": "sq_ok ffhi_ok ff_ok",
            "GLA": "wglr_hi_ok wglr_ok glr_mm glr_ok gate_mm gx_abs gx_exp gx_u gx_ln g_log lev_d lev_e lev_x lev_mm lev_ok "
                   "og_mm og_ok og_sq og_ms og_rt gla_f gla_h gla_ok",
            "MoBA": "turn_mm turn_read rope_ok sc_mm max_ok exp_ok p_ok pt_mm pt_ok ym_mm ym_h ym_ok",
            "second MLP": "fpadded fc_pool fc_done fc_silu glu_f glu_h glu_ok",
            "result": "fin_ok stored",
            "a register's wait was carried (read by nobody)": "settled",
        }
        S = {n: sem(n) for line in names.values() for n in line.split()}
        def col(name, k=0, n=1):
            return cols[:, COL[name] + k:COL[name] + k + n]

        def col_at(name, k):
            return cols[:, bass.ds(k + COL[name], 1)]

        block = ctx.enter_context(nc.Block())

        @block.sync
        def _(sp):
            sp.dma_start(cols[:], cols_d).then_inc(S["x_in"], 16)
            sp.dma_start(xres[:], x_t).then_inc(S["x_in"], 16)
            for s in range(SLOTS):
                sp.dma_start(raw[:, s, :], panels[s]).then_inc(landed[s], 16)
            with sp.Fori(1, N_RAW) as i:
                for s in range(SLOTS):
                    sp.wait_ge(taken, i * SLOTS + (s + 1 - SLOTS))
                    sp.dma_start(raw[:, s, :], panels[bass.ds(i * SLOTS + s, 1)].rearrange("a p n -> p (a n)")
                                 ).then_inc(landed[s], 16)
            for h in range(2):
                sp.wait_ge(S["fin_ok"], h + 1)
                sp.dma_start(out[:, 4 * h:4 * h + 4, :], tmp_b[:, 4 * h:4 * h + 4, :]).then_inc(S["stored"], 16)
            sp.wait_ge(S["stored"], 32)

        def need(eng, s, value):
            if not isinstance(value, int) or value > 0:
                eng.wait_ge(s, value)

        def settle(eng):
            eng.sem_inc(S["settled"], 1)

        def flat(ap):
            return ap.rearrange("p a b -> p (a b)")

        @block.gpsimd
        def _(pool):
            step = Steps(pool, S["pool_step"])
            for dst, src in ((square, square_d), (wst, ws_t), (bs_sb, bs_rows), (wdt, wdt_d)):
                pool.dma_start(dst[:], src).then_inc(S["early_in"], 16)
            pool.wait_ge(S["early_in"], 64)
            nc.gpsimd.affine_select(out=wst[:], in_=wst[:], pattern=[[0, GROUPS_SGU], [1, P]], base=0,
                                    channel_multiplier=-1, compare_op=ALU.is_ge, fill=0.0).then_inc(S["ws_masked"], 1)

            def two_taps(dst, src, taps, scale, bias, conv_t, done):
                nc.gpsimd.tensor_scalar(out=dst, in0=src[:, taps - 1:taps - 1 + T], scalar1=scale(taps - 1), scalar2=bias,
                                        op0=ALU.mult, op1=ALU.add)
                step(nc.gpsimd.tensor_scalar(out=conv_t, in0=src[:, taps - 2:taps - 2 + T], scalar1=scale(taps - 2),
                                             scalar2=0.0, op0=ALU.mult, op1=ALU.add))
                nc.gpsimd.tensor_tensor(out=dst, in0=dst, in1=conv_t, op=ALU.add).then_inc(done, 1)

            def chunk_taps(c, name, taps):
                for at_col, where, width in ((0, name + "_w", NT * taps), (16, name + "_b", NT)):
                    src = cols[:, bass.ds(c * width + COL[where], width)] if not isinstance(c, int) else col(where, c * width, width)
                    settle(pool)
                    last = nc.gpsimd.tensor_copy(taps_sb[:, at_col:at_col + width], src)
                step(last)
                settle(pool)

            def conv_chunk(c, par):
                pool.wait_ge(evac_act, EVAC_XBC + c + 1)
                need(pool, S["xbc_done"], c)
                need(pool, S["conv_pool"], c * NT)
                chunk_taps(c, "conv", 4)
                for nt in range(NT):
                    two_taps(conv_acc[:, par, nt], conv_in[:, par, nt], 4,
                             lambda j: taps_sb[:, 4 * nt + j:4 * nt + j + 1], taps_sb[:, 16 + nt:17 + nt], conv_t[:, nt], S["conv_pool"])

            per = NT + 1
            conv_chunk(0, 0)
            with step.loop(3, 2 * per) as i:
                conv_chunk(i * 2 + 1, 1)
                conv_chunk(i * 2 + 2, 0)
            conv_chunk(7, 1)

            def ssd_side(g, par):
                pool.wait_ge(S["y_ok"], g + 1)
                settle(pool)
                nc.gpsimd.tensor_copy(stg[:, par, 0:2], xbc[:, bass.ds(g * 2, 2), :])
                nc.gpsimd.tensor_copy(stg[:, par, 2:3], xbc[:, bass.ds(g + 16, 1), :])
                nc.gpsimd.tensor_copy(stg[:, par, 3:4], xbc[:, bass.ds(g + 24, 1), :]).then_inc(S["stg_ok"], 1)
                for c in range(2):
                    pool.wait_ge(S["seg_mm"], g * 2 + (c + 1))
                    if c == 1:
                        pool.wait_ge(S["cum_mm"], g + 1)
                    settle(pool)
                    nc.gpsimd.tensor_tensor(out=a_upto[:, c], in0=spread(dts[:, 1, c, bass.ds(g * HPG, HPG)], 2, P),
                                            in1=spread(upto, 1, HPG), op=ALU.mult).then_inc(S["upto_ok"], 1)
                pool.wait_ge(S["xdt_ok"], g + 1)
                settle(pool)
                nc.gpsimd.tensor_tensor(out=xw[:].rearrange("p (h d) -> p h d", h=HPG),
                                        in0=xdt[:, 0].rearrange("p (h d) -> p h d", h=HPG),
                                        in1=spread(dts[:, 2, 0, bass.ds(g * HPG, HPG)], 2, 64),
                                        op=ALU.mult).then_inc(S["xw_ok"], 1)
                pool.wait_ge(S["ecum_ok"], g + 2)
                nc.gpsimd.tensor_tensor(out=c_in[:], in0=c_in[:], in1=spread(stg[:, par, 3, P:T], 1, HPG),
                                        op=ALU.mult).then_inc(S["cin_ok"], 1)

            pool.wait_ge(S["xbc_done"], 8 + 1)
            pool.wait_ge(S["dt_ok"], 1)
            pool.wait_ge(S["wend_ok"], 1)
            pool.wait_ge(S["sgu_y"], 2)
            pool.wait_ge(S["sgu_done"], 1)
            with pool.Fori(0, 4) as i:
                ssd_side(i * 2, 0)
                ssd_side(i * 2 + 1, 1)

            q_all = flat(gqk[:, 0:2])
            k_all = flat(gqk[:, 2:4])
            for e, m in enumerate(LEVELS + [P]):
                halves = lambda ap: ap.rearrange("p (n m) -> p n m", m=2 * m)
                pool.wait_ge(S["lev_e"], e + 1)
                if e >= 2:
                    pool.wait_ge(S["lev_mm"], e)
                nc.gpsimd.tensor_tensor(out=halves(gx[:, e % 2])[:, :, m:2 * m], in0=halves(q_all)[:, :, m:2 * m],
                                        in1=halves(gd[:, e % 2])[:, :, m:2 * m], op=ALU.mult)
                nc.gpsimd.tensor_tensor(out=halves(gx[:, e % 2])[:, :, 0:m], in0=halves(k_all)[:, :, 0:m],
                                        in1=halves(gd[:, e % 2])[:, :, 0:m], op=ALU.mult).then_inc(S["lev_x"], 1)

            def fconv_chunk(c, par):
                pool.wait_ge(evac_act, EVAC_UP + c + 1)
                need(pool, S["glu_f"], c)
                need(pool, S["fc_pool"], c * NT)
                chunk_taps(c, "fconv", 3)
                for nt in range(NT):
                    two_taps(fconv_acc[:, par, nt], fconv_in[:, par, nt], 3,
                             lambda j: taps_sb[:, 3 * nt + j:3 * nt + j + 1], taps_sb[:, 16 + nt:17 + nt], conv_t[:, nt], S["fc_pool"])

            fconv_chunk(0, 0)
            with step.loop(5, 2 * per) as i:
                fconv_chunk(i * 2 + 1, 1)
                fconv_chunk(i * 2 + 2, 0)

        @block.scalar
        def _(act):
            def split_hi(g, s, rg=None):
                rg = landed_group(g) if rg is None else rg
                act.wait_ge(landed[s], rg * 16 + 16)
                need(act, used, g * SLOTS + (s + 1 - SLOTS))
                nc.scalar.copy(w_hi[:, s, :], raw[:, s, :]).then_inc(hi_done, 1)

            def split_all(g, rg=None):
                for s in range(SLOTS):
                    split_hi(g, s, rg)

            def evac(dst, g, par, func=ACT.Copy, scale=1.0):
                act.wait_ge(used, g * SLOTS + SLOTS)
                if not isinstance(g, int):
                    settle(act)
                src = proj_ps[:, par].rearrange("p (n t) -> p n t", n=dst.shape[1])
                return nc.scalar.activation(dst, src, func, scale=scale).then_inc(evac_act, 1)

            def squares(n, h):
                nc.scalar.activation(tmp_b[:, 4 * h:4 * h + 4], xres[:, 4 * h:4 * h + 4], ACT.Square).then_inc(S["sq_done"], 1)

            def root(n):
                act.wait_ge(S["ms_mm"], n + 1)
                nc.scalar.activation(rt_sb[:], aux[:, 2, 0:T], ACT.Sqrt, bias=eps[:]).then_inc(S["rt_done"], 1)

            def norm_hi(a, shift):
                for k in range(KT):
                    act.wait_ge(S["nrm_t"], KT * a + k + 1)
                    nc.scalar.activation(act_hi[:, k], tmp_a[:, k], ACT.Identity, bias=shift(k)).then_inc(S["nrm_hi"], 1)

            act.wait_ge(S["x_in"], 32)
            nc.scalar.activation(silu_c[:], col("c", 0, 8), ACT.Silu).then_inc(S["c_ready"], 1)
            nc.scalar.activation(exp_a[:], col("a_log", 0, HEADS), ACT.Exp).then_inc(S["exp_a_ok"], 1)
            for h in range(2):
                squares(0, h)
            act.wait_ge(S["ready"], N_READY)
            root(0)
            act.wait_ge(S["early_in"], 64)
            nc.scalar.copy(wdt_hi[:], wdt[:]).then_inc(S["wdt_hi_ok"], 1)
            norm_hi(0, lambda k: modc[:, k:k + 1])
            split_all(0)
            for j in range(2):
                split_all(GROUP["v"] + j + 1)
                evac(v_sb[:, :, 512 * j:512 * j + 512], GROUP["v"] + j, j, ACT.Gelu_apprx_tanh)
            act.wait_ge(evac_act, 2)
            for t in range(TT):
                nc.scalar.activation(flat(tmp_b[:, 4 * t:4 * t + 4]), v_sb[:, t], ACT.Square,
                                     accum_out=small[:, t:t + 1]).then_inc(S["v_ss"], 1)
            act.wait_ge(S["v_ss"], 2)
            nc.scalar.activation(small[:, 2:4], small[:, 0:2], ACT.Sqrt, bias=eps[:], scale=1.0 / D).then_inc(S["v_rt"], 1)
            for j in range(2):
                split_all(GROUP["u"] + j + 1)
                evac(u_sb[:, 4 * j:4 * j + 4], GROUP["u"] + j, j, ACT.Gelu_apprx_tanh)
            act.wait_ge(S["dt_abs"], 1)
            nc.scalar.activation(dts[:, 5], dts[:, 4], ACT.Exp, scale=-1.0).then_inc(S["dt_exp"], 1)
            act.wait_ge(S["dt_u"], 1)
            nc.scalar.activation(dts[:, 7], dts[:, 6], ACT.Ln).then_inc(S["dt_ln"], 1)
            act.wait_ge(S["padded"], 1)

            def conv_silu(c, par, fixed):
                act.wait_ge(S["conv_done"], c * NT + (NT + NT))
                dst = xbc[:, 4 * c:4 * c + 4] if fixed else xbc[:, bass.ds(c * NT, NT), :]
                settle(act)
                nc.scalar.activation(dst, conv_acc[:, par], ACT.Silu).then_inc(S["xbc_done"], 1)

            def conv_step(c, par, fixed=False):
                split_all(c + (GROUP["xbc"] + 1), c + (landed_group(GROUP["xbc"]) + 1))
                need(act, S["conv_done"], c * NT)
                evac(conv_in[:, par, :, 3:3 + T], c + GROUP["xbc"], par)
                if not fixed or c > 0:
                    conv_silu(c - 1, 1 - par, fixed)

            conv_step(0, 0, True)
            with act.Fori(0, 3) as i:
                conv_step(i * 2 + 1, 1)
                conv_step(i * 2 + 2, 0)
            conv_step(7, 1, True)
            conv_silu(7, 1, True)
            act.wait_ge(S["wend_mm"], 1)
            nc.scalar.activation(dts[:, 2, 0], aux[:, 0, 0:HEADS], ACT.Exp).then_inc(S["wend_ok"], 1)
            act.wait_ge(S["sgu_y"], 2)
            nc.scalar.copy(ya_hi[:], u_sb[:]).then_inc(S["sgu_hi"], 1)
            act.wait_ge(S["sgu_done"], 1)
            act.wait_ge(S["wdt_ok"], 1)
            act.wait_ge(S["dt_mm"], 1)
            for dst, src in ((rope_sb, rope_d), (level_sb, levels_d), (neg_sb, neg_d), (wgu, wgu_d), (wglr, wglr_d)):
                act.dma_start(dst[:], src).then_inc(S["late_in"], 16)

            def ssd_act(g, par):
                act.wait_ge(S["cb_mm"], g + 1)
                nc.scalar.copy(b_tok[:], aux[:, 1, T:T + P]).then_inc(S["btok_ok"], 1)
                for c in range(2):
                    act.wait_ge(S["seg_mm"], g * 2 + (c + 3))
                    nc.scalar.activation(flat(decay[:, c]), aux[:, 2 + c], ACT.Exp).then_inc(S["decay_ok"], 1)
                nxt, landed_nxt = g + (GROUP["zg"] + 1), g * 2 + (landed_group(GROUP["zg"]) + 2)
                split_hi(nxt, 0, landed_nxt)
                act.wait_ge(S["cum_mm"], g + 2)
                nc.scalar.activation(flat(c_in[:]), aux[:, 0], ACT.Exp).then_inc(S["ecum_ok"], 1)
                split_hi(nxt, 1, landed_nxt)
                act.wait_ge(S["st_mm"], g + 1)
                nc.scalar.copy(state[:], aux[:, 1, 0:T]).then_inc(S["state_ok"], 1)
                split_hi(nxt, 2, landed_nxt)
                split_hi(nxt, 3, landed_nxt)
                evac(zg[:, bass.ds(g * NT, NT), :], g + GROUP["zg"], par)

            with act.Fori(0, 4) as i:
                ssd_act(i * 2, 0)
                ssd_act(i * 2 + 1, 1)
            act.wait_ge(evac_act, EVAC_ZG + 8)
            for q in range(4):
                nc.scalar.activation(zg[:, 4 * q:4 * q + 4], zg[:, 4 * q:4 * q + 4], ACT.Silu).then_inc(S["silu_z"], 1)
            nc.scalar.activation(zg[:, 16:32], zg[:, 16:32], ACT.Sigmoid).then_inc(S["sig_ok"], 1)
            split_hi(GROUP["gm"] + 1, 0)
            for q in range(4):
                act.wait_ge(S["g_ok"], q + 1)
                nc.scalar.activation(zg[:, 4 * q:4 * q + 4], xbc[:, 4 * q:4 * q + 4], ACT.Square).then_inc(S["g2_ok"], 1)
            for s in range(1, SLOTS):
                split_hi(GROUP["gm"] + 1, s)
            for q in range(4):
                act.wait_ge(S["gsum_mm"], q + 1)
                nc.scalar.activation(flat(group_rs[:, 2 * q:2 * q + 2]), aux[:, q], ACT.Sqrt, bias=eps[:]).then_inc(S["grt_ok"], 1)
            for q in range(4):
                act.wait_ge(S["yb_f"], q + 1)
                nc.scalar.copy(yb_hi[:, 4 * q:4 * q + 4], xbc[:, 4 * q:4 * q + 4]).then_inc(S["yb_h"], 1)
            split_all(GROUP["ssm"])
            for j in range(2):
                split_all(GROUP["ssm"] + 2 * j + 1)
                split_all(GROUP["ssm"] + 2 * j + 2)
                act.wait_ge(S["mix_f"], j + 1)
                nc.scalar.copy(act_hi[:, 4 * j:4 * j + 4], zg[:, 16 + 4 * j:20 + 4 * j]).then_inc(S["mix_h"], 1)
            for j in range(2):
                split_all(GROUP["out"] + j + 1)
                act.wait_ge(evac_dve, DVE_OUT + j + 1)
                squares(1, j)
            root(1)
            norm_hi(1, lambda k: modc[:, 24 + k:25 + k])
            def ff1_step(c, par):
                split_all(c + (GROUP["ff1"] + 1), c + (landed_group(GROUP["ff1"]) + 1))
                evac(relu_sb[:, par].rearrange("p (n t) -> p n t", n=NT), c + GROUP["ff1"], par, ACT.Relu)
                act.wait_ge(S["sq_ok"], c + 1)
                settle(act)
                nc.scalar.copy(ff_hi[:, bass.ds(c * NT, NT), :], sq_sb[:, par].rearrange("p (n t) -> p n t", n=NT)
                               ).then_inc(S["ffhi_ok"], 1)

            with act.Fori(0, 4) as i:
                ff1_step(i * 2, 0)
                ff1_step(i * 2 + 1, 1)
            for j in range(2):
                for g in range(4):
                    split_all(GROUP["ff2"] + 4 * j + g + 1)
                act.wait_ge(evac_dve, DVE_FF2 + j + 1)
                squares(2, j)
            root(2)
            for h in range(2):
                act.wait_ge(S["mid_ok"], h + 1)
                squares(3, h)
            root(3)
            norm_hi(2, lambda k: zero8[:, k:k + 1])
            act.wait_ge(S["late_in"], 80)
            nc.scalar.copy(wglr_hi[:], wglr[:]).then_inc(S["wglr_hi_ok"], 1)

            i2 = GROUP["in2"]

            def level_exp(e):
                m = (LEVELS + [P])[e]
                view = gd[:, e % 2].rearrange("p (n m) -> p n m", m=2 * m)
                act.wait_ge(S["lev_d"], e + 1)
                nc.scalar.activation(view[:, :, m:2 * m], view[:, :, m:2 * m], ACT.Exp)
                nc.scalar.activation(view[:, :, 0:m], view[:, :, 0:m], ACT.Exp, scale=-1.0).then_inc(S["lev_e"], 1)

            split_all(i2 + 1)
            act.wait_ge(used, i2 * SLOTS + SLOTS)
            nc.scalar.activation(gqk[:, 0:2], proj_ps[:, 0, 0:2 * T].rearrange("p (n t) -> p n t", n=2), ACT.Copy, scale=0.125)
            nc.scalar.activation(gqk[:, 2:4], proj_ps[:, 0, 2 * T:].rearrange("p (n t) -> p n t", n=2), ACT.Copy).then_inc(evac_act, 1)
            split_all(i2 + 2)
            evac(gv_sb[:], i2 + 1, 1)
            act.wait_ge(S["glr_mm"], 1)
            nc.scalar.copy(glr_sb[:], aux[0:16, 0, 0:T]).then_inc(S["glr_ok"], 1)
            split_hi(i2 + 3, 0)
            split_hi(i2 + 3, 1)
            act.wait_ge(S["gx_abs"], 1)
            nc.scalar.activation(gt[:, 1], gt[:, 0], ACT.Exp, scale=-1.0).then_inc(S["gx_exp"], 1)
            act.wait_ge(S["gx_u"], 1)
            nc.scalar.activation(glog[:], gt[:, 2], ACT.Ln).then_inc(S["gx_ln"], 1)
            level_exp(0)
            split_hi(i2 + 3, 2)
            split_hi(i2 + 3, 3)
            evac(gr_sb[:], i2 + 2, 0, ACT.Silu)
            for s in range(SLOTS):
                level_exp(s + 1)
                split_hi(i2 + 4, s)
            evac(mv_sb[:], i2 + 3, 1)
            for s in range(SLOTS):
                if s + 5 < len(LEVELS) + 1:
                    level_exp(s + 5)
                split_hi(i2 + 5, s)
            evac(q_sb[:], i2 + 4, 0)
            split_hi(i2 + 6, 0)
            split_hi(i2 + 6, 1)
            act.wait_ge(S["og_mm"], 1)
            nc.scalar.copy(og[:], aux[:, 2:4].rearrange("p b (n t) -> p (b n) t", n=2)).then_inc(S["og_ok"], 1)
            act.wait_ge(S["og_ok"], 1)
            nc.scalar.activation(og2[:], og[:], ACT.Square).then_inc(S["og_sq"], 1)
            split_hi(i2 + 6, 2)
            split_hi(i2 + 6, 3)
            evac(k_sb[:], i2 + 5, 1)
            act.wait_ge(S["og_ms"], 1)
            nc.scalar.activation(og2[:], aux[:, 0:2].rearrange("p b (n t) -> p (b n) t", n=2), ACT.Sqrt, bias=eps[:]).then_inc(S["og_rt"], 1)
            act.wait_ge(S["gla_f"], 1)
            nc.scalar.copy(mix_hi[:, 0:4], og[:]).then_inc(S["gla_h"], 1)
            for w in range(UNITS + 1):
                if w < UNITS:
                    act.wait_ge(S["max_ok"], w + 1)
                    n = 4 if w < 2 else 2
                    for h in range(n):
                        part = prob[:, w, h * (512 // n):(h + 1) * (512 // n)]
                        last = nc.scalar.activation(part, part, ACT.Exp, bias=small[:, 32 + 4 * w + h:33 + 4 * w + h], scale=0.125,
                                                    accum_out=small[:, 64 + 4 * w + h:65 + 4 * w + h])
                    last.then_inc(S["exp_ok"], 1)
                if w > 0:
                    act.wait_ge(S["pt_mm"], w)
                    nc.scalar.copy(prob_t[:, w - 1], aux[:, 2 + (w - 1) % 2]).then_inc(S["pt_ok"], 1)
            act.wait_ge(S["ym_mm"], 1)
            nc.scalar.copy(flat(mix_hi[:, 4:8]), proj_ps[:, 1]).then_inc(S["ym_h"], 1)
            for j in range(2):
                split_all(GROUP["out2"] + j + 1)
                act.wait_ge(evac_dve, DVE_OUT2 + j + 1)
                squares(4, j)
            root(4)
            norm_hi(3, lambda k: zero8[:, k:k + 1])
            act.wait_ge(S["fpadded"], 1)

            def glu_act(c, par, fixed):
                act.wait_ge(S["fc_done"], c * NT + (NT + NT))
                nc.scalar.activation(fconv_acc[:, par, 0:2], fconv_acc[:, par, 0:2], ACT.Silu).then_inc(S["fc_silu"], 1)
                act.wait_ge(S["glu_f"], c + 2)
                settle(act)
                dst = glu_hi[:, 2 * c:2 * c + 2] if fixed else glu_hi[:, bass.ds(c * 2, 2), :]
                nc.scalar.copy(dst, glu_sb[:, par]).then_inc(S["glu_h"], 1)

            def up_step(c, par, fixed=False):
                split_all(c + (GROUP["up"] + 1), c + (landed_group(GROUP["up"]) + 1))
                need(act, S["fc_done"], c * NT)
                evac(fconv_in[:, par, :, 2:2 + T], c + GROUP["up"], par)
                if not fixed:
                    glu_act(c - 1, 1 - par, False)

            up_step(0, 0, True)
            with act.Fori(0, 5) as i:
                up_step(i * 2 + 1, 1)
                up_step(i * 2 + 2, 0)
            glu_act(10, 0, True)
            for j in range(2):
                for g in range(3):
                    if GROUP["down"] + 3 * j + g + 1 < N_SPLIT:
                        split_all(GROUP["down"] + 3 * j + g + 1)
                act.wait_ge(evac_dve, DVE_DOWN + j + 1)
                squares(5, j)
            root(5)

        @block.vector
        def _(dve):
            step = Steps(dve, S["dve_step"])
            tt, ts, stt = nc.vector.tensor_tensor, nc.vector.tensor_scalar, nc.vector.scalar_tensor_tensor

            def split_lo(g, s):
                dve.wait_ge(hi_done, g * SLOTS + (s + 1))
                tt(out=w_lo[:, s, :], in0=raw[:, s, :], in1=w_hi[:, s, :].bitcast(F32), op=ALU.subtract).then_inc(taken, 1)

            def split_all(g):
                for s in range(SLOTS):
                    split_lo(g, s)

            def mod_panel(rg, par, s):
                dve.wait_ge(landed[s], rg * 16 + 16)
                acc = mod_acc[:, par]
                for k in range(2):
                    src, c_k = raw[:, s, 512 * k:512 * k + 512], silu_c[:, 2 * s + k:2 * s + k + 1]
                    if s == 0 and k == 0:
                        step(ts(out=acc, in0=src, scalar1=c_k, scalar2=0.0, op0=ALU.mult, op1=ALU.add))
                    elif k == 0:
                        step(stt(out=acc, in0=src, scalar=c_k, in1=acc, op0=ALU.mult, op1=ALU.add))
                    else:
                        stt(out=acc, in0=src, scalar=c_k, in1=acc, op0=ALU.mult, op1=ALU.add).then_inc(taken, 1)
                        dve.wait_ge(taken, rg * SLOTS + (s + 1))

            def mod_evac(m, fixed=True):
                dve.wait_ge(S["mod_mm"], m + 1)
                dst = modc[:, 4 * m:4 * m + 4] if fixed else modc[:, bass.ds(m * 4, 4)]
                b = col("b_mod", 4 * m, 4) if fixed else cols[:, bass.ds(m * 4 + COL["b_mod"], 4)]
                tt(out=dst, in0=aux[:, 3, 0:4], in1=b, op=ALU.add).then_inc(S["mod_done"], 1)

            def norm_scale(n):
                dve.wait_ge(S["rt_done"], n + 1)
                nc.vector.reciprocal(rs_sb[:], rt_sb[:]).then_inc(S["rs_done"], 1)
                dve.wait_ge(S["rs_done"], n + 1)

            def norm_apply(a, scale, shift):
                for k in range(KT + 2):
                    if k < KT:
                        stt(out=tmp_a[:, k], in0=xres[:, k], scalar=scale(k), in1=rs_sb[:], op0=ALU.mult,
                            op1=ALU.mult).then_inc(S["nrm_t"], 1)
                    if k >= 2:
                        dve.wait_ge(S["nrm_hi"], KT * a + k - 1)
                        stt(out=act_lo[:, k - 2], in0=tmp_a[:, k - 2], scalar=shift(k - 2), in1=act_hi[:, k - 2].bitcast(F32),
                            op0=ALU.add, op1=ALU.subtract).then_inc(S["nrm_lo"], 1)

            def softplus_rest(e, u, ln, small_part):
                step(stt(out=small_part, in0=u, scalar=1.0, in1=e, op0=ALU.subtract, op1=ALU.subtract))
                step(nc.vector.reciprocal(u, u))
                step(stt(out=small_part, in0=small_part, scalar=-1.0, in1=u, op0=ALU.mult, op1=ALU.mult))
                step(tt(out=ln, in0=ln, in1=small_part, op=ALU.add))

            def add_residual(j, par, gate):
                for nt in range(NT):
                    k = 4 * j + nt
                    src = proj_ps[:, par, nt * T:nt * T + T]
                    if gate is None:
                        last = tt(out=xres[:, k], in0=xres[:, k], in1=src, op=ALU.add)
                    else:
                        last = stt(out=xres[:, k], in0=src, scalar=modc[:, gate + k:gate + k + 1], in1=xres[:, k],
                                   op0=ALU.mult, op1=ALU.add)
                last.then_inc(evac_dve, 1)

            nc.vector.memset(ones[:], 1.0).then_inc(S["ready"], 1)
            nc.vector.memset(avg_d[:], 1.0 / D).then_inc(S["ready"], 1)
            nc.vector.memset(avg_g[:], 1.0 / 256).then_inc(S["ready"], 1)
            nc.vector.memset(avg_v[:], 1.0 / P).then_inc(S["ready"], 1)
            nc.vector.memset(eps[:], EPS).then_inc(S["ready"], 1)
            nc.vector.memset(zero8[:], 0.0).then_inc(S["ready"], 1)
            for n, (name, credit) in enumerate((("conv_done", NT), ("xbc_done", 1), ("seg_mm", 2), ("cum_mm", 1), ("ecum_ok", 1),
                                                ("state_ok", 1), ("y_ok", 2), ("fc_done", NT), ("glu_f", 1))):
                nc.vector.memset(junk[:, n:n + 1], 0.0).then_inc(S[name], credit)
            dve.wait_ge(S["x_in"], 32)
            dve.wait_ge(S["c_ready"], 1)
            for m in range(MOD_FIRST):
                if m >= 2:
                    dve.wait_ge(S["mod_mm"], m - 1)
                for s in range(SLOTS):
                    mod_panel(m, m % 2, s)
                if m >= 1:
                    mod_evac(m - 1)
            norm_scale(0)
            mod_evac(MOD_FIRST - 1)
            dve.wait_ge(S["mod_done"], MOD_FIRST)
            step(ts(out=modc[:, 8:16], in0=modc[:, 8:16], scalar1=1.0, scalar2=None, op0=ALU.add))
            norm_apply(0, lambda k: modc[:, 8 + k:9 + k], lambda k: modc[:, k:k + 1])
            split_all(0)
            dve.wait_ge(S["wdt_hi_ok"], 1)
            tt(out=wdt_lo[:], in0=wdt[:], in1=wdt_hi[:].bitcast(F32), op=ALU.subtract).then_inc(S["wdt_ok"], 1)
            for g in range(1, GROUP["xbc"] + 1):
                split_all(g)
                if g == 3:
                    dve.wait_ge(S["v_rt"], 1)
                    step(nc.vector.reciprocal(small[:, 4:6], small[:, 2:4]))
                    for t in range(TT):
                        ts(out=v_sb[:, t], in0=v_sb[:, t], scalar1=small[:, 4 + t:5 + t], scalar2=None,
                           op0=ALU.mult).then_inc(S["v_ready"], 1)
            dve.wait_ge(S["dt_mm"], 1)
            step(tt(out=dts[:, 3], in0=aux[:, 0, 0:TT * HEADS].rearrange("p (t h) -> p t h", t=TT),
                    in1=spread(col("dt_bias", 0, HEADS), 1, TT), op=ALU.add))
            stt(out=dts[:, 4], in0=dts[:, 3], scalar=-1.0, in1=dts[:, 3], op0=ALU.mult, op1=ALU.max).then_inc(S["dt_abs"], 1)
            dve.wait_ge(S["dt_exp"], 1)
            ts(out=dts[:, 6], in0=dts[:, 5], scalar1=1.0, scalar2=None, op0=ALU.add).then_inc(S["dt_u"], 1)
            dve.wait_ge(S["dt_ln"], 1)
            softplus_rest(dts[:, 5], dts[:, 6], dts[:, 7], dts[:, 4])
            step(stt(out=dts[:, 0], in0=dts[:, 3], scalar=0.0, in1=dts[:, 7], op0=ALU.max, op1=ALU.add))
            dve.wait_ge(S["exp_a_ok"], 1)
            stt(out=dts[:, 1], in0=dts[:, 0], scalar=-1.0, in1=spread(exp_a[:], 1, TT), op0=ALU.mult,
                op1=ALU.mult).then_inc(S["dt_ok"], 1)
            nc.vector.memset(conv_in[:, :, :, 0:3], 0.0).then_inc(S["padded"], 1)

            def conv_chunk(c, par):
                split_all(c + (GROUP["xbc"] + 1))
                for nt in range(NT):
                    dve.wait_ge(S["conv_pool"], c * NT + (nt + 1))
                    acc, src = conv_acc[:, par, nt], conv_in[:, par, nt]
                    w = c * (NT * 4) + nt * 4
                    step(stt(out=acc, in0=src[:, 1:1 + T], scalar=col_at("conv_w", w + 1), in1=acc, op0=ALU.mult, op1=ALU.add))
                    stt(out=acc, in0=src[:, 0:T], scalar=col_at("conv_w", w), in1=acc, op0=ALU.mult,
                        op1=ALU.add).then_inc(S["conv_done"], 1)

            conv_chunk(0, 0)
            with step.loop(3, 2 * NT) as i:
                conv_chunk(i * 2 + 1, 1)
                conv_chunk(i * 2 + 2, 0)
            conv_chunk(7, 1)
            dve.wait_ge(S["early_in"], 64)
            dve.wait_ge(evac_act, EVAC_XBC)
            dve.wait_ge(S["xbc_done"], 9)
            for g in range(GROUPS_SGU):
                if g % 2 == 0:
                    dve.wait_ge(S["sgu_mm"], g // 2 + 1)
                last = stt(out=tmp_b[:, g].rearrange("p (c i) -> p c i", c=TT),
                           in0=aux[:, g // 2, (g % 2) * T:(g % 2) * T + T].rearrange("p (c i) -> p c i", c=TT),
                           scalar=col("gm_norm_w", g), in1=spread(bs_sb[:, g], 1, TT), op0=ALU.mult, op1=ALU.add)
            last.then_inc(S["sgu_y"], 1)
            dve.wait_ge(S["sgu_y"], 1)
            tt(out=u_sb[:], in0=u_sb[:], in1=tmp_b[:], op=ALU.mult).then_inc(S["sgu_y"], 1)
            dve.wait_ge(S["sgu_hi"], 1)
            dve.wait_ge(S["sgu_y"], 2)
            tt(out=ya_lo[:], in0=u_sb[:], in1=ya_hi[:].bitcast(F32), op=ALU.subtract).then_inc(S["sgu_done"], 1)

            def ssd_dve(g, par):
                rg = g * 2 + (landed_group(GROUP["zg"]) + 1)
                dve.wait_ge(S["t_mm"], g + 1)
                tt(out=xdt[:].rearrange("p c (h d) -> p c h d", h=HPG),
                   in0=aux[:, 0].rearrange("p (c h d) -> p c h d", c=2, h=HPG),
                   in1=spread(dts[:, 0, :, bass.ds(g * HPG, HPG)], 3, 64), op=ALU.mult).then_inc(S["xdt_ok"], 1)
                dve.wait_ge(S["btok_ok"], g + 1)
                tt(out=cbm[:], in0=aux[:, 1, 0:2 * P].rearrange("p (c i) -> p c i", c=2), in1=spread(upto, 1, 2),
                   op=ALU.mult).then_inc(S["cbm_ok"], 1)
                dve.wait_ge(S["mod_mm"], g + (MOD_FIRST - 1))
                for c in range(2):
                    mod_panel(rg, par, 2 * c)
                    mod_panel(rg, par, 2 * c + 1)
                    dve.wait_ge(S["decay_ok"], g * 2 + (c + 1))
                    dve.wait_ge(S["cbm_ok"], g + 1)
                    tt(out=decay[:, c], in0=decay[:, c], in1=spread(cbm[:, c], 1, HPG), op=ALU.mult).then_inc(S["m_ok"], 1)
                for s in range(SLOTS):
                    split_lo(g + (GROUP["zg"] + 1), s)
                dve.wait_ge(S["y_mm"], g + 1)
                for pair in range(2):
                    last = stt(out=xbc[:, bass.ds(g * 2 + pair, 1), :].rearrange("p a t -> p (a t)"), in0=stg[:, par, pair],
                               scalar=col_at("d_skip", g * 2 + pair), in1=aux[:, 2, pair * T:pair * T + T],
                               op0=ALU.mult, op1=ALU.add)
                last.then_inc(S["y_ok"], 1)
                mod_evac(g + MOD_FIRST, fixed=False)

            with step.loop(4, 2 * SLOTS) as i:
                ssd_dve(i * 2, 0)
                ssd_dve(i * 2 + 1, 1)
            dve.wait_ge(S["mod_done"], 12)
            step(ts(out=modc[:, 32:40], in0=modc[:, 32:40], scalar1=1.0, scalar2=None, op0=ALU.add))
            dve.wait_ge(S["y_ok"], 2 + SSD_GROUPS)
            for q in range(4):
                dve.wait_ge(S["silu_z"], q + 1)
                tt(out=xbc[:, 4 * q:4 * q + 4], in0=xbc[:, 4 * q:4 * q + 4], in1=zg[:, 4 * q:4 * q + 4],
                   op=ALU.mult).then_inc(S["g_ok"], 1)
            split_all(GROUP["gm"] + 1)
            for q in range(4):
                dve.wait_ge(S["grt_ok"], q + 1)
                step(nc.vector.reciprocal(group_rs[:, 2 * q:2 * q + 2], group_rs[:, 2 * q:2 * q + 2]))
                for k in range(4 * q, 4 * q + 4):
                    last = stt(out=xbc[:, k], in0=xbc[:, k], scalar=col("ssm_norm_w", k), in1=group_rs[:, k // 2],
                               op0=ALU.mult, op1=ALU.mult)
                last.then_inc(S["yb_f"], 1)
                dve.wait_ge(S["yb_h"], q + 1)
                tt(out=yb_lo[:, 4 * q:4 * q + 4], in0=xbc[:, 4 * q:4 * q + 4], in1=yb_hi[:, 4 * q:4 * q + 4].bitcast(F32),
                   op=ALU.subtract).then_inc(S["yb_ok"], 1)
                if q == 1:
                    dve.wait_ge(S["sig_ok"], 1)
                    dve.wait_ge(used, (GROUP["gm"] + 1) * SLOTS)
                    tt(out=zg[:, 16:20], in0=zg[:, 16:20], in1=proj_ps[:, 0].rearrange("p (n t) -> p n t", n=NT),
                       op=ALU.mult).then_inc(evac_dve, 1)
            split_all(GROUP["ssm"])
            dve.wait_ge(used, (GROUP["gm"] + 2) * SLOTS)
            tt(out=zg[:, 20:24], in0=zg[:, 20:24], in1=proj_ps[:, 1].rearrange("p (n t) -> p n t", n=NT),
               op=ALU.mult).then_inc(evac_dve, 1)
            for j in range(2):
                split_all(GROUP["ssm"] + 2 * j + 1)
                split_all(GROUP["ssm"] + 2 * j + 2)
                ga, gb = zg[:, 16 + 4 * j:20 + 4 * j], zg[:, 24 + 4 * j:28 + 4 * j]
                dve.wait_ge(used, (GROUP["ssm"] + 2 * j + 2) * SLOTS)
                tt(out=gb, in0=gb, in1=proj_ps[:, j].rearrange("p (n t) -> p n t", n=NT), op=ALU.mult).then_inc(evac_dve, 1)
                dve.wait_ge(evac_dve, 3 + j)
                tt(out=ga, in0=ga, in1=gb, op=ALU.add).then_inc(S["mix_f"], 1)
                dve.wait_ge(S["mix_h"], j + 1)
                dve.wait_ge(S["mix_f"], j + 1)
                tt(out=act_lo[:, 4 * j:4 * j + 4], in0=ga, in1=act_hi[:, 4 * j:4 * j + 4].bitcast(F32),
                   op=ALU.subtract).then_inc(S["mix_ok"], 1)
            for j in range(2):
                split_all(GROUP["out"] + j + 1)
                dve.wait_ge(used, (GROUP["out"] + j + 1) * SLOTS)
                add_residual(j, j, 16)
            dve.wait_ge(evac_dve, DVE_OUT + 2)
            norm_scale(1)
            norm_apply(1, lambda k: modc[:, 32 + k:33 + k], lambda k: modc[:, 24 + k:25 + k])

            def ff1_step(c, par):
                split_all(c + (GROUP["ff1"] + 1))
                dve.wait_ge(evac_act, c + (EVAC_FF1 + 1))
                tt(out=sq_sb[:, par], in0=relu_sb[:, par], in1=relu_sb[:, par], op=ALU.mult).then_inc(S["sq_ok"], 1)
                dve.wait_ge(S["ffhi_ok"], c + 1)
                tt(out=ff_lo[:, bass.ds(c * NT, NT), :], in0=sq_sb[:, par].rearrange("p (n t) -> p n t", n=NT),
                   in1=ff_hi[:, bass.ds(c * NT, NT), :].bitcast(F32), op=ALU.subtract).then_inc(S["ff_ok"], 1)

            with dve.Fori(0, 4) as i:
                ff1_step(i * 2, 0)
                ff1_step(i * 2 + 1, 1)
            for j in range(2):
                for g in range(4):
                    split_all(GROUP["ff2"] + 4 * j + g + 1)
                dve.wait_ge(used, (GROUP["ff2"] + 4 * j + 4) * SLOTS)
                add_residual(j, j, 40)
            dve.wait_ge(evac_dve, DVE_FF2 + 2)
            norm_scale(2)
            for k in range(KT):
                last = stt(out=xres[:, k], in0=xres[:, k], scalar=col("final_norm_w", k), in1=rs_sb[:], op0=ALU.mult, op1=ALU.mult)
                if k % 4 == 3:
                    last.then_inc(S["mid_ok"], 1)
            dve.wait_ge(S["mid_ok"], 2)
            norm_scale(3)
            norm_apply(2, lambda k: col("attn_g", k), lambda k: zero8[:, k:k + 1])
            dve.wait_ge(S["wglr_hi_ok"], 1)
            tt(out=wglr_lo[:], in0=wglr[:], in1=wglr_hi[:].bitcast(F32), op=ALU.subtract).then_inc(S["wglr_ok"], 1)
            step(nc.vector.memset(scores_t[:], 0.0))
            i2 = GROUP["in2"]
            split_all(i2 + 1)
            split_all(i2 + 2)
            dve.wait_ge(S["gate_mm"], 1)
            for t in range(2):
                last = ts(out=og[:, t], in0=aux[:, 1, t * T:t * T + T], scalar1=col("b_gate", t), scalar2=None, op0=ALU.add)
            step(last)
            stt(out=gt[:, 0], in0=og[:, 0:2], scalar=-1.0, in1=og[:, 0:2], op0=ALU.mult, op1=ALU.max).then_inc(S["gx_abs"], 1)
            dve.wait_ge(S["gx_exp"], 1)
            ts(out=gt[:, 2], in0=gt[:, 1], scalar1=1.0, scalar2=None, op0=ALU.add).then_inc(S["gx_u"], 1)
            dve.wait_ge(S["gx_ln"], 1)
            softplus_rest(gt[:, 1], gt[:, 2], glog[:], gt[:, 0])
            step(stt(out=gt[:, 0], in0=og[:, 0:2], scalar=0.0, in1=glog[:], op0=ALU.min, op1=ALU.subtract))
            step(ts(out=gt[:, 0], in0=gt[:, 0], scalar1=1.0 / 16, scalar2=None, op0=ALU.mult))
            step(nc.vector.memset(gt[:, 1], 1.0))
            for t in range(2):
                last = nc.vector.tensor_tensor_scan(out=glog[:, t], data0=gt[:, 1, t], data1=gt[:, 0, t], initial=0.0,
                                                    op0=ALU.mult, op1=ALU.add)
            step(last)

            def level_diff(e):
                m = (LEVELS + [P])[e]
                view = flat(glog[:]).rearrange("p (n m) -> p n m", m=2 * m)
                if e >= 2:
                    dve.wait_ge(S["lev_x"], e - 1)
                tt(out=gd[:, e % 2].rearrange("p (n m) -> p n m", m=2 * m), in0=view,
                   in1=view[:, :, m - 1:m].broadcast_to(list(view.shape)), op=ALU.subtract).then_inc(S["lev_d"], 1)

            def level_pick(l):
                dve.wait_ge(S["lev_mm"], l + 1)
                bank = 2 * (l % 2)
                if l == 8:
                    nc.vector.tensor_copy(scores_t[:, 2].rearrange("p (a b) i -> p a (b i)", a=2), aux[:, bank:bank + 2, 0:2 * P]
                                          ).then_inc(S["lev_ok"], 1)
                    return
                if l > 0:
                    dve.wait_ge(S["lev_ok"], l)
                for t in range(TT):
                    last = nc.vector.copy_predicated(
                        scores_t[:, t].rearrange("p (a b) i -> p a b i", a=2),
                        spread(spread(level_sb[:, l].bitcast(U32), 1, 2), 1, 2),
                        aux[:, bank:bank + 2, 2 * t * P:2 * t * P + 2 * P].rearrange("p a (b i) -> p a b i", b=2))
                last.then_inc(S["lev_ok"], 1)

            level_diff(0)
            split_all(i2 + 3)
            for c in range(2):
                for s in range(SLOTS):
                    l = 4 * c + s
                    if l + 1 < 8:
                        level_diff(l + 1)
                    split_lo(i2 + 4 + c, s)
                    level_pick(l)
            level_pick(8)
            split_lo(i2 + 6, 0)
            split_lo(i2 + 6, 1)
            split_lo(i2 + 6, 2)
            split_lo(i2 + 6, 3)
            dve.wait_ge(S["og_rt"], 1)
            step(nc.vector.reciprocal(og2[:], og2[:]))
            step(tt(out=og[:], in0=og[:], in1=og2[:], op=ALU.mult))
            for h in range(GLA_HEADS):
                last = stt(out=og[:, h], in0=og[:, h], scalar=col("gla_g", h), in1=gr_sb[:, h], op0=ALU.mult, op1=ALU.mult)
            last.then_inc(S["gla_f"], 1)
            dve.wait_ge(S["gla_f"], 1)
            dve.wait_ge(S["gla_h"], 1)
            tt(out=mix_lo[:, 0:4], in0=og[:], in1=mix_hi[:, 0:4].bitcast(F32), op=ALU.subtract).then_inc(S["gla_ok"], 1)
            for w, x in enumerate((q_sb, k_sb)):
                dve.wait_ge(S["turn_mm"], w + 1)
                tt(out=rope_t[:, 0], in0=x[:], in1=spread(rope_sb[:, 0], 1, NT), op=ALU.mult)
                step(tt(out=rope_t[:, 1].rearrange("p (b n) t -> p b n t", b=2),
                        in0=aux[:, 2 * w:2 * w + 2].rearrange("p b (n t) -> p b n t", n=2),
                        in1=spread(spread(rope_sb[:, 1], 1, 2), 1, 2), op=ALU.mult))
                tt(out=x[:], in0=rope_t[:, 0], in1=rope_t[:, 1], op=ALU.add).then_inc(S["rope_ok"], 1)
                dve.wait_ge(S["rope_ok"], w + 1)
            for w in range(UNITS + 1):
                if w < UNITS:
                    n = 4 if w < 2 else 2
                    dve.wait_ge(S["sc_mm"], w + 1)
                    mask = neg_sb[:, 1] if w < 2 else flat(neg_sb[:, 0:2])
                    part = prob[:, w].rearrange("p (h k) -> p h k", h=n)
                    step(tt(out=part, in0=aux[:, w % 2].rearrange("p (h k) -> p h k", h=n), in1=spread(mask, 1, n), op=ALU.add))
                    step(nc.vector.reduce_max(small[:, 4 * w:4 * w + n], part, AX_X))
                    ts(out=small[:, 32 + 4 * w:32 + 4 * w + n], in0=small[:, 4 * w:4 * w + n], scalar1=-0.125, scalar2=None,
                       op0=ALU.mult).then_inc(S["max_ok"], 1)
                if w > 0:
                    n = 4 if w - 1 < 2 else 2
                    at_sum = 64 + 4 * (w - 1)
                    dve.wait_ge(S["exp_ok"], w)
                    step(nc.vector.reciprocal(small[:, at_sum:at_sum + n], small[:, at_sum:at_sum + n]))
                    part = prob[:, w - 1].rearrange("p (h k) -> p h k", h=n)
                    tt(out=part, in0=part, in1=spread(small[:, at_sum:at_sum + n], 2, 512 // n), op=ALU.mult).then_inc(S["p_ok"], 1)
            dve.wait_ge(S["ym_h"], 1)
            tt(out=flat(mix_lo[:, 4:8]), in0=proj_ps[:, 1], in1=flat(mix_hi[:, 4:8]).bitcast(F32), op=ALU.subtract).then_inc(S["ym_ok"], 1)
            for j in range(2):
                split_all(GROUP["out2"] + j + 1)
                dve.wait_ge(used, (GROUP["out2"] + j + 1) * SLOTS)
                add_residual(j, j, None)
            dve.wait_ge(evac_dve, DVE_OUT2 + 2)
            norm_scale(4)
            norm_apply(3, lambda k: col("ffn_g", k), lambda k: zero8[:, k:k + 1])
            nc.vector.memset(fconv_in[:, :, :, 0:2], 0.0).then_inc(S["fpadded"], 1)

            def glu_dve(c, par, fixed):
                dve.wait_ge(S["fc_silu"], c + 1)
                tt(out=glu_sb[:, par], in0=fconv_acc[:, par, 0:2], in1=fconv_acc[:, par, 2:4], op=ALU.mult).then_inc(S["glu_f"], 1)
                dve.wait_ge(S["glu_h"], c + 1)
                part = slice(2 * c, 2 * c + 2) if fixed else bass.ds(c * 2, 2)
                tt(out=glu_lo[:, part, :], in0=glu_sb[:, par], in1=glu_hi[:, part, :].bitcast(F32),
                   op=ALU.subtract).then_inc(S["glu_ok"], 1)

            def up_step(c, par, fixed=False):
                split_all(c + (GROUP["up"] + 1))
                if not fixed:
                    glu_dve(c - 1, 1 - par, False)
                for nt in range(NT):
                    dve.wait_ge(S["fc_pool"], c * NT + (nt + 1))
                    acc = fconv_acc[:, par, nt]
                    stt(out=acc, in0=fconv_in[:, par, nt, 0:T], scalar=col_at("fconv_w", c * (NT * 3) + nt * 3), in1=acc,
                        op0=ALU.mult, op1=ALU.add).then_inc(S["fc_done"], 1)

            up_step(0, 0, True)
            with dve.Fori(0, 5) as i:
                up_step(i * 2 + 1, 1)
                up_step(i * 2 + 2, 0)
            glu_dve(10, 0, True)
            for j in range(2):
                for g in range(3):
                    if GROUP["down"] + 3 * j + g + 1 < N_SPLIT:
                        split_all(GROUP["down"] + 3 * j + g + 1)
                dve.wait_ge(used, (GROUP["down"] + 3 * j + 3) * SLOTS)
                add_residual(j, (j + 1) % 2, None)
            dve.wait_ge(evac_dve, DVE_DOWN + 2)
            norm_scale(5)
            for k in range(KT):
                last = stt(out=tmp_b[:, k], in0=xres[:, k], scalar=col("final_g", k), in1=rs_sb[:], op0=ALU.mult, op1=ALU.mult)
                if k % 4 == 3:
                    last.then_inc(S["fin_ok"], 1)

        @block.tensor
        def _(pe):
            mm = nc.tensor.matmul

            def panel(g, s, par, x_hi, x_lo, k0=0, first=False, last=False, rg=None, ks=2, release=1):
                rg = landed_group(g) if rg is None else rg
                pe.wait_ge(taken, rg * SLOTS + (s + 1))
                for nt in range(NT):
                    dst = proj_ps[:, par, nt * T:nt * T + T]
                    for k in range(ks):
                        hi = w_hi[:, s, k * 512 + nt * P:k * 512 + nt * P + P]
                        lo = w_lo[:, s, k * 512 + nt * P:k * 512 + nt * P + P]
                        xh, xl = x_hi[:, k0 + k], x_lo[:, k0 + k]
                        mm(dst, hi, xh, start=first and k == 0 and nt % 2 == 0, stop=False, skip_group_check=True)
                        mm(dst, hi, xl, start=False, stop=False, skip_group_check=True)
                        ins = mm(dst, lo, xh, start=False, stop=last and k == ks - 1, skip_group_check=True)
                ins.then_inc(used, release)

            def chunk(g, par, rg=None, x_ready=None):
                for s in range(SLOTS):
                    if x_ready:
                        pe.wait_ge(x_ready[0], x_ready[1] + 2 * s + 2)
                    panel(g, s, par, act_hi, act_lo, 2 * s, s == 0, s == SLOTS - 1, rg)

            def token_panel(g, s, par):
                pe.wait_ge(taken, landed_group(g) * SLOTS + (s + 1))
                for t in range(TT):
                    dst = proj_ps[:, par, t * 512:t * 512 + 512]
                    for k in range(2):
                        wh, wl = w_hi[:, s, k * 512:k * 512 + 512], w_lo[:, s, k * 512:k * 512 + 512]
                        xh, xl = (a[:, 2 * s + k, t * P:t * P + P] for a in (act_hi, act_lo))
                        mm(dst, xh, wh, start=s == 0 and k == 0, stop=False)
                        mm(dst, xh, wl, start=False, stop=False)
                        ins = mm(dst, xl, wh, start=False, stop=s == SLOTS - 1 and k == 1)
                ins.then_inc(used, 1)

            def chunk_tokens(g, par, x_ready=None):
                for s in range(SLOTS):
                    if x_ready:
                        pe.wait_ge(x_ready[0], x_ready[1] + 2 * s + 2)
                    token_panel(g, s, par)

            def mean_square(n):
                for h in range(2):
                    pe.wait_ge(S["sq_done"], 2 * n + h + 1)
                    for k in range(4 * h, 4 * h + 4):
                        ins = mm(aux[:, 2, 0:T], avg_d[:], tmp_b[:, k], start=k == 0, stop=k == KT - 1)
                ins.then_inc(S["ms_mm"], 1)

            def mod_sum(m, par):
                for nt in range(NT):
                    ins = mm(aux[:, 3, nt:nt + 1], mod_acc[:, par, nt * P:nt * P + P], ones[:, 0:1], start=True, stop=True)
                ins.then_inc(S["mod_mm"], 1)

            pe.wait_ge(S["ready"], N_READY)
            mean_square(0)
            for m in range(MOD_FIRST):
                pe.wait_ge(taken, SLOTS * (m + 1))
                if m >= 1:
                    pe.wait_ge(S["mod_done"], m)
                mod_sum(m, m % 2)
            for j in range(2):
                chunk_tokens(GROUP["v"] + j, j, (S["nrm_lo"], 0))
            for j in range(2):
                pe.wait_ge(evac_act, j + 1)
                chunk(GROUP["u"] + j, j)
            pe.wait_ge(S["wdt_ok"], 1)
            for t in range(TT):
                for k in range(KT):
                    xh, xl = (a[:, k, t * P:t * P + P] for a in (act_hi, act_lo))
                    dst = aux[:, 0, t * HEADS:t * HEADS + HEADS]
                    mm(dst, xh, wdt_hi[:, k], start=k == 0, stop=False)
                    mm(dst, xh, wdt_lo[:, k], start=False, stop=False)
                    ins = mm(dst, xl, wdt_hi[:, k], start=False, stop=k == KT - 1)
            ins.then_inc(S["dt_mm"], 1)
            with pe.Fori(0, 4) as i:
                for par in range(2):
                    c = i * 2 + par
                    pe.wait_ge(evac_act, c + (EVAC_XBC - 1))
                    chunk(c + GROUP["xbc"], par, c + landed_group(GROUP["xbc"]))
            pe.wait_ge(S["dt_ok"], 1)
            pe.wait_ge(S["early_in"], 64)
            mm(aux[:, 0, 0:HEADS], after, dts[:, 1, 0], start=True, stop=True).then_inc(S["wend_mm"], 1)
            pe.wait_ge(S["v_ready"], 2)
            pe.wait_ge(S["ws_masked"], 1)
            pe.wait_ge(S["wend_ok"], 1)
            for g in range(GROUPS_SGU):
                for c in range(TT):
                    ins = mm(aux[:, g // 2, (g % 2) * T + c * P:(g % 2) * T + c * P + P], v_sb[:, c, g * P:g * P + P],
                             wst[:, g], start=True, stop=True)
                if g % 2:
                    ins.then_inc(S["sgu_mm"], 1)

            def ssd(g, par):
                zg_panel = lambda s: panel(g + GROUP["zg"], s, par, act_hi, act_lo, 2 * s, s == 0, s == SLOTS - 1,
                                           g * 2 + landed_group(GROUP["zg"]))
                x, b, c_t = stg[:, par, 0:2], stg[:, par, 2], stg[:, par, 3]
                pe.wait_ge(evac_act, g + (EVAC_ZG - 1))
                zg_panel(0)
                pe.wait_ge(S["stg_ok"], g + 1)
                pe.wait_ge(S["ecum_ok"], g + 1)
                for c in range(2):
                    for pair in range(2):
                        ins = nc.tensor.transpose(aux[:, 0, c * T + pair * P:c * T + pair * P + P], x[:, pair, c * P:c * P + P], ident)
                ins.then_inc(S["t_mm"], 1)
                pe.wait_ge(S["state_ok"], g + 1)
                nc.tensor.transpose(aux[:, 1, T:T + P], b[:, 0:P], ident)
                for c in range(2):
                    ins = mm(aux[:, 1, c * P:c * P + P], b[:, c * P:c * P + P], c_t[:, c * P:c * P + P], start=True, stop=True)
                ins.then_inc(S["cb_mm"], 1)
                for c in range(2):
                    pe.wait_ge(S["upto_ok"], g * 2 + (c + 1))
                    if c == 0:
                        pe.wait_ge(S["y_ok"], g + 2)
                    else:
                        pe.wait_ge(S["mod_done"], g + MOD_FIRST)
                    mm(aux[:, 2 + c], after, flat(a_upto[:, c]), start=True, stop=True).then_inc(S["seg_mm"], 1)
                zg_panel(1)
                pe.wait_ge(S["xdt_ok"], g + 1)
                mm(aux[:, 0], ones[:], flat(a_upto[:, 1]), start=True, stop=True).then_inc(S["cum_mm"], 1)
                zg_panel(2)
                pe.wait_ge(S["xw_ok"], g + 1)
                pe.wait_ge(S["btok_ok"], g + 1)
                pe.wait_ge(S["cbm_ok"], g + 1)
                mm(aux[:, 1, 0:T], b_tok[:], xw[:], start=True, stop=True).then_inc(S["st_mm"], 1)
                y = lambda h, c: aux[64 * (h % 2):64 * (h % 2) + 64, 2, (h // 2) * T + c * P:(h // 2) * T + c * P + P]
                pe.wait_ge(S["m_ok"], g * 2 + 1)
                for h in range(HPG):
                    mm(y(h, 0), xdt[:, 0, 64 * h:64 * h + 64], decay[:, 0, h], start=True, stop=True)
                zg_panel(3)
                pe.wait_ge(S["m_ok"], g * 2 + 2)
                pe.wait_ge(S["state_ok"], g + 2)
                pe.wait_ge(S["cin_ok"], g + 1)
                for h in range(HPG):
                    mm(y(h, 1), xdt[:, 1, 64 * h:64 * h + 64], decay[:, 1, h], start=True, stop=False)
                    ins = mm(y(h, 1), state[:, 64 * h:64 * h + 64], c_in[:, h], start=False, stop=True)
                ins.then_inc(S["y_mm"], 1)
                pe.wait_ge(taken, g * (2 * SLOTS) + (landed_group(GROUP["zg"]) + 2) * SLOTS)
                mod_sum(g + MOD_FIRST, par)

            pe.wait_ge(S["sgu_y"], 1)
            with pe.Fori(0, 4) as i:
                ssd(i * 2, 0)
                ssd(i * 2 + 1, 1)
            pe.wait_ge(S["sgu_done"], 1)
            for j in range(2):
                pe.wait_ge(evac_act, EVAC_ZG + 7 + j)
                for s in range(SLOTS):
                    panel(GROUP["gm"] + j, s, j, ya_hi, ya_lo, 2 * s, s == 0, s == SLOTS - 1)
                if j == 0:
                    pe.wait_ge(S["mod_done"], 12)
                    for grp in range(8):
                        pe.wait_ge(S["g2_ok"], grp // 2 + 1)
                        for k in range(2):
                            ins = mm(aux[:, grp // 2, (grp % 2) * T:(grp % 2) * T + T], avg_g[:], zg[:, 2 * grp + k],
                                     start=k == 0, stop=k == 1)
                        if grp % 2:
                            ins.then_inc(S["gsum_mm"], 1)
            for j in range(2):
                pe.wait_ge(evac_dve, j + 1)
                for g in range(2):
                    for s in range(SLOTS):
                        pe.wait_ge(S["yb_ok"], (8 * g + 2 * s) // 4 + 1)
                        panel(GROUP["ssm"] + 2 * j + g, s, j, yb_hi, yb_lo, 8 * g + 2 * s, g == 0 and s == 0, g == 1 and s == 3)
            for j in range(2):
                pe.wait_ge(evac_dve, 3 + j)
                for s in range(SLOTS):
                    pe.wait_ge(S["mix_ok"], s // 2 + 1)
                    panel(GROUP["out"] + j, s, j, act_hi, act_lo, 2 * s, s == 0, s == 3)
            mean_square(1)
            pe.wait_ge(evac_dve, DVE_OUT + 2)
            with pe.Fori(0, 4) as i:
                for par in range(2):
                    c = i * 2 + par
                    pe.wait_ge(evac_act, c + (EVAC_FF1 - 1))
                    chunk(c + GROUP["ff1"], par, c + landed_group(GROUP["ff1"]), (S["nrm_lo"], KT))
            for j in range(2):
                pe.wait_ge(evac_act, EVAC_FF1 + 7 + j)
                for g in range(4):
                    for s in range(SLOTS):
                        pe.wait_ge(S["ff_ok"], (8 * g + 2 * s) // 4 + 1)
                        panel(GROUP["ff2"] + 4 * j + g, s, j, ff_hi, ff_lo, 8 * g + 2 * s, g == 0 and s == 0, g == 3 and s == 3)
            mean_square(2)
            mean_square(3)
            i2 = GROUP["in2"]
            pe.wait_ge(evac_dve, DVE_FF2 + 2)
            ready2 = (S["nrm_lo"], 2 * KT)
            chunk(i2, 0, x_ready=ready2)
            chunk_tokens(i2 + 1, 1)
            pe.wait_ge(S["wglr_ok"], 1)
            for k in range(KT):
                dst = aux[0:16, 0, 0:T]
                mm(dst, wglr_hi[:, k], act_hi[:, k], start=k == 0, stop=False)
                mm(dst, wglr_hi[:, k], act_lo[:, k], start=False, stop=False)
                ins = mm(dst, wglr_lo[:, k], act_hi[:, k], start=False, stop=k == KT - 1)
            ins.then_inc(S["glr_mm"], 1)
            pe.wait_ge(evac_act, EVAC_IN2 + 1)
            panel(i2 + 2, 0, 0, act_hi, act_lo, 0, True)
            pe.wait_ge(S["glr_ok"], 1)
            pe.wait_ge(S["late_in"], 80)
            for t in range(2):
                ins = mm(aux[:, 1, t * T:t * T + T], wgu[:, t * P:t * P + P], glr_sb[:], start=True, stop=True)
            ins.then_inc(S["gate_mm"], 1)
            for s in range(1, SLOTS):
                panel(i2 + 2, s, 0, act_hi, act_lo, 2 * s, False, s == 3)

            def level_mm(l):
                if l == 0:
                    pe.wait_ge(S["gx_abs"], 1)
                else:
                    pe.wait_ge(S["lev_x"], l)
                if l >= 2:
                    pe.wait_ge(S["lev_ok"], l - 1)
                bank = 2 * (l % 2)
                for t in range(1 if l == 8 else TT):
                    for h in range(GLA_HEADS):
                        rows, pair = slice(64 * (h % 2), 64 * (h % 2) + 64), h // 2
                        if l == 0:
                            keys, queries = (gqk[rows, a + pair, t * P:t * P + P] for a in (2, 0))
                        elif l == 8:
                            keys, queries = (gx[rows, (l - 1) % 2, pair * T + a * P:pair * T + a * P + P] for a in (0, 1))
                        else:
                            keys = queries = gx[rows, (l - 1) % 2, pair * T + t * P:pair * T + t * P + P]
                        at_col = (2 * t + pair) * P
                        ins = mm(aux[:, bank + h % 2, at_col:at_col + P], keys, queries, start=True, stop=True)
                ins.then_inc(S["lev_mm"], 1)

            pe.wait_ge(evac_act, EVAC_IN2 + 2)
            for s in range(SLOTS):
                token_panel(i2 + 3, s, 1)
                level_mm(s)
            pe.wait_ge(evac_act, EVAC_IN2 + 3)
            for s in range(SLOTS):
                panel(i2 + 4, s, 0, act_hi, act_lo, 2 * s, s == 0, s == 3)
                level_mm(4 + s)
            pe.wait_ge(evac_act, EVAC_IN2 + 4)
            panel(i2 + 5, 0, 1, act_hi, act_lo, 0, True)
            level_mm(8)
            panel(i2 + 5, 1, 1, act_hi, act_lo, 2)
            pe.wait_ge(S["lev_ok"], 9)
            for h in range(GLA_HEADS):
                dst = aux[:, 2 + h // 2, (h % 2) * T:(h % 2) * T + T]
                at_h = (h % 2) * 2 + h // 2
                mm(dst[:, 0:P], gv_sb[:, 0, h * P:h * P + P], scores_t[:, 0, at_h], start=True, stop=True)
                mm(dst[:, P:T], gv_sb[:, 1, h * P:h * P + P], scores_t[:, 1, at_h], start=True, stop=False)
                ins = mm(dst[:, P:T], gv_sb[:, 0, h * P:h * P + P], scores_t[:, 2, at_h], start=False, stop=True)
            ins.then_inc(S["og_mm"], 1)
            panel(i2 + 5, 2, 1, act_hi, act_lo, 4)
            panel(i2 + 5, 3, 1, act_hi, act_lo, 6, False, True)
            pe.wait_ge(S["og_sq"], 1)
            for b in range(2):
                ins = mm(aux[:, b], avg_v[:], flat(og2[:, 2 * b:2 * b + 2]), start=True, stop=True)
            ins.then_inc(S["og_ms"], 1)
            pe.wait_ge(S["og_rt"], 1)
            pe.wait_ge(evac_act, EVAC_IN2 + 6)
            for w, x in enumerate((q_sb, k_sb)):
                for nt in range(NT):
                    ins = mm(aux[:, 2 * w + nt // 2, (nt % 2) * T:(nt % 2) * T + T], turn, x[:, nt], start=True, stop=True)
                ins.then_inc(S["turn_mm"], 1)
            pe.wait_ge(S["gla_ok"], 1)
            o2 = GROUP["out2"]
            panel(o2, 0, 0, mix_hi, mix_lo, 0, True)
            panel(o2, 1, 0, mix_hi, mix_lo, 2)
            pe.wait_ge(S["rope_ok"], 2)

            def unit(w):
                return (0, range(w, MOBA_HEADS, 2)) if w < 2 else (1, range(w % 2 + 4 * (w // 2 - 1), 4 * (w // 2), 2))

            for w in range(UNITS + 2):
                if w < UNITS:
                    tile, heads = unit(w)
                    if w >= 2:
                        pe.wait_ge(S["max_ok"], w - 1)
                    for i, h in enumerate(heads):
                        rows = slice(64 * (h % 2), 64 * (h % 2) + 64)
                        n = P * (tile + 1)
                        ins = mm(aux[:, w % 2, i * n:i * n + n], q_sb[rows, h // 2, tile * P:tile * P + P],
                                 k_sb[rows, h // 2, 0:n], start=True, stop=True)
                    ins.then_inc(S["sc_mm"], 1)
                if 1 <= w <= UNITS:
                    v = w - 1
                    pe.wait_ge(S["p_ok"], v + 1)
                    if v >= 2:
                        pe.wait_ge(S["pt_ok"], v - 1)
                    for b in range(4):
                        ins = nc.tensor.transpose(aux[:, 2 + v % 2, b * P:b * P + P], prob[:, v, b * P:b * P + P], ident)
                    ins.then_inc(S["pt_mm"], 1)
                if w >= 2:
                    v = w - 2
                    tile, heads = unit(v)
                    pe.wait_ge(S["pt_ok"], v + 1)
                    b = 0
                    for h in heads:
                        for kt in range(tile + 1):
                            ins = mm(proj_ps[64 * (h % 2):64 * (h % 2) + 64, 1, (h // 2) * T + tile * P:(h // 2) * T + tile * P + P],
                                     mv_sb[:, kt, 64 * h:64 * h + 64], prob_t[:, v, b * P:b * P + P],
                                     start=kt == 0, stop=kt == tile)
                            b += 1
            ins.then_inc(S["ym_mm"], 1)
            pe.wait_ge(S["ym_ok"], 1)
            panel(o2, 2, 0, mix_hi, mix_lo, 4)
            panel(o2, 3, 0, mix_hi, mix_lo, 6, False, True)
            for s in range(SLOTS):
                panel(o2 + 1, s, 1, mix_hi, mix_lo, 2 * s, s == 0, s == 3)
            mean_square(4)
            pe.wait_ge(evac_dve, DVE_OUT2 + 2)

            def up_chunk(c, par):
                pe.wait_ge(evac_act, c + (EVAC_UP - 1))
                chunk(c + GROUP["up"], par, c + landed_group(GROUP["up"]), (S["nrm_lo"], 3 * KT))

            up_chunk(0, 0)
            with pe.Fori(0, 5) as i:
                up_chunk(i * 2 + 1, 1)
                up_chunk(i * 2 + 2, 0)
            for j in range(2):
                par = (j + 1) % 2
                pe.wait_ge(evac_act, EVAC_UP + 10 + j)
                for g in range(3):
                    for s in range(SLOTS):
                        n = g * SLOTS + s
                        if n == 11:
                            continue
                        pe.wait_ge(S["glu_ok"], n + 1)
                        panel(GROUP["down"] + 3 * j + g, s, par, glu_hi, glu_lo, 2 * n, n == 0, n == 10, release=1 + (n == 10))
            mean_square(5)


def kernel(**inputs):
    import numpy as np
    import concourse.bacc as bacc
    from concourse.bass_utils import run_bass_kernel_spmd

    w = {k: np.asarray(v) for k, v in inputs.items()}

    def panels_of(m):
        rows, n = m.shape
        return m.reshape(rows // 256, 2, P, n // 512, 512).transpose(3, 0, 2, 1, 4).reshape(-1, P, 1024)

    w_in, w_mod = w["w_in"][0], panels_of(w["w_mod"][0])
    u0, v0, z0, x0, dt0, g0 = 0, 1024, 2048, 4096, 8192, 8224
    z_gates = panels_of(np.concatenate([w_in[:, z0:x0], w_in[:, g0:g0 + 2048]], 1)).reshape(8, 4, P, 1024)
    alternate = np.stack([z_gates, w_mod[16:].reshape(8, 4, P, 1024)], 1).reshape(-1, P, 1024)
    w2 = w["w_in_2"][0]
    in2 = np.concatenate([w2[:, 1536:2048], w2[:, 2048:2560], w2[:, 2560:3072], w2[:, 1024:1536], w2[:, 0:512],
                          w2[:, 512:1024]], 1)
    out2 = np.concatenate([w["w_out_2"][0][512:], w["w_out_2"][0][:512]], 0)
    half = GLU_TILES * P

    def glu_order(a):
        lead = a.shape[:-1]
        return np.moveaxis(a.reshape(lead + (2, GLU_TILES // 2, 2 * P)), -3, -2).reshape(lead + (2 * half,))

    down = np.concatenate([w["w_ffn_down_2"][0], np.zeros((256, D), np.float32)], 0)
    stream = np.concatenate([
        w_mod[:16], panels_of(w_in[:, v0:z0]), panels_of(w_in[:, u0:v0]), panels_of(w_in[:, x0:dt0]), alternate,
        panels_of(w["w_branch_gm"][0]), panels_of(w["w_branch_ssm"][0]), panels_of(w["w_out"][0]),
        panels_of(w["w_ff1"][0]), panels_of(w["w_ff2"][0]), panels_of(in2), panels_of(out2),
        panels_of(glu_order(w["w_ffn_up_2"][0])), panels_of(down)], 0)

    def tiles(v):
        return np.ascontiguousarray(v.reshape(-1, P).T)

    def taps(m):
        return m.reshape(m.shape[0], -1, P).transpose(2, 1, 0).reshape(P, -1)

    parts = {
        "b_mod": tiles(w["b_mod"][0]), "conv_w": taps(w["conv_w"][0]), "conv_b": tiles(w["conv_b"][0]),
        "gm_norm_w": tiles(w["gm_norm_w"][0]), "ssm_norm_w": tiles(w["ssm_norm_w"][0]),
        "d_skip": tiles(np.repeat(w["d_skip"][0], 64)), "final_norm_w": tiles(w["final_norm_w"]), "c": tiles(w["c"][0]),
        "attn_g": tiles(w["attn_norm_g_2"][0]), "b_gate": tiles(w["b_gate_2"][0]), "gla_g": tiles(w["gla_norm_g_2"][0].reshape(-1)),
        "ffn_g": tiles(w["ffn_norm_g_2"][0]), "fconv_w": taps(glu_order(w["conv_w_2"][0])),
        "fconv_b": tiles(glu_order(w["conv_b_2"][0])), "final_g": tiles(w["final_norm_g_2"]),
        "dt_bias": np.broadcast_to(w["dt_bias"][0], (P, HEADS)), "a_log": np.broadcast_to(w["a_log"][0], (P, HEADS)),
    }
    table = np.concatenate([parts[n] for n, _ in _WIDTHS], 1)

    r = np.arange(P)
    turn = np.zeros((P, P), np.float32)
    lower = r % 64 < 32
    turn[r[lower] + 32, r[lower]] = -1.0
    turn[r[~lower] - 32, r[~lower]] = 1.0
    square = np.stack([(r[:, None] <= r[None, :]), (r[:, None] > r[None, :]), np.eye(P), turn], 1).astype(np.float32)
    inv_freq = (1.0 / (np.float32(10000.0) ** (np.arange(0, 64, 2, dtype=np.float32) / np.float32(64)))).astype(np.float32)
    angle = np.arange(T, dtype=np.float32)[None, :] * inv_freq[r % 32][:, None]
    rope = np.stack([np.cos(angle), np.sin(angle)], 1).astype(np.float32)
    levels = [r[:, None] == r[None, :]]
    for m in LEVELS:
        levels.append((r[:, None] // (2 * m) == r[None, :] // (2 * m)) & (r[:, None] % (2 * m) < m) & (r[None, :] % (2 * m) >= m))
    levels = np.stack(levels, 1).astype(np.float32)
    neg = np.zeros((P, 3, P), np.float32)
    neg[:, 1] = np.where(r[None, :] <= r[:, None], 0.0, NEG)

    def by_row_tile(m):
        return m.reshape(KT, P, -1).transpose(1, 0, 2)

    arrays = {
        "panels": stream, "x_t": by_row_tile(w["x"][0].T), "cols": table, "square": square,
        "ws_t": w["gm_ws"][0].transpose(2, 0, 1), "bs_rows": np.broadcast_to(w["gm_bs"][0], (P, GROUPS_SGU, P)),
        "wdt": by_row_tile(w_in[:, dt0:g0]), "wglr": by_row_tile(w2[:, 3072:3088]), "wgu": w["w_gate_up_2"][0],
        "rope": rope, "levels": levels, "neg": neg,
    }
    nc = bacc.Bacc("TRN2", target_bir_lowering=False, num_devices=1)
    arrays = {"in_" + n: np.ascontiguousarray(a) for n, a in arrays.items()}
    args = [nc.dram_tensor(n, a.shape, F32, kind="ExternalInput").ap() for n, a in arrays.items()]
    out = nc.dram_tensor("out_t", (P, KT, T), F32, kind="ExternalOutput").ap()
    two_blocks(nc, *args, out)
    got = run_bass_kernel_spmd(nc, [arrays], core_ids=[0]).results[0]["out_t"]
    return np.ascontiguousarray(np.asarray(got).transpose(1, 0, 2).reshape(D, T).T)[None]
```

```python
from contextlib import ExitStack, contextmanager

import concourse.bass as bass
from concourse import mybir

ALU = mybir.AluOpType
ACT = mybir.ActivationFunctionType
AX_X = mybir.AxisListType.X
F32 = mybir.dt.float32
F32R = mybir.dt.float32r
U32 = mybir.dt.uint32

P = 128
T = 256
TT = T // P
D = 1024
KT = D // P
EPS = 1e-6
NT = 4
SLOTS = 4
GROUPS_SGU = 8
HEADS = 32
SSD_GROUPS = 8
HPG = HEADS // SSD_GROUPS
FF_TILES = 32
GLU_TILES = 22
GLA_HEADS = 4
MOBA_HEADS = 8
LEVELS = [1, 2, 4, 8, 16, 32, 64]
NEG = -3.0e38

_WIDTHS = [("b_mod", 48), ("conv_w", 32 * 4), ("conv_b", 32), ("gm_norm_w", 8), ("ssm_norm_w", 16), ("d_skip", 16),
           ("final_norm_w", 8), ("c", 8), ("attn_g", 8), ("b_gate", 2), ("gla_g", 4), ("ffn_g", 8),
           ("fconv_w", 44 * 3), ("fconv_b", 44), ("final_g", 8), ("dt_bias", 32), ("a_log", 32)]
COL, NCOLS = {}, 0
for _name, _w in _WIDTHS:
    COL[_name] = NCOLS
    NCOLS += _w

STAGES = [("v", 2, 1), ("u", 2, 1), ("xbc", 8, 1), ("zg", 8, 1), ("gm", 2, 1), ("ssm", 2, 2), ("out", 2, 1),
          ("ff1", 8, 1), ("ff2", 2, 4), ("in2", 6, 1), ("out2", 2, 1), ("up", 11, 1), ("down", 2, 3)]
GROUP, _g = {}, 0
for _name, _c, _n in STAGES:
    GROUP[_name] = _g
    _g += _c * _n
MOD_FIRST = 4
MOD_SPARE = 2
RAW_FIRST = MOD_FIRST - MOD_SPARE
N_SPLIT = _g
N_RAW = _g + 12 - MOD_SPARE
EVAC_XBC, EVAC_ZG, EVAC_FF1, EVAC_IN2, EVAC_UP = 4, 12, 20, 28, 34
RES_OUT, RES_FF2, RES_OUT2, RES_DOWN = 0, 8, 16, 24
N_READY = 6
UNITS = 6
OUT2_PANELS = [(0, 0), (0, 2), (1, 0), (1, 2), (0, 4), (0, 6), (1, 4), (1, 6)]


def landed_group(g):
    if g < GROUP["zg"]:
        return RAW_FIRST + g
    if g < GROUP["gm"]:
        return RAW_FIRST + GROUP["zg"] + 2 * (g - GROUP["zg"])
    return RAW_FIRST + 8 + g


class Steps:

    def __init__(self, eng, sem):
        self.eng, self.sem, self.base, self.n = eng, sem, 0, 0

    def __call__(self, ins):
        self.n += 1
        ins.then_inc(self.sem, 1)
        self.eng.wait_ge(self.sem, self.base + self.n)

    @contextmanager
    def loop(self, trips, per):
        start = self.n
        with self.eng.Fori(0, trips) as i:
            self.base, self.n = i * per + start, 0
            yield i
            assert self.n == per, self.n
        self.base, self.n = 0, start + trips * per


def spread(ap, axis, n):
    ap = ap.unsqueeze(axis)
    shape = list(ap.shape)
    shape[axis] = n
    return ap.broadcast_to(shape)


def two_blocks(nc, panels, x_t, cols_d, square_d, ws_t, bs_rows, wdt_d, wglr_d, wgu_d, rope_d, levels_d, neg_d, out):
    with ExitStack() as ctx:
        def at(name, kb, shape, dt=F32):
            return nc.alloc_sbuf_tensor_at(name, [P] + shape, dt, offset=16896 + int(kb * 1024))

        def sem(name):
            return ctx.enter_context(nc.semaphore(name))

        raw = at("raw", 0, [SLOTS, 1024])
        w_hi = at("w_hi", 16, [SLOTS, 1024], F32R)
        w_lo = at("w_lo", 32, [SLOTS, 1024], F32R)
        spare = at("spare", 16, [MOD_SPARE, SLOTS, 1024])
        xres = at("xres", 48, [KT, T])
        act_hi = at("act_hi", 56, [KT, T], F32R)
        act_lo = at("act_lo", 64, [KT, T], F32R)
        xbc = at("xbc", 72, [32, T])
        zg = at("zg", 104, [32, T])
        u_sb = at("u_sb", 136, [KT, T])
        v_sb = at("v_sb", 144, [TT, D])
        ya_hi = at("ya_hi", 144, [KT, T], F32R)
        ya_lo = at("ya_lo", 136, [KT, T], F32R)
        sgu_t = at("sgu_t", 104, [KT, T])
        yb_hi = at("yb_hi", 104, [16, T], F32R)
        yb_lo = at("yb_lo", 88, [16, T], F32R)
        g_diag = at("g_diag", 152, [4, 4, P])
        g_sq = at("g_sq", 202.5, [2, T])
        g_stat = at("g_stat", 200.5, [2, SSD_GROUPS, TT])
        conv_acc = at("conv_acc", 152, [2, NT, T])
        conv_in = at("conv_in", 160, [2, NT, T + 3])
        stg = at("stg", 152, [2, 4, T])
        a_upto = at("a_upto", 160, [2, HPG, P])
        decay = at("decay", 164, [2, HPG, P])
        xdt = at("xdt", 168, [2, T])
        c_in = at("c_in", 172, [HPG, P])
        state = at("state", 174, [T])
        xw = at("xw", 175, [T])
        b_tok = at("b_tok", 201, [P])
        cbm = at("cbm", 201.5, [2, P])
        tmp_a = at("tmp_a", 160, [KT, T])
        tmp_b = at("tmp_b", 168, [KT, T])
        ff_hi = at("ff_hi", 72, [FF_TILES, T], F32R)
        ff_lo = at("ff_lo", 104, [FF_TILES, T], F32R)
        relu_sb = at("relu_sb", 136, [2, NT * T])
        sq_sb = at("sq_sb", 144, [2, NT * T])
        q_sb = at("q_sb", 72, [4, T])
        k_sb = at("k_sb", 76, [4, T])
        mv_sb = at("mv_sb", 80, [TT, 512])
        gqk = at("gqk", 84, [4, T])
        gv_sb = at("gv_sb", 88, [TT, 512])
        gr_sb = at("gr_sb", 92, [4, T])
        gd = at("gd", 96, [2, 2 * T])
        gx = at("gx", 100, [2, 2 * T])
        scores_t = at("scores_t", 104, [3, GLA_HEADS, P])
        glog = at("glog", 110, [2, T])
        glr_sb = nc.alloc_sbuf_tensor_at("glr_sb", [16, T], F32, offset=16896 + 112 * 1024)
        gt = at("gt", 113, [3, 2, T])
        og = at("og", 119, [GLA_HEADS, T])
        og2 = at("og2", 123, [GLA_HEADS, T])
        rope_c = at("rope_c", 127, [2, NT, T])
        rope_s = at("rope_s", 164, [NT, T])
        og_stat = at("og_stat", 200.5, [2, GLA_HEADS * TT])
        mix_hi = at("mix_hi", 136, [KT, T], F32R)
        mix_lo = at("mix_lo", 144, [KT, T], F32R)
        prob = at("prob", 152, [6, 512])
        prob_t = at("prob_t", 164, [6, 512])
        glu_hi = at("glu_hi", 72, [GLU_TILES, T], F32R)
        glu_lo = at("glu_lo", 94, [GLU_TILES, T], F32R)
        fconv_in = at("fconv_in", 116, [2, NT, T + 2])
        fconv_acc = at("fconv_acc", 125, [2, NT, T])
        glu_sb = at("glu_sb", 133, [2, 2, T])
        cols = at("cols", 176, [NCOLS])
        square = at("square", 178.25, [4, P])
        ones = at("ones", 180.25, [P])
        avg_d = at("avg_d", 180.75, [P])
        avg_g = at("avg_g", 181.25, [P])
        avg_v = at("avg_v", 181.75, [P])
        modc = at("modc", 182.25, [48])
        silu_c = at("silu_c", 182.5, [8])
        eps = at("eps", 182.625, [1])
        zero8 = at("zero8", 182.6875, [8])
        wst = at("wst", 183, [GROUPS_SGU, P])
        bs_sb = at("bs_sb", 187, [GROUPS_SGU, P])
        rope_sb = at("rope_sb", 183, [2, T])
        level_sb = at("level_sb", 185, [8, P])
        neg_sb = at("neg_sb", 189, [3, P])
        wgu = nc.alloc_sbuf_tensor_at("wgu", [16, 2 * P], F32, offset=16896 + int(190.5 * 1024))
        wdt = at("wdt", 191.5, [KT, HEADS])
        wdt_hi = at("wdt_hi", 192.5, [KT, HEADS], F32R)
        wdt_lo = at("wdt_lo", 193.5, [KT, HEADS], F32R)
        wglr = at("wglr", 191.5, [KT, 16])
        wglr_hi = at("wglr_hi", 192.5, [KT, 16], F32R)
        wglr_lo = at("wglr_lo", 193.5, [KT, 16], F32R)
        dts = at("dts", 194.5, [8, TT, HEADS])
        dt_sb, a_sb, wend = dts[:, 0], dts[:, 1], dts[:, 2, 0]
        mod_acc = at("mod_acc", 196.5, [2, 512])
        diag = at("diag", 202.5, [TT, P])
        stat = at("stat", 204.875, [4, TT])
        conv_t = at("conv_t", 169, [NT, T])
        small = at("small", 204.5, [96])
        exp_a = at("exp_a", 205, [HEADS])
        junk = at("junk", 205.25, [16])
        taps_sb = at("taps_sb", 205.5, [20])
        upto, after, ident, turn = (square[:, i, :] for i in range(4))

        proj_ps = ctx.enter_context(nc.psum_tensor("proj_ps", [P, 2, NT * T], F32))
        aux = ctx.enter_context(nc.psum_tensor("aux", [P, 4, 512], F32))

        landed = [sem(f"landed_{s}") for s in range(SLOTS)]
        spare_in = [sem(f"spare_in_{n}") for n in range(MOD_SPARE * SLOTS)]
        hi_done = sem("hi_done")
        taken = sem("taken")
        used = sem("used")
        evac_act = sem("evac_act")
        evac_dve = sem("evac_dve")
        names = {
            "SP or GpSimd or ACT loads": "cols_in x_in early_in sgu_in late_in",
            "an engine's own steps": "act_step dve_step pool_step",
            "memsets and first conversions": "ready padded c_ready wdt_hi_ok wdt_ok ws_masked exp_a_ok",
            "modulation": "spare_used mod_mm mod_done",
            "RMS norms": "sq_done ms_mm rt_done rs_done nrm_t nrm_hi nrm_lo sqw_done rs_mm ratio_ok res_ok",
            "SGU": "v_ss v_rt v_ready sgu_mm sgu_y sgu_hi sgu_done",
            "dt": "dt_mm dt_abs dt_exp dt_u dt_ln dt_ok wend_mm wend_ok",
            "convolution": "conv_pool conv_done xbc_done",
            "SSD": "stg_ok upto_ok xw_ok cin_ok t_mm cb_mm seg_mm cum_mm st_mm y_mm xdt_ok cbm_ok m_ok y_ok "
                   "btok_ok decay_ok ecum_ok state_ok",
            "gated group norm": "silu_z sig_ok g_ok g2_ok gs_mm gs_ok grt_ok gdiag_ok grow_mm yb_f yb_h yb_ok",
            "mixers' sum": "mix_f mix_h mix_ok",
            "first MLP": "sq_ok ffhi_ok ff_ok",
            "GLA": "wglr_hi_ok wglr_ok glr_mm glr_ok gate_mm gx_abs gx_exp gx_u gx_ln g_log lev_d lev_e lev_x lev_mm lev_ok "
                   "og_mm og_sq og_ms og_rt og_diag og_row gla_f gla_h gla_ok",
            "MoBA": "turn_mm cos_ok rope_ok sc_mm max_ok exp_ok p_ok pt_mm pt_ok ym_mm ym_h ym_ok",
            "second MLP": "fpadded fc_pool fc_done fc_silu glu_f glu_h glu_ok",
            "result": "fin_ok stored",
            "a register's wait was carried (read by nobody)": "settled",
        }
        S = {n: sem(n) for line in names.values() for n in line.split()}
        def col(name, k=0, n=1):
            return cols[:, COL[name] + k:COL[name] + k + n]

        def col_at(name, k):
            return cols[:, bass.ds(k + COL[name], 1)]

        block = ctx.enter_context(nc.Block())

        @block.sync
        def _(sp):
            sp.dma_start(cols[:], cols_d).then_inc(S["cols_in"], 16)
            for s in range(SLOTS):
                sp.dma_start(raw[:, s, :], panels[s]).then_inc(landed[s], 16)
            for s in range(SLOTS):
                sp.dma_start(spare[:, 0, s, :], panels[SLOTS + s]).then_inc(spare_in[s], 16)
            sp.dma_start(xres[:], x_t).then_inc(S["x_in"], 16)
            for s in range(SLOTS):
                sp.dma_start(spare[:, 1, s, :], panels[2 * SLOTS + s]).then_inc(spare_in[SLOTS + s], 16)
            with sp.Fori(1, N_RAW) as i:
                for s in range(SLOTS):
                    sp.wait_ge(taken, i * SLOTS + (s + 1 - SLOTS))
                    sp.dma_start(raw[:, s, :], panels[bass.ds(i * SLOTS + (MOD_SPARE * SLOTS + s), 1)].rearrange("a p n -> p (a n)")
                                 ).then_inc(landed[s], 16)
            for q in range(4):
                sp.wait_ge(S["fin_ok"], q + 1)
                sp.dma_start(out[:, 2 * q:2 * q + 2, :], tmp_a[:, 2 * q:2 * q + 2, :]).then_inc(S["stored"], 16)
            sp.wait_ge(S["stored"], 4 * 16)

        def need(eng, s, value):
            if not isinstance(value, int) or value > 0:
                eng.wait_ge(s, value)

        def settle(eng):
            eng.sem_inc(S["settled"], 1)

        def flat(ap):
            return ap.rearrange("p a b -> p (a b)")

        @block.gpsimd
        def _(pool):
            step = Steps(pool, S["pool_step"])
            for dst, src in ((square, square_d), (wdt, wdt_d)):
                pool.dma_start(dst[:], src).then_inc(S["early_in"], 16)
            pool.wait_ge(landed[3], (RAW_FIRST + 2) * 16)
            for dst, src in ((wst, ws_t), (bs_sb, bs_rows)):
                pool.dma_start(dst[:], src).then_inc(S["sgu_in"], 16)
            pool.wait_ge(S["early_in"], 32)
            pool.wait_ge(S["sgu_in"], 32)
            nc.gpsimd.affine_select(out=wst[:], in_=wst[:], pattern=[[0, GROUPS_SGU], [1, P]], base=0,
                                    channel_multiplier=-1, compare_op=ALU.is_ge, fill=0.0).then_inc(S["ws_masked"], 1)

            def two_taps(dst, src, taps, scale, bias, conv_t, done):
                nc.gpsimd.tensor_scalar(out=dst, in0=src[:, taps - 1:taps - 1 + T], scalar1=scale(taps - 1), scalar2=bias,
                                        op0=ALU.mult, op1=ALU.add)
                step(nc.gpsimd.tensor_scalar(out=conv_t, in0=src[:, taps - 2:taps - 2 + T], scalar1=scale(taps - 2),
                                             scalar2=0.0, op0=ALU.mult, op1=ALU.add))
                nc.gpsimd.tensor_tensor(out=dst, in0=dst, in1=conv_t, op=ALU.add).then_inc(done, 1)

            def chunk_taps(c, name, taps):
                for at_col, where, width in ((0, name + "_w", NT * taps), (16, name + "_b", NT)):
                    src = cols[:, bass.ds(c * width + COL[where], width)] if not isinstance(c, int) else col(where, c * width, width)
                    settle(pool)
                    last = nc.gpsimd.tensor_copy(taps_sb[:, at_col:at_col + width], src)
                step(last)
                settle(pool)

            def conv_chunk(c, par):
                pool.wait_ge(evac_act, EVAC_XBC + c + 1)
                need(pool, S["xbc_done"], c)
                need(pool, S["conv_pool"], c * NT)
                chunk_taps(c, "conv", 4)
                for nt in range(NT):
                    two_taps(conv_acc[:, par, nt], conv_in[:, par, nt], 4,
                             lambda j: taps_sb[:, 4 * nt + j:4 * nt + j + 1], taps_sb[:, 16 + nt:17 + nt], conv_t[:, nt], S["conv_pool"])

            per = NT + 1
            conv_chunk(0, 0)
            with step.loop(3, 2 * per) as i:
                conv_chunk(i * 2 + 1, 1)
                conv_chunk(i * 2 + 2, 0)
            conv_chunk(7, 1)

            def ssd_side(g, par):
                pool.wait_ge(S["y_ok"], g + 1)
                settle(pool)
                nc.gpsimd.tensor_copy(stg[:, par, 0:2], xbc[:, bass.ds(g * 2, 2), :])
                nc.gpsimd.tensor_copy(stg[:, par, 2:3], xbc[:, bass.ds(g + 16, 1), :])
                nc.gpsimd.tensor_copy(stg[:, par, 3:4], xbc[:, bass.ds(g + 24, 1), :]).then_inc(S["stg_ok"], 1)
                for c in range(2):
                    pool.wait_ge(S["seg_mm"], g * 2 + (c + 1))
                    if c == 1:
                        pool.wait_ge(S["cum_mm"], g + 1)
                    settle(pool)
                    nc.gpsimd.tensor_tensor(out=a_upto[:, c], in0=spread(dts[:, 1, c, bass.ds(g * HPG, HPG)], 2, P),
                                            in1=spread(upto, 1, HPG), op=ALU.mult).then_inc(S["upto_ok"], 1)
                pool.wait_ge(S["xdt_ok"], g + 1)
                settle(pool)
                nc.gpsimd.tensor_tensor(out=xw[:].rearrange("p (h d) -> p h d", h=HPG),
                                        in0=xdt[:, 0].rearrange("p (h d) -> p h d", h=HPG),
                                        in1=spread(dts[:, 2, 0, bass.ds(g * HPG, HPG)], 2, 64),
                                        op=ALU.mult).then_inc(S["xw_ok"], 1)
                pool.wait_ge(S["ecum_ok"], g + 2)
                nc.gpsimd.tensor_tensor(out=c_in[:], in0=c_in[:], in1=spread(stg[:, par, 3, P:T], 1, HPG),
                                        op=ALU.mult).then_inc(S["cin_ok"], 1)

            pool.wait_ge(S["xbc_done"], 8 + 1)
            pool.wait_ge(S["dt_ok"], 1)
            pool.wait_ge(S["wend_ok"], 1)
            ssd_side(0, 0)
            with pool.Fori(0, 3) as i:
                ssd_side(i * 2 + 1, 1)
                ssd_side(i * 2 + 2, 0)
            ssd_side(7, 1)

            pool.wait_ge(S["late_in"], 80)
            q_all = flat(gqk[:, 0:2])
            k_all = flat(gqk[:, 2:4])
            for e, m in enumerate(LEVELS + [P]):
                halves = lambda ap: ap.rearrange("p (n m) -> p n m", m=2 * m)
                pool.wait_ge(S["lev_e"], e + 1)
                if e >= 2:
                    pool.wait_ge(S["lev_mm"], e)
                nc.gpsimd.tensor_tensor(out=halves(gx[:, e % 2])[:, :, m:2 * m], in0=halves(q_all)[:, :, m:2 * m],
                                        in1=halves(gd[:, e % 2])[:, :, m:2 * m], op=ALU.mult)
                nc.gpsimd.tensor_tensor(out=halves(gx[:, e % 2])[:, :, 0:m], in0=halves(k_all)[:, :, 0:m],
                                        in1=halves(gd[:, e % 2])[:, :, 0:m], op=ALU.mult).then_inc(S["lev_x"], 1)

            for w, x in enumerate((q_sb, k_sb)):
                pool.wait_ge(evac_act, EVAC_IN2 + 2 + w)
                nc.gpsimd.tensor_tensor(out=rope_c[:, w], in0=x[:], in1=spread(rope_sb[:, 0], 1, NT), op=ALU.mult
                                        ).then_inc(S["cos_ok"], 1)

            def fconv_chunk(c, par):
                pool.wait_ge(evac_act, EVAC_UP + c + 1)
                need(pool, S["glu_f"], c)
                need(pool, S["fc_pool"], c * NT)
                chunk_taps(c, "fconv", 3)
                for nt in range(NT):
                    two_taps(fconv_acc[:, par, nt], fconv_in[:, par, nt], 3,
                             lambda j: taps_sb[:, 3 * nt + j:3 * nt + j + 1], taps_sb[:, 16 + nt:17 + nt], conv_t[:, nt], S["fc_pool"])

            fconv_chunk(0, 0)
            with step.loop(5, 2 * per) as i:
                fconv_chunk(i * 2 + 1, 1)
                fconv_chunk(i * 2 + 2, 0)

        @block.scalar
        def _(act):
            def split_hi(g, s, rg=None):
                rg = landed_group(g) if rg is None else rg
                act.wait_ge(landed[s], rg * 16 + 16)
                need(act, used, g * SLOTS + (s + 1 - SLOTS))
                nc.scalar.copy(w_hi[:, s, :], raw[:, s, :]).then_inc(hi_done, 1)

            def split_all(g, rg=None):
                for s in range(SLOTS):
                    split_hi(g, s, rg)

            def evac(dst, g, par, func=ACT.Copy):
                act.wait_ge(used, g * SLOTS + SLOTS)
                if not isinstance(g, int):
                    settle(act)
                src = proj_ps[:, par].rearrange("p (n t) -> p n t", n=dst.shape[1])
                if func == ACT.Copy:
                    return nc.scalar.copy(dst, src).then_inc(evac_act, 1)
                return nc.scalar.activation(dst, src, func).then_inc(evac_act, 1)

            def squares(j, res=None, weight=None):
                for k in range(4 * j, 4 * j + 4):
                    if res is not None:
                        act.wait_ge(S["res_ok"], res + k + 1)
                    nc.scalar.activation(tmp_b[:, k], xres[:, k], ACT.Square).then_inc(S["sq_done"], 1)
                    if weight:
                        nc.scalar.activation(tmp_a[:, k], xres[:, k], ACT.Square, scale=weight(k)).then_inc(S["sqw_done"], 1)

            def root(n, src=None):
                if src is None:
                    act.wait_ge(S["ms_mm"], n + 1)
                nc.scalar.activation(stat[:, 0], aux[:, 2, 0:TT] if src is None else src, ACT.Sqrt, bias=eps[:]
                                     ).then_inc(S["rt_done"], 1)

            def norm_hi(a, shift, beside):
                for k in range(KT):
                    act.wait_ge(S["nrm_t"], KT * a + k + 1)
                    nc.scalar.activation(act_hi[:, k], tmp_a[:, k], ACT.Identity, bias=shift(k)).then_inc(S["nrm_hi"], 1)
                    beside(k)

            def ahead(g):
                return lambda k: split_hi(g, SLOTS - 1) if k == 1 else None

            act.wait_ge(S["cols_in"], 16)
            nc.scalar.activation(silu_c[:], col("c", 0, 8), ACT.Silu).then_inc(S["c_ready"], 1)
            nc.scalar.activation(exp_a[:], col("a_log", 0, HEADS), ACT.Exp).then_inc(S["exp_a_ok"], 1)
            act.wait_ge(S["x_in"], 16)
            for j in range(2):
                squares(j)
            act.wait_ge(S["ready"], N_READY)
            root(0)
            act.wait_ge(S["early_in"], 32)
            nc.scalar.copy(wdt_hi[:], wdt[:]).then_inc(S["wdt_hi_ok"], 1)
            norm_hi(0, lambda k: modc[:, k:k + 1], lambda k: split_hi(0, k // 2) if k % 2 else None)
            for j in range(2):
                split_all(GROUP["v"] + j + 1)
                evac(v_sb[:, :, 512 * j:512 * j + 512], GROUP["v"] + j, j, ACT.Gelu_apprx_tanh)
            act.wait_ge(evac_act, 2)
            for t in range(TT):
                nc.scalar.activation(flat(tmp_b[:, 4 * t:4 * t + 4]), v_sb[:, t], ACT.Square,
                                     accum_out=small[:, t:t + 1]).then_inc(S["v_ss"], 1)
            act.wait_ge(S["v_ss"], 2)
            nc.scalar.activation(small[:, 2:4], small[:, 0:2], ACT.Sqrt, bias=eps[:], scale=1.0 / D).then_inc(S["v_rt"], 1)
            for s in range(SLOTS):
                split_hi(GROUP["u"] + 1, s)
                if s == 0:
                    act.wait_ge(S["dt_abs"], 1)
                    nc.scalar.activation(dts[:, 5], dts[:, 4], ACT.Exp, scale=-1.0).then_inc(S["dt_exp"], 1)
                if s == 1:
                    act.wait_ge(S["dt_u"], 1)
                    nc.scalar.activation(dts[:, 7], dts[:, 6], ACT.Ln).then_inc(S["dt_ln"], 1)
            evac(u_sb[:, 0:4], GROUP["u"], 0, ACT.Gelu_apprx_tanh)
            act.wait_ge(S["wend_mm"], 1)
            nc.scalar.activation(dts[:, 2, 0], aux[:, 1, 0:HEADS], ACT.Exp).then_inc(S["wend_ok"], 1)
            split_all(GROUP["u"] + 2)
            evac(u_sb[:, 4:8], GROUP["u"] + 1, 1, ACT.Gelu_apprx_tanh)
            act.wait_ge(S["padded"], 1)

            def conv_silu(c, par, fixed):
                act.wait_ge(S["conv_done"], c * NT + (NT + NT))
                dst = xbc[:, 4 * c:4 * c + 4] if fixed else xbc[:, bass.ds(c * NT, NT), :]
                settle(act)
                nc.scalar.activation(dst, conv_acc[:, par], ACT.Silu).then_inc(S["xbc_done"], 1)

            def conv_step(c, par, silu=True):
                for s in range(SLOTS):
                    split_hi(c + (GROUP["xbc"] + 1), s, c + (landed_group(GROUP["xbc"]) + 1))
                    if silu and s == 1:
                        conv_silu(c - 2, par, False)
                if isinstance(c, int) and c == 0:
                    act.wait_ge(S["sgu_y"], 2)
                    nc.scalar.copy(ya_hi[:], u_sb[:]).then_inc(S["sgu_hi"], 1)
                need(act, S["conv_done"], c * NT)
                evac(conv_in[:, par, :, 3:3 + T], c + GROUP["xbc"], par)

            conv_step(0, 0, silu=False)
            conv_step(1, 1, silu=False)
            with act.Fori(0, 3) as i:
                conv_step(i * 2 + 2, 0)
                conv_step(i * 2 + 3, 1)
            conv_silu(6, 0, True)
            act.wait_ge(S["sgu_done"], 1)
            act.wait_ge(S["wdt_ok"], 1)
            for dst, src in ((rope_sb, rope_d), (level_sb, levels_d), (neg_sb, neg_d), (wgu, wgu_d), (wglr, wglr_d)):
                act.dma_start(dst[:], src).then_inc(S["late_in"], 16)
            zg0 = landed_group(GROUP["zg"])
            split_all(GROUP["zg"] + 1)
            evac(zg[:, 0:4], GROUP["zg"], 0)
            conv_silu(7, 1, True)

            def gate_silu(g):
                z = zg[:, bass.ds(g * 2, 2), :]
                settle(act)
                nc.scalar.activation(z, z, ACT.Silu).then_inc(S["silu_z"], 1)

            def gated_square(g):
                act.wait_ge(S["g_ok"], g + 1)
                act.wait_ge(S["gs_mm"], g + 1)
                settle(act)
                nc.scalar.activation(g_sq[:], xbc[:, bass.ds(g * 2, 2), :], ACT.Square).then_inc(S["g2_ok"], 1)

            def group_mean(g):
                act.wait_ge(S["gs_mm"], g + 2)
                settle(act)
                nc.scalar.copy(g_stat[:, 0, bass.ds(g, 1)].rearrange("p a t -> p (a t)"), aux[:, 1, 3 * P:3 * P + TT]
                                      ).then_inc(S["gs_ok"], 1)

            def ssd_act(g, par, first=False, last=False):
                act.wait_ge(S["cb_mm"], g + 1)
                nc.scalar.copy(b_tok[:], aux[:, 1, T:T + P]).then_inc(S["btok_ok"], 1)
                for c in range(2):
                    act.wait_ge(S["seg_mm"], g * 2 + (c + 3))
                    nc.scalar.activation(flat(decay[:, c]), aux[:, 2 + c], ACT.Exp).then_inc(S["decay_ok"], 1)
                nxt = g + (GROUP["zg"] + 2)
                landed_nxt = landed_group(nxt) if last else g * 2 + (zg0 + 4)
                split_hi(nxt, 0, landed_nxt)
                act.wait_ge(S["cum_mm"], g + 2)
                nc.scalar.activation(flat(c_in[:]), aux[:, 0], ACT.Exp).then_inc(S["ecum_ok"], 1)
                if not first:
                    gated_square(g - 1)
                split_hi(nxt, 1, landed_nxt)
                act.wait_ge(S["st_mm"], g + 1)
                if not first:
                    group_mean(g - 1)
                nc.scalar.copy(state[:], aux[:, 1, 0:T]).then_inc(S["state_ok"], 1)
                split_hi(nxt, 2, landed_nxt)
                split_hi(nxt, 3, landed_nxt)
                if not last:
                    evac(zg[:, bass.ds(g * NT + NT, NT), :], g + (GROUP["zg"] + 1), 1 - par)
                gate_silu(g)

            ssd_act(0, 0, first=True)
            with act.Fori(0, 3) as i:
                ssd_act(i * 2 + 1, 1)
                ssd_act(i * 2 + 2, 0)
            ssd_act(7, 1, last=True)
            gated_square(7)
            group_mean(7)
            nc.scalar.activation(zg[:, 16:24], zg[:, 16:24], ACT.Sigmoid).then_inc(S["sig_ok"], 1)
            split_hi(GROUP["ssm"], 0)
            act.wait_ge(S["gs_ok"], SSD_GROUPS + 1)
            nc.scalar.activation(g_stat[:, 1], g_stat[:, 0], ACT.Sqrt, bias=eps[:]).then_inc(S["grt_ok"], 1)
            split_hi(GROUP["ssm"], 1)
            nc.scalar.activation(zg[:, 24:32], zg[:, 24:32], ACT.Sigmoid).then_inc(S["sig_ok"], 1)
            for q in range(4):
                act.wait_ge(S["yb_f"], q + 1)
                nc.scalar.copy(yb_hi[:, 4 * q:4 * q + 4], xbc[:, 4 * q:4 * q + 4]).then_inc(S["yb_h"], 1)
                if q < 2:
                    split_hi(GROUP["ssm"], q + 2)
            for j in range(2):
                split_all(GROUP["ssm"] + 2 * j + 1)
                split_all(GROUP["ssm"] + 2 * j + 2)
                act.wait_ge(S["mix_f"], j + 1)
                nc.scalar.copy(act_hi[:, 4 * j:4 * j + 4], zg[:, 16 + 4 * j:20 + 4 * j]).then_inc(S["mix_h"], 1)
            split_all(GROUP["out"] + 1)
            squares(0, RES_OUT)
            for s in range(SLOTS - 1):
                split_hi(GROUP["ff1"], s)
            squares(1, RES_OUT)
            root(1)
            norm_hi(1, lambda k: modc[:, 24 + k:25 + k], ahead(GROUP["ff1"]))
            def ff1_step(c, par):
                split_all(c + (GROUP["ff1"] + 1), c + (landed_group(GROUP["ff1"]) + 1))
                evac(relu_sb[:, par].rearrange("p (n t) -> p n t", n=NT), c + GROUP["ff1"], par, ACT.Relu)
                act.wait_ge(S["sq_ok"], c + 1)
                settle(act)
                nc.scalar.copy(ff_hi[:, bass.ds(c * NT, NT), :], sq_sb[:, par].rearrange("p (n t) -> p n t", n=NT)
                               ).then_inc(S["ffhi_ok"], 1)

            with act.Fori(0, 4) as i:
                ff1_step(i * 2, 0)
                ff1_step(i * 2 + 1, 1)
            final_w = lambda k: col("final_norm_w", k)
            for g in range(4):
                split_all(GROUP["ff2"] + g + 1)
            squares(0, RES_FF2, final_w)
            for g in range(4, 7):
                split_all(GROUP["ff2"] + g + 1)
            for s in range(SLOTS - 1):
                split_hi(GROUP["in2"], s)
            squares(1, RES_FF2, final_w)
            root(2)
            act.wait_ge(S["ratio_ok"], 1)
            root(3, stat[:, 3])
            norm_hi(2, lambda k: zero8[:, k:k + 1], ahead(GROUP["in2"]))
            act.wait_ge(S["late_in"], 80)
            nc.scalar.copy(wglr_hi[:], wglr[:]).then_inc(S["wglr_hi_ok"], 1)

            i2 = GROUP["in2"]

            def level_exp(e):
                m = (LEVELS + [P])[e]
                view = gd[:, e % 2].rearrange("p (n m) -> p n m", m=2 * m)
                act.wait_ge(S["lev_d"], e + 1)
                nc.scalar.activation(view[:, :, m:2 * m], view[:, :, m:2 * m], ACT.Exp)
                nc.scalar.activation(view[:, :, 0:m], view[:, :, 0:m], ACT.Exp, scale=-1.0).then_inc(S["lev_e"], 1)

            split_all(i2 + 1)
            act.wait_ge(used, i2 * SLOTS + SLOTS)
            nc.scalar.activation(gqk[:, 0:2], proj_ps[:, 0, 0:2 * T].rearrange("p (n t) -> p n t", n=2), ACT.Copy, scale=0.125)
            nc.scalar.copy(gqk[:, 2:4], proj_ps[:, 0, 2 * T:].rearrange("p (n t) -> p n t", n=2)).then_inc(evac_act, 1)
            act.wait_ge(S["glr_mm"], 1)
            nc.scalar.copy(glr_sb[:], aux[0:16, 0, 0:T]).then_inc(S["glr_ok"], 1)
            split_hi(i2 + 2, 0)
            act.wait_ge(S["gx_abs"], 1)
            nc.scalar.activation(gt[:, 1], gt[:, 0], ACT.Exp, scale=-1.0).then_inc(S["gx_exp"], 1)
            split_hi(i2 + 2, 1)
            act.wait_ge(S["gx_u"], 1)
            nc.scalar.activation(glog[:], gt[:, 2], ACT.Ln).then_inc(S["gx_ln"], 1)
            split_hi(i2 + 2, 2)
            split_hi(i2 + 2, 3)
            evac(q_sb[:], i2 + 1, 1)
            for s in range(SLOTS):
                level_exp(s)
                split_hi(i2 + 3, s)
            evac(k_sb[:], i2 + 2, 0)
            for s in range(SLOTS):
                level_exp(4 + s)
                split_hi(i2 + 4, s)
            evac(gr_sb[:], i2 + 3, 1, ACT.Silu)
            split_all(i2 + 5)
            evac(gv_sb[:], i2 + 4, 0)

            def moba_exp(w):
                act.wait_ge(S["max_ok"], w + 1)
                n = 4 if w < 2 else 2
                for h in range(n):
                    part = prob[:, w, h * (512 // n):(h + 1) * (512 // n)]
                    last = nc.scalar.activation(part, part, ACT.Exp, bias=small[:, 32 + 4 * w + h:33 + 4 * w + h], scale=0.125,
                                                accum_out=small[:, 64 + 4 * w + h:65 + 4 * w + h])
                last.then_inc(S["exp_ok"], 1)

            def moba_keys(w):
                act.wait_ge(S["pt_mm"], w + 1)
                nc.scalar.copy(prob_t[:, w], aux[:, 1]).then_inc(S["pt_ok"], 1)

            for w in range(2 * SLOTS):
                split_hi(i2 + 6 + w // SLOTS, w % SLOTS)
                if w == 0:
                    act.wait_ge(S["og_mm"], 1)
                    nc.scalar.copy(og[:], proj_ps[:, 0].rearrange("p (n t) -> p n t", n=GLA_HEADS))
                    nc.scalar.activation(og2[:], proj_ps[:, 0].rearrange("p (n t) -> p n t", n=GLA_HEADS), ACT.Square
                                         ).then_inc(S["og_sq"], 1)
                if w < UNITS:
                    moba_exp(w)
                if 1 <= w <= UNITS:
                    moba_keys(w - 1)
                if w == 1:
                    act.wait_ge(S["og_ms"], 1)
                    nc.scalar.activation(og_stat[:, 0], proj_ps[:, 0, 0:GLA_HEADS * TT], ACT.Sqrt, bias=eps[:]).then_inc(S["og_rt"], 1)
                if w == 3:
                    act.wait_ge(S["gla_f"], 1)
                    nc.scalar.copy(mix_hi[:, 0:4], og[:]).then_inc(S["gla_h"], 1)
                    evac(mv_sb[:], i2 + 5, 1)
            act.wait_ge(S["ym_mm"], 1)
            nc.scalar.copy(flat(mix_hi[:, 4:8]), flat(aux[:, 2:4])).then_inc(S["ym_h"], 1)
            squares(0, RES_OUT2)
            for s in range(SLOTS - 1):
                split_hi(GROUP["up"], s)
            squares(1, RES_OUT2)
            root(3)
            norm_hi(3, lambda k: zero8[:, k:k + 1], ahead(GROUP["up"]))
            act.wait_ge(S["fpadded"], 1)

            def gate_silu(c, par):
                act.wait_ge(S["fc_done"], c * NT + (NT + NT))
                nc.scalar.activation(fconv_acc[:, par, 0:2], fconv_acc[:, par, 0:2], ACT.Silu).then_inc(S["fc_silu"], 1)

            def glu_high(c, par, fixed=False):
                act.wait_ge(S["glu_f"], c + 2)
                settle(act)
                dst = glu_hi[:, 2 * c:2 * c + 2] if fixed else glu_hi[:, bass.ds(c * 2, 2), :]
                nc.scalar.copy(dst, glu_sb[:, par]).then_inc(S["glu_h"], 1)

            def up_step(c, par, silu=True, glu=True, fixed=False):
                for s in range(SLOTS):
                    split_hi(c + (GROUP["up"] + 1), s, c + (landed_group(GROUP["up"]) + 1))
                    if glu and s == 1:
                        glu_high(c - 2, par, fixed)
                need(act, S["fc_done"], c * NT)
                evac(fconv_in[:, par, :, 2:2 + T], c + GROUP["up"], par)
                if silu:
                    gate_silu(c - 1, 1 - par)

            up_step(0, 0, silu=False, glu=False)
            up_step(1, 1, glu=False)
            with act.Fori(0, 4) as i:
                up_step(i * 2 + 2, 0)
                up_step(i * 2 + 3, 1)
            up_step(10, 0, fixed=True)
            for s in range(SLOTS):
                split_hi(GROUP["down"] + 1, s)
                if s == 1:
                    glu_high(9, 1, True)
            gate_silu(10, 0)
            glu_high(10, 0, True)
            for j in range(2):
                for g in range(1 - j, 3 - j):
                    split_all(GROUP["down"] + 3 * j + g + 1)
                squares(j, RES_DOWN)
            root(4)

        @block.vector
        def _(dve):
            step = Steps(dve, S["dve_step"])
            tt, ts, stt = nc.vector.tensor_tensor, nc.vector.tensor_scalar, nc.vector.scalar_tensor_tensor

            def split_lo(g, s):
                dve.wait_ge(hi_done, g * SLOTS + (s + 1))
                tt(out=w_lo[:, s, :], in0=raw[:, s, :], in1=w_hi[:, s, :].bitcast(F32), op=ALU.subtract).then_inc(taken, 1)

            def split_all(g):
                for s in range(SLOTS):
                    split_lo(g, s)

            def mod_panel(src, par, s, done, count):
                acc = mod_acc[:, par]
                for k in range(2):
                    half, c_k = src[:, 512 * k:512 * k + 512], silu_c[:, 2 * s + k:2 * s + k + 1]
                    if s == 0 and k == 0:
                        step(ts(out=acc, in0=half, scalar1=c_k, scalar2=0.0, op0=ALU.mult, op1=ALU.add))
                    elif k == 0:
                        step(stt(out=acc, in0=half, scalar=c_k, in1=acc, op0=ALU.mult, op1=ALU.add))
                    else:
                        stt(out=acc, in0=half, scalar=c_k, in1=acc, op0=ALU.mult, op1=ALU.add).then_inc(done, 1)
                        dve.wait_ge(done, count)

            def mod_raw_panel(rg, par, s):
                dve.wait_ge(landed[s], rg * 16 + 16)
                mod_panel(raw[:, s], par, s, taken, rg * SLOTS + (s + 1))

            def mod_evac(m):
                dve.wait_ge(S["mod_mm"], m + 1)
                tt(out=modc[:, bass.ds(m * 4, 4)], in0=aux[:, 3, 0:4], in1=cols[:, bass.ds(m * 4 + COL["b_mod"], 4)],
                   op=ALU.add).then_inc(S["mod_done"], 1)

            def inverse(n, dst):
                dve.wait_ge(S["rt_done"], n + 1)
                step(nc.vector.reciprocal(dst, stat[:, 0]))

            def broadcast(n, src):
                tt(out=diag[:], in0=spread(ident, 1, TT), in1=spread(src, 2, P), op=ALU.mult).then_inc(S["rs_done"], 1)
                dve.wait_ge(S["rs_mm"], n + 1)

            rs_ps = aux[:, 3, 0:T]

            def norm_apply(a, scale, shift, beside):
                for k in range(KT + 2):
                    if k < KT:
                        stt(out=tmp_a[:, k], in0=xres[:, k], scalar=scale(k), in1=rs_ps, op0=ALU.mult,
                            op1=ALU.mult).then_inc(S["nrm_t"], 1)
                    if k >= 2:
                        dve.wait_ge(S["nrm_hi"], KT * a + k - 1)
                        stt(out=act_lo[:, k - 2], in0=tmp_a[:, k - 2], scalar=shift(k - 2), in1=act_hi[:, k - 2].bitcast(F32),
                            op0=ALU.add, op1=ALU.subtract).then_inc(S["nrm_lo"], 1)
                        beside(k - 2)

            def ahead(g):
                return lambda k: split_lo(g, SLOTS - 1) if k == KT - 1 else None

            def softplus_rest(e, u, ln, small_part):
                step(stt(out=small_part, in0=u, scalar=1.0, in1=e, op0=ALU.subtract, op1=ALU.subtract))
                step(nc.vector.reciprocal(u, u))
                step(stt(out=small_part, in0=small_part, scalar=-1.0, in1=u, op0=ALU.mult, op1=ALU.mult))
                step(tt(out=ln, in0=ln, in1=small_part, op=ALU.add))

            def add_residual(j, par, gate=None):
                for nt in range(NT):
                    k = 4 * j + nt
                    src = proj_ps[:, par, nt * T:nt * T + T]
                    if gate is None:
                        last = tt(out=xres[:, k], in0=xres[:, k], in1=src, op=ALU.add)
                    else:
                        last = stt(out=xres[:, k], in0=src, scalar=modc[:, gate + k:gate + k + 1], in1=xres[:, k],
                                   op0=ALU.mult, op1=ALU.add)
                    last.then_inc(S["res_ok"], 1)

            nc.vector.memset(ones[:], 1.0).then_inc(S["ready"], 1)
            nc.vector.memset(avg_d[:], 1.0 / D).then_inc(S["ready"], 1)
            nc.vector.memset(avg_g[:], 1.0 / 256).then_inc(S["ready"], 1)
            nc.vector.memset(avg_v[:], 1.0 / P).then_inc(S["ready"], 1)
            nc.vector.memset(eps[:], EPS).then_inc(S["ready"], 1)
            nc.vector.memset(zero8[:], 0.0).then_inc(S["ready"], 1)
            for n, (name, credit) in enumerate((("conv_done", NT), ("xbc_done", 1), ("seg_mm", 2), ("cum_mm", 1), ("ecum_ok", 1),
                                                ("state_ok", 1), ("y_ok", 2), ("gs_mm", 1), ("gs_ok", 1), ("fc_done", NT), ("glu_f", 1))):
                nc.vector.memset(junk[:, n:n + 1], 0.0).then_inc(S[name], credit)
            dve.wait_ge(S["cols_in"], 16)
            dve.wait_ge(S["c_ready"], 1)
            for s in range(SLOTS):
                mod_raw_panel(0, 0, s)
            for m in range(MOD_SPARE):
                if m == 1:
                    dve.wait_ge(S["mod_mm"], 1)
                for s in range(SLOTS):
                    dve.wait_ge(spare_in[m * SLOTS + s], 16)
                    mod_panel(spare[:, m, s], 1 - m, s, S["spare_used"], m * SLOTS + s + 1)
            inverse(0, stat[:, 1])
            dve.wait_ge(S["early_in"], 32)
            broadcast(0, stat[:, 1])
            dve.wait_ge(S["mod_mm"], 2)
            for s in range(SLOTS):
                mod_raw_panel(1, 1, s)
            dve.wait_ge(S["mod_mm"], MOD_FIRST)
            tt(out=modc[:, 0:16], in0=aux[:, 1, 0:16], in1=col("b_mod", 0, 16), op=ALU.add).then_inc(S["mod_done"], MOD_FIRST)
            dve.wait_ge(S["mod_done"], MOD_FIRST)
            step(ts(out=modc[:, 8:16], in0=modc[:, 8:16], scalar1=1.0, scalar2=None, op0=ALU.add))
            norm_apply(0, lambda k: modc[:, 8 + k:9 + k], lambda k: modc[:, k:k + 1],
                       lambda k: split_lo(0, k // 2) if k % 2 else None)
            dve.wait_ge(S["wdt_hi_ok"], 1)
            tt(out=wdt_lo[:], in0=wdt[:], in1=wdt_hi[:].bitcast(F32), op=ALU.subtract).then_inc(S["wdt_ok"], 1)
            for g in range(1, GROUP["u"] + 1):
                split_all(g)
            u1 = GROUP["u"] + 1
            dve.wait_ge(S["dt_mm"], 1)
            step(tt(out=dts[:, 3], in0=aux[:, 0, 0:TT * HEADS].rearrange("p (t h) -> p t h", t=TT),
                    in1=spread(col("dt_bias", 0, HEADS), 1, TT), op=ALU.add))
            stt(out=dts[:, 4], in0=dts[:, 3], scalar=-1.0, in1=dts[:, 3], op0=ALU.mult, op1=ALU.max).then_inc(S["dt_abs"], 1)
            split_lo(u1, 0)
            dve.wait_ge(S["dt_exp"], 1)
            ts(out=dts[:, 6], in0=dts[:, 5], scalar1=1.0, scalar2=None, op0=ALU.add).then_inc(S["dt_u"], 1)
            split_lo(u1, 1)
            dve.wait_ge(S["dt_ln"], 1)
            softplus_rest(dts[:, 5], dts[:, 6], dts[:, 7], dts[:, 4])
            step(stt(out=dts[:, 0], in0=dts[:, 3], scalar=0.0, in1=dts[:, 7], op0=ALU.max, op1=ALU.add))
            dve.wait_ge(S["exp_a_ok"], 1)
            stt(out=dts[:, 1], in0=dts[:, 0], scalar=-1.0, in1=spread(exp_a[:], 1, TT), op0=ALU.mult,
                op1=ALU.mult).then_inc(S["dt_ok"], 1)
            split_lo(u1, 2)
            dve.wait_ge(S["v_rt"], 1)
            step(nc.vector.reciprocal(small[:, 4:6], small[:, 2:4]))
            for t in range(TT):
                ts(out=v_sb[:, t], in0=v_sb[:, t], scalar1=small[:, 4 + t:5 + t], scalar2=None,
                   op0=ALU.mult).then_inc(S["v_ready"], 1)
            split_lo(u1, 3)
            nc.vector.memset(conv_in[:, :, :, 0:3], 0.0).then_inc(S["padded"], 1)
            split_all(GROUP["xbc"])
            dve.wait_ge(S["sgu_in"], 32)
            dve.wait_ge(evac_act, EVAC_XBC)
            for g in range(GROUPS_SGU):
                if g % 2 == 0:
                    dve.wait_ge(S["sgu_mm"], g // 2 + 1)
                last = stt(out=sgu_t[:, g].rearrange("p (c i) -> p c i", c=TT),
                           in0=aux[:, g // 2, (g % 2) * T:(g % 2) * T + T].rearrange("p (c i) -> p c i", c=TT),
                           scalar=col("gm_norm_w", g), in1=spread(bs_sb[:, g], 1, TT), op0=ALU.mult, op1=ALU.add)
            last.then_inc(S["sgu_y"], 1)
            dve.wait_ge(S["sgu_y"], 1)
            tt(out=u_sb[:], in0=u_sb[:], in1=sgu_t[:], op=ALU.mult).then_inc(S["sgu_y"], 1)
            def last_taps(c, par, nt):
                dve.wait_ge(S["conv_pool"], c * NT + (nt + 1))
                acc, src = conv_acc[:, par, nt], conv_in[:, par, nt]
                w = c * (NT * 4) + nt * 4
                step(stt(out=acc, in0=src[:, 1:1 + T], scalar=col_at("conv_w", w + 1), in1=acc, op0=ALU.mult, op1=ALU.add))
                stt(out=acc, in0=src[:, 0:T], scalar=col_at("conv_w", w), in1=acc, op0=ALU.mult,
                    op1=ALU.add).then_inc(S["conv_done"], 1)

            def conv_step(c, par, first=False, last=False):
                for s in range(SLOTS):
                    if not last:
                        split_lo(c + (GROUP["xbc"] + 1), s)
                    if not first:
                        last_taps(c - 1, 1 - par, s)

            conv_step(0, 0, first=True)
            dve.wait_ge(S["sgu_hi"], 1)
            dve.wait_ge(S["sgu_y"], 2)
            tt(out=ya_lo[:], in0=u_sb[:], in1=ya_hi[:].bitcast(F32), op=ALU.subtract).then_inc(S["sgu_done"], 1)
            conv_step(1, 1)
            with step.loop(3, 2 * NT) as i:
                conv_step(i * 2 + 2, 0)
                conv_step(i * 2 + 3, 1)
            zg0 = landed_group(GROUP["zg"])
            dve.wait_ge(S["mod_mm"], MOD_FIRST - 1)
            for s in range(SLOTS):
                mod_raw_panel(zg0 + 1, 0, s)
            for s in range(SLOTS):
                split_lo(GROUP["zg"] + 1, s)
                last_taps(7, 1, s)
            mod_evac(MOD_FIRST)

            def ssd_dve(g, par, first=False, last=False):
                dve.wait_ge(S["t_mm"], g + 1)
                tt(out=xdt[:].rearrange("p c (h d) -> p c h d", h=HPG),
                   in0=aux[:, 0].rearrange("p (c h d) -> p c h d", c=2, h=HPG),
                   in1=spread(dts[:, 0, :, bass.ds(g * HPG, HPG)], 3, 64), op=ALU.mult).then_inc(S["xdt_ok"], 1)
                dve.wait_ge(S["btok_ok"], g + 1)
                tt(out=cbm[:], in0=aux[:, 1, 0:2 * P].rearrange("p (c i) -> p c i", c=2), in1=spread(upto, 1, 2),
                   op=ALU.mult).then_inc(S["cbm_ok"], 1)
                dve.wait_ge(S["mod_mm"], g + MOD_FIRST)
                for c in range(2):
                    if not last:
                        mod_raw_panel(g * 2 + (zg0 + 3), 1 - par, 2 * c)
                        mod_raw_panel(g * 2 + (zg0 + 3), 1 - par, 2 * c + 1)
                    dve.wait_ge(S["decay_ok"], g * 2 + (c + 1))
                    dve.wait_ge(S["cbm_ok"], g + 1)
                    tt(out=decay[:, c], in0=decay[:, c], in1=spread(cbm[:, c], 1, HPG), op=ALU.mult).then_inc(S["m_ok"], 1)
                for s in range(SLOTS):
                    split_lo(g + (GROUP["zg"] + 2), s)
                dve.wait_ge(S["y_mm"], g + 1)
                for pair in range(2):
                    last_y = stt(out=xbc[:, bass.ds(g * 2 + pair, 1), :].rearrange("p a t -> p (a t)"), in0=stg[:, par, pair],
                                 scalar=col_at("d_skip", g * 2 + pair), in1=aux[:, 2, pair * T:pair * T + T],
                                 op0=ALU.mult, op1=ALU.add)
                last_y.then_inc(S["y_ok"], 1)
                if not last:
                    mod_evac(g + (MOD_FIRST + 1))
                dve.wait_ge(S["silu_z"], g + 1)
                dve.wait_ge(S["y_ok"], g + 3)
                y = xbc[:, bass.ds(g * 2, 2), :]
                tt(out=y, in0=y, in1=zg[:, bass.ds(g * 2, 2), :], op=ALU.mult).then_inc(S["g_ok"], 1)

            ssd_dve(0, 0, first=True)
            with step.loop(3, 2 * SLOTS) as i:
                ssd_dve(i * 2 + 1, 1)
                ssd_dve(i * 2 + 2, 0)
            ssd_dve(7, 1, last=True)
            dve.wait_ge(S["mod_done"], 12)
            step(ts(out=modc[:, 32:40], in0=modc[:, 32:40], scalar1=1.0, scalar2=None, op0=ALU.add))

            def branch_gm(j):
                dve.wait_ge(S["sig_ok"], 1)
                dve.wait_ge(used, (GROUP["gm"] + j + 1) * SLOTS)
                tt(out=zg[:, 16 + 4 * j:20 + 4 * j], in0=zg[:, 16 + 4 * j:20 + 4 * j],
                   in1=proj_ps[:, j].rearrange("p (n t) -> p n t", n=NT), op=ALU.mult).then_inc(evac_dve, 1)

            branch_gm(0)
            dve.wait_ge(S["grt_ok"], 1)
            step(nc.vector.reciprocal(g_stat[:, 1], g_stat[:, 1]))
            for q in range(4):
                tt(out=g_diag[:, q], in0=spread(ident, 1, 4), in1=spread(g_stat[:, 1, 2 * q:2 * q + 2].rearrange("p g t -> p (g t)"), 2, P),
                   op=ALU.mult).then_inc(S["gdiag_ok"], 1)
            split_lo(GROUP["ssm"], 0)
            for q in range(4):
                dve.wait_ge(S["grow_mm"], q + 1)
                for k in range(4 * q, 4 * q + 4):
                    last = stt(out=xbc[:, k], in0=xbc[:, k], scalar=col("ssm_norm_w", k),
                               in1=aux[:, q, (k // 2 % 2) * T:(k // 2 % 2) * T + T], op0=ALU.mult, op1=ALU.mult)
                last.then_inc(S["yb_f"], 1)
                if q < 3:
                    split_lo(GROUP["ssm"], q + 1)
                dve.wait_ge(S["yb_h"], q + 1)
                dve.wait_ge(S["yb_f"], q + 1)
                tt(out=yb_lo[:, 4 * q:4 * q + 4], in0=xbc[:, 4 * q:4 * q + 4], in1=yb_hi[:, 4 * q:4 * q + 4].bitcast(F32),
                   op=ALU.subtract).then_inc(S["yb_ok"], 1)
            branch_gm(1)
            for j in range(2):
                split_all(GROUP["ssm"] + 2 * j + 1)
                split_all(GROUP["ssm"] + 2 * j + 2)
                ga, gb = zg[:, 16 + 4 * j:20 + 4 * j], zg[:, 24 + 4 * j:28 + 4 * j]
                dve.wait_ge(S["sig_ok"], 2)
                dve.wait_ge(used, (GROUP["ssm"] + 2 * j + 2) * SLOTS)
                tt(out=gb, in0=gb, in1=proj_ps[:, j].rearrange("p (n t) -> p n t", n=NT), op=ALU.mult).then_inc(evac_dve, 1)
                dve.wait_ge(evac_dve, 3 + j)
                tt(out=ga, in0=ga, in1=gb, op=ALU.add).then_inc(S["mix_f"], 1)
                dve.wait_ge(S["mix_h"], j + 1)
                dve.wait_ge(S["mix_f"], j + 1)
                tt(out=act_lo[:, 4 * j:4 * j + 4], in0=ga, in1=act_hi[:, 4 * j:4 * j + 4].bitcast(F32),
                   op=ALU.subtract).then_inc(S["mix_ok"], 1)
            for j in range(2):
                for s in range(SLOTS - j):
                    split_lo(GROUP["out"] + j + 1, s)
                dve.wait_ge(used, (GROUP["out"] + j + 1) * SLOTS)
                add_residual(j, j, 16)
            dve.wait_ge(S["res_ok"], RES_OUT + KT)
            inverse(1, stat[:, 1])
            broadcast(1, stat[:, 1])
            norm_apply(1, lambda k: modc[:, 32 + k:33 + k], lambda k: modc[:, 24 + k:25 + k], ahead(GROUP["ff1"]))

            def ff1_step(c, par):
                split_all(c + (GROUP["ff1"] + 1))
                dve.wait_ge(evac_act, c + (EVAC_FF1 + 1))
                tt(out=sq_sb[:, par], in0=relu_sb[:, par], in1=relu_sb[:, par], op=ALU.mult).then_inc(S["sq_ok"], 1)
                dve.wait_ge(S["ffhi_ok"], c + 1)
                tt(out=ff_lo[:, bass.ds(c * NT, NT), :], in0=sq_sb[:, par].rearrange("p (n t) -> p n t", n=NT),
                   in1=ff_hi[:, bass.ds(c * NT, NT), :].bitcast(F32), op=ALU.subtract).then_inc(S["ff_ok"], 1)

            with dve.Fori(0, 4) as i:
                ff1_step(i * 2, 0)
                ff1_step(i * 2 + 1, 1)
            step(tt(out=small[:, 88:96], in0=col("final_norm_w", 0, KT), in1=col("attn_g", 0, KT), op=ALU.mult))
            for j in range(2):
                for g in range(4):
                    for s in range(SLOTS - (j == 1 and g == 3)):
                        split_lo(GROUP["ff2"] + 4 * j + g + 1, s)
                dve.wait_ge(used, (GROUP["ff2"] + 4 * j + 4) * SLOTS)
                add_residual(j, j, 40)
            dve.wait_ge(S["res_ok"], RES_FF2 + KT)
            inverse(2, stat[:, 2])
            step(tt(out=stat[:, 3], in0=stat[:, 2], in1=aux[:, 2, TT:2 * TT], op=ALU.mult))
            tt(out=stat[:, 3], in0=stat[:, 3], in1=stat[:, 2], op=ALU.mult).then_inc(S["ratio_ok"], 1)
            inverse(3, stat[:, 1])
            step(tt(out=stat[:, 1], in0=stat[:, 1], in1=stat[:, 2], op=ALU.mult))
            broadcast(2, stat[:, 1])
            norm_apply(2, lambda k: small[:, 88 + k:89 + k], lambda k: zero8[:, k:k + 1], ahead(GROUP["in2"]))
            dve.wait_ge(S["wglr_hi_ok"], 1)
            tt(out=wglr_lo[:], in0=wglr[:], in1=wglr_hi[:].bitcast(F32), op=ALU.subtract).then_inc(S["wglr_ok"], 1)
            step(nc.vector.memset(scores_t[:], 0.0))
            i2 = GROUP["in2"]
            split_all(i2 + 1)
            dve.wait_ge(S["nrm_t"], 3 * KT)
            broadcast(3, stat[:, 2])
            for k in range(KT):
                last = stt(out=xres[:, k], in0=xres[:, k], scalar=col("final_norm_w", k), in1=rs_ps, op0=ALU.mult, op1=ALU.mult)
            step(last)
            dve.wait_ge(S["gate_mm"], 1)
            for t in range(2):
                last = ts(out=og[:, t], in0=aux[:, 1, t * T:t * T + T], scalar1=col("b_gate", t), scalar2=None, op0=ALU.add)
            step(last)
            stt(out=gt[:, 0], in0=og[:, 0:2], scalar=-1.0, in1=og[:, 0:2], op0=ALU.mult, op1=ALU.max).then_inc(S["gx_abs"], 1)
            split_lo(i2 + 2, 0)
            dve.wait_ge(S["gx_exp"], 1)
            ts(out=gt[:, 2], in0=gt[:, 1], scalar1=1.0, scalar2=None, op0=ALU.add).then_inc(S["gx_u"], 1)
            split_lo(i2 + 2, 1)
            dve.wait_ge(S["gx_ln"], 1)
            softplus_rest(gt[:, 1], gt[:, 2], glog[:], gt[:, 0])
            step(stt(out=gt[:, 0], in0=og[:, 0:2], scalar=0.0, in1=glog[:], op0=ALU.min, op1=ALU.subtract))
            split_lo(i2 + 2, 2)
            step(ts(out=gt[:, 0], in0=gt[:, 0], scalar1=1.0 / 16, scalar2=None, op0=ALU.mult))
            step(nc.vector.memset(gt[:, 1], 1.0))
            for t in range(2):
                last = nc.vector.tensor_tensor_scan(out=glog[:, t], data0=gt[:, 1, t], data1=gt[:, 0, t], initial=0.0,
                                                    op0=ALU.mult, op1=ALU.add)
            step(last)

            def level_diff(e):
                m = (LEVELS + [P])[e]
                view = flat(glog[:]).rearrange("p (n m) -> p n m", m=2 * m)
                if e >= 2:
                    dve.wait_ge(S["lev_x"], e - 1)
                tt(out=gd[:, e % 2].rearrange("p (n m) -> p n m", m=2 * m), in0=view,
                   in1=view[:, :, m - 1:m].broadcast_to(list(view.shape)), op=ALU.subtract).then_inc(S["lev_d"], 1)

            def level_pick(l):
                dve.wait_ge(S["lev_mm"], l + 1)
                bank = 2 * (l % 2)
                if l == 8:
                    nc.vector.tensor_copy(scores_t[:, 2].rearrange("p (a b) i -> p a (b i)", a=2), aux[:, bank:bank + 2, 0:2 * P]
                                          ).then_inc(S["lev_ok"], 1)
                    return
                if l > 0:
                    dve.wait_ge(S["lev_ok"], l)
                for t in range(TT):
                    last = nc.vector.copy_predicated(
                        scores_t[:, t].rearrange("p (a b) i -> p a b i", a=2),
                        spread(spread(level_sb[:, l].bitcast(U32), 1, 2), 1, 2),
                        aux[:, bank:bank + 2, 2 * t * P:2 * t * P + 2 * P].rearrange("p a (b i) -> p a b i", b=2))
                last.then_inc(S["lev_ok"], 1)

            level_diff(0)
            split_lo(i2 + 2, 3)
            for c in range(2):
                for s in range(SLOTS):
                    l = 4 * c + s
                    if l + 1 < 8:
                        level_diff(l + 1)
                    split_lo(i2 + 3 + c, s)
                    level_pick(l)

            def rope(w, x):
                dve.wait_ge(S["turn_mm"], w + 1)
                bank = 2 - 2 * w
                step(tt(out=rope_s[:].rearrange("p (b n) t -> p b n t", b=2),
                        in0=aux[:, bank:bank + 2].rearrange("p b (n t) -> p b n t", n=2),
                        in1=spread(spread(rope_sb[:, 1], 1, 2), 1, 2), op=ALU.mult))
                dve.wait_ge(S["cos_ok"], w + 1)
                tt(out=x[:], in0=rope_c[:, w], in1=rope_s[:], op=ALU.add).then_inc(S["rope_ok"], 1)
                dve.wait_ge(S["rope_ok"], w + 1)

            split_lo(i2 + 5, 0)
            level_pick(8)
            rope(0, q_sb)
            split_lo(i2 + 5, 1)
            rope(1, k_sb)
            split_lo(i2 + 5, 2)
            split_lo(i2 + 5, 3)

            def moba_max(w):
                n = 4 if w < 2 else 2
                dve.wait_ge(S["sc_mm"], w + 1)
                mask = neg_sb[:, 1] if w < 2 else flat(neg_sb[:, 0:2])
                part = prob[:, w].rearrange("p (h k) -> p h k", h=n)
                step(tt(out=part, in0=aux[:, 0].rearrange("p (h k) -> p h k", h=n), in1=spread(mask, 1, n), op=ALU.add))
                step(nc.vector.reduce_max(small[:, 4 * w:4 * w + n], part, AX_X))
                ts(out=small[:, 32 + 4 * w:32 + 4 * w + n], in0=small[:, 4 * w:4 * w + n], scalar1=-0.125, scalar2=None,
                   op0=ALU.mult).then_inc(S["max_ok"], 1)

            def moba_normalise(w):
                n = 4 if w < 2 else 2
                at_sum = 64 + 4 * w
                dve.wait_ge(S["exp_ok"], w + 1)
                step(nc.vector.reciprocal(small[:, at_sum:at_sum + n], small[:, at_sum:at_sum + n]))
                part = prob[:, w].rearrange("p (h k) -> p h k", h=n)
                tt(out=part, in0=part, in1=spread(small[:, at_sum:at_sum + n], 2, 512 // n), op=ALU.mult).then_inc(S["p_ok"], 1)

            for w in range(2 * SLOTS):
                if w < UNITS:
                    moba_max(w)
                split_lo(i2 + 6 + w // SLOTS, w % SLOTS)
                if w < UNITS:
                    moba_normalise(w)
                if w == 1:
                    dve.wait_ge(S["og_rt"], 1)
                    step(nc.vector.reciprocal(og_stat[:, 1], og_stat[:, 0]))
                    tt(out=og2[:].rearrange("p h (t i) -> p (h t) i", t=TT), in0=spread(ident, 1, GLA_HEADS * TT),
                       in1=spread(og_stat[:, 1], 2, P), op=ALU.mult).then_inc(S["og_diag"], 1)
                if w == 2:
                    dve.wait_ge(S["og_row"], 1)
                    step(tt(out=og[:], in0=og[:], in1=proj_ps[:, 0].rearrange("p (n t) -> p n t", n=GLA_HEADS), op=ALU.mult))
                    for h in range(GLA_HEADS):
                        last = stt(out=og[:, h], in0=og[:, h], scalar=col("gla_g", h), in1=gr_sb[:, h], op0=ALU.mult, op1=ALU.mult)
                    last.then_inc(S["gla_f"], 1)
                if w == 3:
                    dve.wait_ge(S["gla_f"], 1)
                    dve.wait_ge(S["gla_h"], 1)
                    tt(out=mix_lo[:, 0:4], in0=og[:], in1=mix_hi[:, 0:4].bitcast(F32), op=ALU.subtract).then_inc(S["gla_ok"], 1)
            dve.wait_ge(S["ym_h"], 1)
            tt(out=flat(mix_lo[:, 4:8]), in0=flat(aux[:, 2:4]), in1=flat(mix_hi[:, 4:8]).bitcast(F32), op=ALU.subtract).then_inc(S["ym_ok"], 1)
            for j in range(2):
                dve.wait_ge(used, GROUP["out2"] * SLOTS + 6 + 2 * j)
                add_residual(j, j)
                if j == 0:
                    for s in range(SLOTS - 1):
                        split_lo(GROUP["up"], s)
            dve.wait_ge(S["res_ok"], RES_OUT2 + KT)
            inverse(4, stat[:, 1])
            broadcast(4, stat[:, 1])
            norm_apply(3, lambda k: col("ffn_g", k), lambda k: zero8[:, k:k + 1], ahead(GROUP["up"]))
            nc.vector.memset(fconv_in[:, :, :, 0:2], 0.0).then_inc(S["fpadded"], 1)

            def glu_product(c, par):
                dve.wait_ge(S["fc_silu"], c + 1)
                tt(out=glu_sb[:, par], in0=fconv_acc[:, par, 0:2], in1=fconv_acc[:, par, 2:4], op=ALU.mult).then_inc(S["glu_f"], 1)

            def glu_low(c, par, fixed=False):
                dve.wait_ge(S["glu_h"], c + 1)
                part = slice(2 * c, 2 * c + 2) if fixed else bass.ds(c * 2, 2)
                tt(out=glu_lo[:, part, :], in0=glu_sb[:, par], in1=glu_hi[:, part, :].bitcast(F32),
                   op=ALU.subtract).then_inc(S["glu_ok"], 1)

            def first_tap(c, par, nt):
                dve.wait_ge(S["fc_pool"], c * NT + (nt + 1))
                acc = fconv_acc[:, par, nt]
                stt(out=acc, in0=fconv_in[:, par, nt, 0:T], scalar=col_at("fconv_w", c * (NT * 3) + nt * 3), in1=acc,
                    op0=ALU.mult, op1=ALU.add).then_inc(S["fc_done"], 1)

            def up_step(c, par, taps=True, glu=True, fixed=False):
                if glu:
                    glu_product(c - 2, par)
                for s in range(SLOTS):
                    split_lo(c + (GROUP["up"] + 1), s)
                    if taps:
                        first_tap(c - 1, 1 - par, s)
                    if glu and s == 2:
                        glu_low(c - 2, par, fixed)

            up_step(0, 0, taps=False, glu=False)
            up_step(1, 1, glu=False)
            with dve.Fori(0, 4) as i:
                up_step(i * 2 + 2, 0)
                up_step(i * 2 + 3, 1)
            up_step(10, 0, fixed=True)
            glu_product(9, 1)
            for s in range(SLOTS):
                split_lo(GROUP["down"] + 1, s)
                first_tap(10, 0, s)
                if s == 2:
                    glu_low(9, 1, True)
            glu_product(10, 0)
            glu_low(10, 0, True)
            for j in range(2):
                for g in range(1 - j, 3 - j):
                    split_all(GROUP["down"] + 3 * j + g + 1)
                dve.wait_ge(used, (GROUP["down"] + 3 * j + 3) * SLOTS)
                add_residual(j, (j + 1) % 2)
            dve.wait_ge(S["res_ok"], RES_DOWN + KT)
            inverse(5, stat[:, 1])
            broadcast(5, stat[:, 1])
            for k in range(KT):
                last = stt(out=tmp_a[:, k], in0=xres[:, k], scalar=col("final_g", k), in1=rs_ps, op0=ALU.mult, op1=ALU.mult)
                if k % 2:
                    last.then_inc(S["fin_ok"], 1)

        @block.tensor
        def _(pe):
            mm = nc.tensor.matmul

            def panel(g, s, par, x_hi, x_lo, k0=0, first=False, last=False, rg=None, ks=2, release=1):
                rg = landed_group(g) if rg is None else rg
                pe.wait_ge(taken, rg * SLOTS + (s + 1))
                for nt in range(NT):
                    dst = proj_ps[:, par, nt * T:nt * T + T]
                    for k in range(ks):
                        hi = w_hi[:, s, k * 512 + nt * P:k * 512 + nt * P + P]
                        lo = w_lo[:, s, k * 512 + nt * P:k * 512 + nt * P + P]
                        xh, xl = x_hi[:, k0 + k], x_lo[:, k0 + k]
                        mm(dst, hi, xh, start=first and k == 0 and nt % 2 == 0, stop=False, skip_group_check=True)
                        mm(dst, hi, xl, start=False, stop=False, skip_group_check=True)
                        ins = mm(dst, lo, xh, start=False, stop=last and k == ks - 1, skip_group_check=True)
                ins.then_inc(used, release)

            def chunk(g, par, rg=None, x_ready=None):
                for s in range(SLOTS):
                    if x_ready:
                        pe.wait_ge(x_ready[0], x_ready[1] + 2 * s + 2)
                    panel(g, s, par, act_hi, act_lo, 2 * s, s == 0, s == SLOTS - 1, rg)

            def token_panel(g, s, par):
                pe.wait_ge(taken, landed_group(g) * SLOTS + (s + 1))
                for t in range(TT):
                    dst = proj_ps[:, par, t * 512:t * 512 + 512]
                    for k in range(2):
                        wh, wl = w_hi[:, s, k * 512:k * 512 + 512], w_lo[:, s, k * 512:k * 512 + 512]
                        xh, xl = (a[:, 2 * s + k, t * P:t * P + P] for a in (act_hi, act_lo))
                        mm(dst, xh, wh, start=s == 0 and k == 0, stop=False)
                        mm(dst, xh, wl, start=False, stop=False)
                        ins = mm(dst, xl, wh, start=False, stop=s == SLOTS - 1 and k == 1)
                ins.then_inc(used, 1)

            def chunk_tokens(g, par, x_ready=None):
                for s in range(SLOTS):
                    if x_ready:
                        pe.wait_ge(x_ready[0], x_ready[1] + 2 * s + 2)
                    token_panel(g, s, par)

            def mean_square(n, j, weighted=False):
                for k in range(4 * j, 4 * j + 4):
                    for w, (sq, done) in enumerate(((tmp_b, "sq_done"), (tmp_a, "sqw_done"))[:1 + weighted]):
                        pe.wait_ge(S[done], (0 if w else KT * n) + k + 1)
                        for t in range(TT):
                            ins = mm(aux[:, 2, w * TT + t:w * TT + t + 1], sq[:, k, t * P:t * P + P], avg_d[:, 0:1],
                                     start=k + w + t == 0, stop=k == KT - 1, skip_group_check=True)
                if j == 1:
                    ins.then_inc(S["ms_mm"], 1)

            def row_of(n):
                pe.wait_ge(S["rs_done"], n + 1)
                mm(aux[:, 3, 0:T], ones[:], flat(diag[:]), start=True, stop=True).then_inc(S["rs_mm"], 1)

            def mod_sum(dst, par):
                for nt in range(NT):
                    ins = mm(dst[:, nt:nt + 1], mod_acc[:, par, nt * P:nt * P + P], ones[:, 0:1], start=True, stop=True)
                ins.then_inc(S["mod_mm"], 1)

            pe.wait_ge(S["ready"], N_READY)
            pe.wait_ge(taken, SLOTS)
            mod_sum(aux[:, 1, 0:4], 0)
            for j in range(2):
                mean_square(0, j)
            pe.wait_ge(S["spare_used"], SLOTS)
            mod_sum(aux[:, 1, 4:8], 1)
            pe.wait_ge(S["spare_used"], 2 * SLOTS)
            mod_sum(aux[:, 1, 8:12], 0)
            row_of(0)
            pe.wait_ge(taken, 2 * SLOTS)
            mod_sum(aux[:, 1, 12:16], 1)
            for j in range(2):
                chunk_tokens(GROUP["v"] + j, j, (S["nrm_lo"], 0))
            pe.wait_ge(S["wdt_ok"], 1)
            for t in range(TT):
                for k in range(KT):
                    xh, xl = (a[:, k, t * P:t * P + P] for a in (act_hi, act_lo))
                    dst = aux[:, 0, t * HEADS:t * HEADS + HEADS]
                    mm(dst, xh, wdt_hi[:, k], start=k == 0, stop=False)
                    mm(dst, xh, wdt_lo[:, k], start=False, stop=False)
                    ins = mm(dst, xl, wdt_hi[:, k], start=False, stop=k == KT - 1)
            ins.then_inc(S["dt_mm"], 1)
            pe.wait_ge(evac_act, 1)
            chunk(GROUP["u"], 0)
            pe.wait_ge(S["dt_ok"], 1)
            pe.wait_ge(S["early_in"], 32)
            mm(aux[:, 1, 0:HEADS], after, dts[:, 1, 0], start=True, stop=True).then_inc(S["wend_mm"], 1)
            pe.wait_ge(evac_act, 2)
            chunk(GROUP["u"] + 1, 1)
            pe.wait_ge(S["v_ready"], 2)
            pe.wait_ge(S["ws_masked"], 1)
            pe.wait_ge(S["wend_ok"], 1)
            for g in range(GROUPS_SGU):
                for c in range(TT):
                    ins = mm(aux[:, g // 2, (g % 2) * T + c * P:(g % 2) * T + c * P + P], v_sb[:, c, g * P:g * P + P],
                             wst[:, g], start=True, stop=True)
                if g % 2:
                    ins.then_inc(S["sgu_mm"], 1)
            with pe.Fori(0, 4) as i:
                for par in range(2):
                    c = i * 2 + par
                    pe.wait_ge(evac_act, c + (EVAC_XBC - 1))
                    chunk(c + GROUP["xbc"], par, c + landed_group(GROUP["xbc"]))
            zg0 = landed_group(GROUP["zg"])
            pe.wait_ge(evac_act, EVAC_ZG - 1)
            chunk(GROUP["zg"], 0)
            pe.wait_ge(S["sgu_y"], 1)
            pe.wait_ge(taken, (zg0 + 2) * SLOTS)
            mod_sum(aux[:, 3, 0:4], 0)

            def group_sum(g):
                pe.wait_ge(S["g2_ok"], g + 1)
                pe.wait_ge(S["gs_ok"], g + 1)
                for k in range(2):
                    for t in range(TT):
                        ins = mm(aux[:, 1, 3 * P + t:3 * P + t + 1], g_sq[:, k, t * P:t * P + P], avg_g[:, 0:1],
                                 start=k + t == 0, stop=k == 1, skip_group_check=True)
                ins.then_inc(S["gs_mm"], 1)

            def ssd(g, par, first=False, last=False):
                x_hi, x_lo = (ya_hi, ya_lo) if last else (act_hi, act_lo)
                zg_panel = lambda s: panel(g + (GROUP["zg"] + 1), s, 1 - par, x_hi, x_lo, 2 * s, s == 0, s == SLOTS - 1,
                                           g * 2 + (zg0 + 2))
                x, b, c_t = stg[:, par, 0:2], stg[:, par, 2], stg[:, par, 3]
                pe.wait_ge(evac_act, g + EVAC_ZG)
                if last:
                    pe.wait_ge(S["sgu_done"], 1)
                zg_panel(0)
                pe.wait_ge(S["stg_ok"], g + 1)
                pe.wait_ge(S["ecum_ok"], g + 1)
                for c in range(2):
                    for pair in range(2):
                        ins = nc.tensor.transpose(aux[:, 0, c * T + pair * P:c * T + pair * P + P], x[:, pair, c * P:c * P + P], ident)
                ins.then_inc(S["t_mm"], 1)
                pe.wait_ge(S["state_ok"], g + 1)
                nc.tensor.transpose(aux[:, 1, T:T + P], b[:, 0:P], ident)
                for c in range(2):
                    ins = mm(aux[:, 1, c * P:c * P + P], b[:, c * P:c * P + P], c_t[:, c * P:c * P + P], start=True, stop=True)
                ins.then_inc(S["cb_mm"], 1)
                for c in range(2):
                    pe.wait_ge(S["upto_ok"], g * 2 + (c + 1))
                    if c == 0:
                        pe.wait_ge(S["y_ok"], g + 2)
                    else:
                        pe.wait_ge(S["mod_done"], g + (MOD_FIRST + 1))
                    mm(aux[:, 2 + c], after, flat(a_upto[:, c]), start=True, stop=True).then_inc(S["seg_mm"], 1)
                zg_panel(1)
                pe.wait_ge(S["xdt_ok"], g + 1)
                mm(aux[:, 0], ones[:], flat(a_upto[:, 1]), start=True, stop=True).then_inc(S["cum_mm"], 1)
                zg_panel(2)
                pe.wait_ge(S["xw_ok"], g + 1)
                pe.wait_ge(S["btok_ok"], g + 1)
                pe.wait_ge(S["cbm_ok"], g + 1)
                if not first:
                    group_sum(g - 1)
                mm(aux[:, 1, 0:T], b_tok[:], xw[:], start=True, stop=True).then_inc(S["st_mm"], 1)
                y = lambda h, c: aux[64 * (h % 2):64 * (h % 2) + 64, 2, (h // 2) * T + c * P:(h // 2) * T + c * P + P]
                pe.wait_ge(S["m_ok"], g * 2 + 1)
                for h in range(HPG):
                    mm(y(h, 0), xdt[:, 0, 64 * h:64 * h + 64], decay[:, 0, h], start=True, stop=True)
                zg_panel(3)
                pe.wait_ge(S["m_ok"], g * 2 + 2)
                pe.wait_ge(S["state_ok"], g + 2)
                pe.wait_ge(S["cin_ok"], g + 1)
                for h in range(HPG):
                    mm(y(h, 1), xdt[:, 1, 64 * h:64 * h + 64], decay[:, 1, h], start=True, stop=False)
                    ins = mm(y(h, 1), state[:, 64 * h:64 * h + 64], c_in[:, h], start=False, stop=True)
                ins.then_inc(S["y_mm"], 1)
                if not last:
                    pe.wait_ge(taken, g * (2 * SLOTS) + (zg0 + 4) * SLOTS)
                    mod_sum(aux[:, 3, 0:4], 1 - par)

            ssd(0, 0, first=True)
            with pe.Fori(0, 3) as i:
                ssd(i * 2 + 1, 1)
                ssd(i * 2 + 2, 0)
            ssd(7, 1, last=True)
            pe.wait_ge(evac_act, EVAC_ZG + 8)
            for s in range(SLOTS):
                panel(GROUP["gm"] + 1, s, 1, ya_hi, ya_lo, 2 * s, s == 0, s == SLOTS - 1)
                if s == 0:
                    group_sum(7)
                for q in ((), (), (0, 1), (2, 3))[s]:
                    pe.wait_ge(S["gdiag_ok"], q + 1)
                    pe.wait_ge(*((S["ecum_ok"], 9), (S["gs_ok"], 9), (S["y_ok"], 10), (S["mod_done"], 12))[q])
                    mm(aux[:, q], ones[:], flat(g_diag[:, q]), start=True, stop=True).then_inc(S["grow_mm"], 1)
            for j in range(2):
                pe.wait_ge(evac_dve, j + 1)
                for g in range(2):
                    for s in range(SLOTS):
                        pe.wait_ge(S["yb_ok"], (8 * g + 2 * s) // 4 + 1)
                        panel(GROUP["ssm"] + 2 * j + g, s, j, yb_hi, yb_lo, 8 * g + 2 * s, g == 0 and s == 0, g == 1 and s == 3)
            for j in range(2):
                pe.wait_ge(evac_dve, 3 + j)
                for s in range(SLOTS):
                    pe.wait_ge(S["mix_ok"], s // 2 + 1)
                    panel(GROUP["out"] + j, s, j, act_hi, act_lo, 2 * s, s == 0, s == 3)
                    if (j, s) == (1, 1):
                        mean_square(1, 0)
            mean_square(1, 1)
            row_of(1)
            pe.wait_ge(S["res_ok"], RES_OUT + KT)
            with pe.Fori(0, 4) as i:
                for par in range(2):
                    c = i * 2 + par
                    pe.wait_ge(evac_act, c + (EVAC_FF1 - 1))
                    chunk(c + GROUP["ff1"], par, c + landed_group(GROUP["ff1"]), (S["nrm_lo"], KT))
            for j in range(2):
                pe.wait_ge(evac_act, EVAC_FF1 + 7 + j)
                for g in range(4):
                    for s in range(SLOTS):
                        pe.wait_ge(S["ff_ok"], (8 * g + 2 * s) // 4 + 1)
                        panel(GROUP["ff2"] + 4 * j + g, s, j, ff_hi, ff_lo, 8 * g + 2 * s, g == 0 and s == 0, g == 3 and s == 3)
                        if (j, g, s) == (1, 1, 0):
                            mean_square(2, 0, True)
            mean_square(2, 1, True)
            row_of(2)
            i2 = GROUP["in2"]
            pe.wait_ge(S["res_ok"], RES_FF2 + KT)
            ready2 = (S["nrm_lo"], 2 * KT)
            chunk(i2, 0, x_ready=ready2)
            pe.wait_ge(S["wglr_ok"], 1)
            for k in range(KT):
                dst = aux[0:16, 0, 0:T]
                mm(dst, wglr_hi[:, k], act_hi[:, k], start=k == 0, stop=False)
                mm(dst, wglr_hi[:, k], act_lo[:, k], start=False, stop=False)
                ins = mm(dst, wglr_lo[:, k], act_hi[:, k], start=False, stop=k == KT - 1)
            ins.then_inc(S["glr_mm"], 1)
            row_of(3)
            panel(i2 + 1, 0, 1, act_hi, act_lo, 0, True)
            pe.wait_ge(S["glr_ok"], 1)
            pe.wait_ge(S["late_in"], 80)
            for t in range(2):
                ins = mm(aux[:, 1, t * T:t * T + T], wgu[:, t * P:t * P + P], glr_sb[:], start=True, stop=True)
            ins.then_inc(S["gate_mm"], 1)
            for s in range(1, SLOTS):
                panel(i2 + 1, s, 1, act_hi, act_lo, 2 * s, False, s == 3)

            def level_mm(l):
                if l == 0:
                    pe.wait_ge(S["gx_abs"], 1)
                else:
                    pe.wait_ge(S["lev_x"], l)
                if l >= 2:
                    pe.wait_ge(S["lev_ok"], l - 1)
                bank = 2 * (l % 2)
                for t in range(1 if l == 8 else TT):
                    for h in range(GLA_HEADS):
                        rows, pair = slice(64 * (h % 2), 64 * (h % 2) + 64), h // 2
                        if l == 0:
                            keys, queries = (gqk[rows, a + pair, t * P:t * P + P] for a in (2, 0))
                        elif l == 8:
                            keys, queries = (gx[rows, (l - 1) % 2, pair * T + a * P:pair * T + a * P + P] for a in (0, 1))
                        else:
                            keys = queries = gx[rows, (l - 1) % 2, pair * T + t * P:pair * T + t * P + P]
                        at_col = (2 * t + pair) * P
                        ins = mm(aux[:, bank + h % 2, at_col:at_col + P], keys, queries, start=True, stop=True)
                ins.then_inc(S["lev_mm"], 1)

            for c in range(2):
                pe.wait_ge(evac_act, EVAC_IN2 + 1 + c)
                for s in range(SLOTS):
                    panel(i2 + 2 + c, s, c, act_hi, act_lo, 2 * s, s == 0, s == 3)
                    level_mm(4 * c + s)
            pe.wait_ge(evac_act, EVAC_IN2 + 3)
            for s in range(SLOTS):
                token_panel(i2 + 4, s, 0)
                if s == 0:
                    level_mm(8)
                if s < 2:
                    pe.wait_ge(S["lev_ok"], 8 + s)
                    for nt in range(NT):
                        ins = mm(aux[:, 2 - 2 * s + nt // 2, (nt % 2) * T:(nt % 2) * T + T], turn, (q_sb, k_sb)[s][:, nt],
                                 start=True, stop=True)
                    ins.then_inc(S["turn_mm"], 1)

            def unit(w):
                return (0, range(w, MOBA_HEADS, 2)) if w < 2 else (1, range(w % 2 + 4 * (w // 2 - 1), 4 * (w // 2), 2))

            def moba_scores(w):
                tile, heads = unit(w)
                if w == 0:
                    pe.wait_ge(S["rope_ok"], 2)
                else:
                    pe.wait_ge(S["max_ok"], w)
                for i, h in enumerate(heads):
                    rows = slice(64 * (h % 2), 64 * (h % 2) + 64)
                    n = P * (tile + 1)
                    ins = mm(aux[:, 0, i * n:i * n + n], q_sb[rows, h // 2, tile * P:tile * P + P],
                             k_sb[rows, h // 2, 0:n], start=True, stop=True)
                ins.then_inc(S["sc_mm"], 1)

            def moba_turn(w):
                pe.wait_ge(S["p_ok"], w + 1)
                need(pe, S["pt_ok"], w)
                for b in range(4):
                    ins = nc.tensor.transpose(aux[:, 1, b * P:b * P + P], prob[:, w, b * P:b * P + P], ident)
                ins.then_inc(S["pt_mm"], 1)

            def moba_values(w):
                tile, heads = unit(w)
                pe.wait_ge(S["pt_ok"], w + 1)
                b = 0
                for h in heads:
                    at_h = (h // 2 % 2) * T + tile * P
                    for kt in range(tile + 1):
                        ins = mm(aux[64 * (h % 2):64 * (h % 2) + 64, 2 + h // 4, at_h:at_h + P],
                                 mv_sb[:, kt, 64 * h:64 * h + 64], prob_t[:, w, b * P:b * P + P],
                                 start=kt == 0, stop=kt == tile)
                        b += 1
                if w == UNITS - 1:
                    ins.then_inc(S["ym_mm"], 1)

            o2 = GROUP["out2"]

            def out2_panel(n):
                j, k0 = OUT2_PANELS[n]
                panel(o2 + n // SLOTS, n % SLOTS, j, mix_hi, mix_lo, k0, k0 == 0, k0 == 6)

            pe.wait_ge(evac_act, EVAC_IN2 + 4)
            for w in range(2 * SLOTS):
                if w < SLOTS:
                    token_panel(i2 + 5, w, 1)
                else:
                    if w == SLOTS:
                        pe.wait_ge(S["gla_ok"], 1)
                        pe.wait_ge(evac_act, EVAC_IN2 + 6)
                    out2_panel(w - SLOTS)
                if w < UNITS:
                    moba_scores(w)
                if w == 0:
                    pe.wait_ge(evac_act, EVAC_IN2 + 5)
                    pe.wait_ge(S["lev_ok"], 9)
                    for h in range(GLA_HEADS):
                        dst = proj_ps[:, 0, h * T:h * T + T]
                        at_h = (h % 2) * 2 + h // 2
                        mm(dst[:, 0:P], gv_sb[:, 0, h * P:h * P + P], scores_t[:, 0, at_h], start=True, stop=True)
                        mm(dst[:, P:T], gv_sb[:, 1, h * P:h * P + P], scores_t[:, 1, at_h], start=True, stop=False)
                        ins = mm(dst[:, P:T], gv_sb[:, 0, h * P:h * P + P], scores_t[:, 2, at_h], start=False, stop=True)
                    ins.then_inc(S["og_mm"], 1)
                if w == 1:
                    pe.wait_ge(S["og_sq"], 1)
                    for h in range(GLA_HEADS):
                        for t in range(TT):
                            ins = mm(proj_ps[:, 0, h * TT + t:h * TT + t + 1], og2[:, h, t * P:t * P + P], avg_v[:, 0:1],
                                     start=True, stop=True)
                    ins.then_inc(S["og_ms"], 1)
                if 1 <= w <= UNITS:
                    moba_turn(w - 1)
                if w == 2:
                    pe.wait_ge(S["og_diag"], 1)
                    for b in range(2):
                        ins = mm(proj_ps[:, 0, b * 512:b * 512 + 512], ones[:], flat(og2[:, 2 * b:2 * b + 2]), start=True, stop=True)
                    ins.then_inc(S["og_row"], 1)
                for v in ((), (), (), (), (0, 1), (2, 3), (4,), (5,))[w]:
                    moba_values(v)
            pe.wait_ge(S["ym_ok"], 1)
            for n in range(4, 8):
                out2_panel(n)
                if n == 6:
                    mean_square(3, 0)
                    mean_square(3, 0)
            mean_square(3, 1)
            row_of(4)
            pe.wait_ge(S["res_ok"], RES_OUT2 + KT)

            def up_chunk(c, par):
                pe.wait_ge(evac_act, c + (EVAC_UP - 1))
                chunk(c + GROUP["up"], par, c + landed_group(GROUP["up"]), (S["nrm_lo"], 3 * KT))

            up_chunk(0, 0)
            with pe.Fori(0, 5) as i:
                up_chunk(i * 2 + 1, 1)
                up_chunk(i * 2 + 2, 0)
            for j in range(2):
                par = (j + 1) % 2
                pe.wait_ge(evac_act, EVAC_UP + 10 + j)
                for g in range(3):
                    for s in range(SLOTS):
                        n = g * SLOTS + s
                        if n == 11:
                            continue
                        pe.wait_ge(S["glu_ok"], n + 1)
                        panel(GROUP["down"] + 3 * j + g, s, par, glu_hi, glu_lo, 2 * n, n == 0, n == 10, release=1 + (n == 10))
                        if (j, n) == (1, 4):
                            mean_square(4, 0)
            mean_square(4, 1)
            row_of(5)



def kernel(**inputs):
    import numpy as np
    import concourse.bacc as bacc
    from concourse.bass_utils import run_bass_kernel_spmd

    w = {k: np.asarray(v) for k, v in inputs.items()}

    def panels_of(m):
        rows, n = m.shape
        return m.reshape(rows // 256, 2, P, n // 512, 512).transpose(3, 0, 2, 1, 4).reshape(-1, P, 1024)

    w_in, w_mod = w["w_in"][0], panels_of(w["w_mod"][0])
    u0, v0, z0, x0, dt0, g0 = 0, 1024, 2048, 4096, 8192, 8224
    z_gates = panels_of(np.concatenate([w_in[:, z0:x0], w_in[:, g0:g0 + 2048]], 1)).reshape(8, 4, P, 1024)
    alternate = np.stack([z_gates, w_mod[16:].reshape(8, 4, P, 1024)], 1).reshape(-1, P, 1024)
    w2 = w["w_in_2"][0]
    in2 = np.concatenate([w2[:, 1536:2048], w2[:, 0:512], w2[:, 512:1024], w2[:, 2560:3072], w2[:, 2048:2560],
                          w2[:, 1024:1536]], 1)
    out2 = np.concatenate([w["w_out_2"][0][512:], w["w_out_2"][0][:512]], 0)
    half = GLU_TILES * P

    def glu_order(a):
        lead = a.shape[:-1]
        return np.moveaxis(a.reshape(lead + (2, GLU_TILES // 2, 2 * P)), -3, -2).reshape(lead + (2 * half,))

    down = np.concatenate([w["w_ffn_down_2"][0], np.zeros((256, D), np.float32)], 0)
    stream = np.concatenate([
        w_mod[:16], panels_of(w_in[:, v0:z0]), panels_of(w_in[:, u0:v0]), panels_of(w_in[:, x0:dt0]), alternate,
        panels_of(w["w_branch_gm"][0]), panels_of(w["w_branch_ssm"][0]), panels_of(w["w_out"][0]),
        panels_of(w["w_ff1"][0]), panels_of(w["w_ff2"][0]), panels_of(in2), panels_of(out2)[[4 * j + k // 2 for j, k in OUT2_PANELS]],
        panels_of(glu_order(w["w_ffn_up_2"][0])), panels_of(down)], 0)

    def tiles(v):
        return np.ascontiguousarray(v.reshape(-1, P).T)

    def taps(m):
        return m.reshape(m.shape[0], -1, P).transpose(2, 1, 0).reshape(P, -1)

    parts = {
        "b_mod": tiles(w["b_mod"][0]), "conv_w": taps(w["conv_w"][0]), "conv_b": tiles(w["conv_b"][0]),
        "gm_norm_w": tiles(w["gm_norm_w"][0]), "ssm_norm_w": tiles(w["ssm_norm_w"][0]),
        "d_skip": tiles(np.repeat(w["d_skip"][0], 64)), "final_norm_w": tiles(w["final_norm_w"]), "c": tiles(w["c"][0]),
        "attn_g": tiles(w["attn_norm_g_2"][0]), "b_gate": tiles(w["b_gate_2"][0]), "gla_g": tiles(w["gla_norm_g_2"][0].reshape(-1)),
        "ffn_g": tiles(w["ffn_norm_g_2"][0]), "fconv_w": taps(glu_order(w["conv_w_2"][0])),
        "fconv_b": tiles(glu_order(w["conv_b_2"][0])), "final_g": tiles(w["final_norm_g_2"]),
        "dt_bias": np.broadcast_to(w["dt_bias"][0], (P, HEADS)), "a_log": np.broadcast_to(w["a_log"][0], (P, HEADS)),
    }
    table = np.concatenate([parts[n] for n, _ in _WIDTHS], 1)

    r = np.arange(P)
    turn = np.zeros((P, P), np.float32)
    lower = r % 64 < 32
    turn[r[lower] + 32, r[lower]] = -1.0
    turn[r[~lower] - 32, r[~lower]] = 1.0
    square = np.stack([(r[:, None] <= r[None, :]), (r[:, None] > r[None, :]), np.eye(P), turn], 1).astype(np.float32)
    inv_freq = (1.0 / (np.float32(10000.0) ** (np.arange(0, 64, 2, dtype=np.float32) / np.float32(64)))).astype(np.float32)
    angle = np.arange(T, dtype=np.float32)[None, :] * inv_freq[r % 32][:, None]
    rope = np.stack([np.cos(angle), np.sin(angle)], 1).astype(np.float32)
    levels = [r[:, None] == r[None, :]]
    for m in LEVELS:
        levels.append((r[:, None] // (2 * m) == r[None, :] // (2 * m)) & (r[:, None] % (2 * m) < m) & (r[None, :] % (2 * m) >= m))
    levels = np.stack(levels, 1).astype(np.float32)
    neg = np.zeros((P, 3, P), np.float32)
    neg[:, 1] = np.where(r[None, :] <= r[:, None], 0.0, NEG)

    def by_row_tile(m):
        return m.reshape(KT, P, -1).transpose(1, 0, 2)

    arrays = {
        "panels": stream, "x_t": by_row_tile(w["x"][0].T), "cols": table, "square": square,
        "ws_t": w["gm_ws"][0].transpose(2, 0, 1), "bs_rows": np.broadcast_to(w["gm_bs"][0], (P, GROUPS_SGU, P)),
        "wdt": by_row_tile(w_in[:, dt0:g0]), "wglr": by_row_tile(w2[:, 3072:3088]), "wgu": w["w_gate_up_2"][0],
        "rope": rope, "levels": levels, "neg": neg,
    }
    nc = bacc.Bacc("TRN2", target_bir_lowering=False, num_devices=1)
    arrays = {"in_" + n: np.ascontiguousarray(a) for n, a in arrays.items()}
    args = [nc.dram_tensor(n, a.shape, F32, kind="ExternalInput").ap() for n, a in arrays.items()]
    out = nc.dram_tensor("out_t", (P, KT, T), F32, kind="ExternalOutput").ap()
    two_blocks(nc, *args, out)
    got = run_bass_kernel_spmd(nc, [arrays], core_ids=[0]).results[0]["out_t"]
    return np.ascontiguousarray(np.asarray(got).transpose(1, 0, 2).reshape(D, T).T)[None]
```

```python
from contextlib import ExitStack, contextmanager

import concourse.bass as bass
from concourse import mybir

ALU = mybir.AluOpType
ACT = mybir.ActivationFunctionType
AX_X = mybir.AxisListType.X
F32 = mybir.dt.float32
F32R = mybir.dt.float32r
U32 = mybir.dt.uint32

P = 128
T = 256
TT = T // P
D = 1024
KT = D // P
EPS = 1e-6
NT = 4
SLOTS = 4
GROUPS_SGU = 8
HEADS = 32
SSD_GROUPS = 8
HPG = HEADS // SSD_GROUPS
FF_TILES = 32
GLU_TILES = 22
GLA_HEADS = 4
MOBA_HEADS = 8
LEVELS = [1, 2, 4, 8, 16, 32, 64]
NEG = -3.0e38

_WIDTHS = [("b_mod", 48), ("conv_w", 32 * 4), ("conv_b", 32), ("gm_norm_w", 8), ("ssm_norm_w", 16), ("d_skip", 16),
           ("final_norm_w", 8), ("c", 8), ("attn_g", 8), ("b_gate", 2), ("gla_g", 4), ("ffn_g", 8),
           ("fconv_w", 44 * 3), ("fconv_b", 44), ("final_g", 8), ("dt_bias", 32), ("a_log", 32)]
COL, NCOLS = {}, 0
for _name, _w in _WIDTHS:
    COL[_name] = NCOLS
    NCOLS += _w

STAGES = [("v", 2, 1), ("u", 2, 1), ("xbc", 8, 1), ("zg", 8, 1), ("gm", 2, 1), ("ssm", 2, 2), ("out", 2, 1),
          ("ff1", 8, 1), ("ff2", 2, 4), ("in2", 6, 1), ("out2", 2, 1), ("up", 11, 1), ("down", 2, 3)]
GROUP, _g = {}, 0
for _name, _c, _n in STAGES:
    GROUP[_name] = _g
    _g += _c * _n
MOD_FIRST = 4
MOD_SPARE = 3
RAW_FIRST = MOD_FIRST - MOD_SPARE
N_RAW = _g + 12 - MOD_SPARE
EVAC_XBC, EVAC_ZG, EVAC_FF1, EVAC_IN2, EVAC_UP = 4, 12, 20, 28, 34
RES_OUT, RES_FF2, RES_OUT2, RES_DOWN = 0, 8, 16, 24
N_READY = 6
UNITS = 6
OUT2_PANELS = [(0, 0), (0, 2), (1, 0), (1, 2), (0, 4), (0, 6), (1, 4), (1, 6)]


def landed_group(g):
    if g <= GROUP["zg"]:
        return RAW_FIRST + g
    if g <= GROUP["gm"]:
        return RAW_FIRST + GROUP["zg"] + 2 * (g - GROUP["zg"]) - 1
    return RAW_FIRST + 8 + g


class Steps:

    def __init__(self, eng, sem):
        self.eng, self.sem, self.base, self.n = eng, sem, 0, 0

    def __call__(self, ins):
        self.n += 1
        ins.then_inc(self.sem, 1)
        self.eng.wait_ge(self.sem, self.base + self.n)

    @contextmanager
    def loop(self, trips, per):
        start = self.n
        with self.eng.Fori(0, trips) as i:
            self.base, self.n = i * per + start, 0
            yield i
            assert self.n == per, self.n
        self.base, self.n = 0, start + trips * per


def spread(ap, axis, n):
    ap = ap.unsqueeze(axis)
    shape = list(ap.shape)
    shape[axis] = n
    return ap.broadcast_to(shape)


def two_blocks(nc, panels, x_t, cols_d, square_d, ws_t, bs_rows, wdt_d, wglr_d, wgu_d, rope_d, levels_d, neg_d, out):
    with ExitStack() as ctx:
        def at(name, kb, shape, dt=F32):
            return nc.alloc_sbuf_tensor_at(name, [P] + shape, dt, offset=16896 + int(kb * 1024))

        def sem(name):
            return ctx.enter_context(nc.semaphore(name))

        raw = at("raw", 0, [SLOTS, 1024])
        w_hi = at("w_hi", 16, [SLOTS, 1024], F32R)
        w_lo = at("w_lo", 32, [SLOTS, 1024], F32R)
        spare = [at(f"spare_{n}", kb, [SLOTS, 1024]) for n, kb in enumerate((16, 32, 104))]
        xres = at("xres", 48, [KT, T])
        act_hi = at("act_hi", 56, [KT, T], F32R)
        act_lo = at("act_lo", 64, [KT, T], F32R)
        xbc = at("xbc", 72, [32, T])
        zg = at("zg", 104, [32, T])
        u_sb = at("u_sb", 136, [KT, T])
        v_sb = at("v_sb", 144, [TT, D])
        ya_hi = at("ya_hi", 144, [KT, T], F32R)
        ya_lo = at("ya_lo", 136, [KT, T], F32R)
        sgu_t = at("sgu_t", 104, [KT, T])
        yb_hi = at("yb_hi", 104, [16, T], F32R)
        yb_lo = at("yb_lo", 88, [16, T], F32R)
        g_diag = at("g_diag", 152, [4, 4, P])
        g_sq = at("g_sq", 202.5, [2, T])
        g_stat = at("g_stat", 200.5, [2, SSD_GROUPS, TT])
        conv_acc = at("conv_acc", 152, [2, NT, T])
        conv_in = at("conv_in", 160, [2, NT, T + 3])
        stg = at("stg", 152, [2, 4, T])
        a_upto_hi = at("a_upto_hi", 160, [2, HPG, P], F32R)
        a_upto_lo = at("a_upto_lo", 183, [2, HPG, P], F32R)
        after_r = at("after_r", 187, [P], F32R)
        ones_r = at("ones_r", 187.5, [P], F32R)
        decay = at("decay", 164, [2, HPG, P])
        xdt = at("xdt", 168, [2, T])
        c_in = at("c_in", 172, [HPG, P])
        state = at("state", 174, [T])
        xw = at("xw", 175, [T])
        b_tok = at("b_tok", 201, [P])
        cbm = at("cbm", 201.5, [2, P])
        tmp_a = at("tmp_a", 160, [KT, T])
        tmp_b = at("tmp_b", 168, [KT, T])
        ff_hi = at("ff_hi", 72, [FF_TILES, T], F32R)
        ff_lo = at("ff_lo", 104, [FF_TILES, T], F32R)
        relu_sb = at("relu_sb", 136, [2, NT * T])
        sq_sb = at("sq_sb", 144, [2, NT * T])
        q_sb = at("q_sb", 72, [4, T])
        k_sb = at("k_sb", 76, [4, T])
        mv_sb = at("mv_sb", 80, [TT, 512])
        gqk = at("gqk", 84, [4, T])
        gv_sb = at("gv_sb", 88, [TT, 512])
        gr_sb = at("gr_sb", 92, [4, T])
        gd = at("gd", 96, [2, 2 * T])
        gx = at("gx", 100, [2, 2 * T])
        scores_t = at("scores_t", 104, [3, GLA_HEADS, P])
        glog = at("glog", 110, [2, T])
        glr_sb = nc.alloc_sbuf_tensor_at("glr_sb", [16, T], F32, offset=16896 + 112 * 1024)
        gt = at("gt", 113, [3, 2, T])
        og = at("og", 119, [GLA_HEADS, T])
        og2 = at("og2", 123, [GLA_HEADS, T])
        rope_c = at("rope_c", 127, [2, NT, T])
        rope_s = at("rope_s", 164, [NT, T])
        og_stat = at("og_stat", 200.5, [2, GLA_HEADS * TT])
        mix_hi = at("mix_hi", 136, [KT, T], F32R)
        mix_lo = at("mix_lo", 144, [KT, T], F32R)
        prob = at("prob", 152, [6, 512])
        prob_t = at("prob_t", 164, [6, 512])
        glu_hi = at("glu_hi", 72, [GLU_TILES, T], F32R)
        glu_lo = at("glu_lo", 94, [GLU_TILES, T], F32R)
        fconv_in = at("fconv_in", 116, [2, NT, T + 2])
        fconv_acc = at("fconv_acc", 125, [2, NT, T])
        glu_sb = at("glu_sb", 133, [2, 2, T])
        cols = at("cols", 176, [NCOLS])
        square = at("square", 178.25, [4, P])
        ones = at("ones", 180.25, [P])
        avg_d = at("avg_d", 180.75, [P])
        avg_g = at("avg_g", 181.25, [P])
        avg_v = at("avg_v", 181.75, [P])
        modc = at("modc", 182.25, [48])
        silu_c = at("silu_c", 182.5, [8])
        eps = at("eps", 182.625, [1])
        zero8 = at("zero8", 182.6875, [8])
        wst = at("wst", 183, [GROUPS_SGU, P])
        bs_sb = at("bs_sb", 187, [GROUPS_SGU, P])
        rope_sb = at("rope_sb", 183, [2, T])
        level_sb = at("level_sb", 185, [8, P])
        neg_sb = at("neg_sb", 189, [2, P])
        wgu = nc.alloc_sbuf_tensor_at("wgu", [16, 2 * P], F32, offset=16896 + int(190.5 * 1024))
        wdt = at("wdt", 191.5, [KT, HEADS])
        wdt_hi = at("wdt_hi", 192.5, [KT, HEADS], F32R)
        wdt_lo = at("wdt_lo", 193.5, [KT, HEADS], F32R)
        wglr = at("wglr", 191.5, [KT, 16])
        wglr_hi = at("wglr_hi", 192.5, [KT, 16], F32R)
        wglr_lo = at("wglr_lo", 193.5, [KT, 16], F32R)
        dts = at("dts", 194.5, [8, TT, HEADS])
        a_hi = at("a_hi", 195.25, [TT, HEADS], F32R)
        a_lo = at("a_lo", 195.5, [TT, HEADS], F32R)
        mod_acc = at("mod_acc", 196.5, [2, 512])
        mod_scaled = at("mod_scaled", 72, [KT, 512])
        mod_pool = at("mod_pool", 88, [512])
        diag = at("diag", 202.5, [TT, P])
        stat = at("stat", 204.875, [4, TT])
        conv_t = at("conv_t", 169, [NT, T])
        small = at("small", 204.5, [96])
        exp_a = at("exp_a", 205, [HEADS])
        junk = at("junk", 205.25, [16])
        taps_sb = at("taps_sb", 205.5, [20])
        upto, after, ident, turn = (square[:, i, :] for i in range(4))

        proj_ps = ctx.enter_context(nc.psum_tensor("proj_ps", [P, 2, NT * T], F32))
        aux = ctx.enter_context(nc.psum_tensor("aux", [P, 4, 512], F32))

        landed = [sem(f"landed_{s}") for s in range(SLOTS)]
        spare_in = [sem(f"spare_in_{n}") for n in range(MOD_SPARE * SLOTS)]
        hi_done = sem("hi_done")
        taken = sem("taken")
        used = sem("used")
        evac_act = sem("evac_act")
        evac_dve = sem("evac_dve")
        names = {
            "SP or GpSimd or ACT loads": "cols_in x_in early_in sgu_in late_in",
            "an engine's own steps": "dve_step pool_step",
            "memsets and first conversions": "ready padded c_ready narrow_hi_ok narrow_ok ws_masked exp_a_ok",
            "modulation": "spare_used scaled_ok pool_sum mod_mm mod_done",
            "RMS norms": "sq_done ms_mm rt_done rs_done nrm_t nrm_hi nrm_lo sqw_done sq_sum sqw_sum rs_mm ratio_ok res_ok",
            "SGU": "v_ss v_rt v_ready sgu_mm sgu_y sgu_hi sgu_done",
            "dt": "dt_mm dt_abs dt_exp dt_u dt_ln dt_ok a_hi_ok a_parts_ok sums_ok wend_mm wend_ok",
            "convolution": "conv_pool conv_done xbc_done",
            "SSD": "stg_ok upto_ok xw_ok cin_ok t_mm cb_mm seg_mm cum_mm st_mm y_mm xdt_ok cbm_ok m_ok y_ok "
                   "btok_ok decay_ok ecum_ok state_ok",
            "gated group norm": "silu_z sig_ok g_ok g2_ok gsq_ok gs_mm gs_ok grt_ok gdiag_ok grow_mm yb_f yb_h yb0_ok yb_ok",
            "mixers' sum": "mix_f mix_h mix_ok",
            "first MLP": "sq_ok ffhi_ok ff_ok",
            "GLA": "glr_mm glr_ok gate_mm gx_abs gx_exp gx_u gx_ln gx_inv lev_d lev_e lev_x lev_mm lev_ok "
                   "og_mm og_sq og_ms og_rt og_diag og_row gla_f gla_h gla_ok",
            "MoBA": "turn_mm cos_ok rope_ok sc_mm max_ok exp_ok p_ok pt_mm pt_ok ym_mm ym_h ym_ok",
            "second MLP": "fpadded fc_pool fc_done fc_silu glu_f glu_h glu_ok",
            "result": "fin_ok stored",
            "a register's wait was carried (read by nobody)": "settled",
        }
        S = {n: sem(n) for line in names.values() for n in line.split()}
        def col(name, k=0, n=1):
            return cols[:, COL[name] + k:COL[name] + k + n]

        def col_at(name, k):
            return cols[:, bass.ds(k + COL[name], 1)]

        block = ctx.enter_context(nc.Block())

        @block.sync
        def _(sp):
            sp.dma_start(cols[:], cols_d).then_inc(S["cols_in"], 16)
            for s in range(SLOTS):
                sp.dma_start(raw[:, s, :], panels[s]).then_inc(landed[s], 16)
            sp.dma_start(xres[:], x_t).then_inc(S["x_in"], 16)
            for s in range(SLOTS):
                for m in range(2):
                    sp.dma_start(spare[m][:, s, :], panels[(m + 1) * SLOTS + s]).then_inc(spare_in[m * SLOTS + s], 16)
            for s in range(SLOTS):
                sp.dma_start(spare[2][:, s, :], panels[3 * SLOTS + s]).then_inc(spare_in[2 * SLOTS + s], 16)
            with sp.Fori(1, N_RAW) as i:
                for s in range(SLOTS):
                    sp.wait_ge(taken, i * SLOTS + (s + 1 - SLOTS))
                    sp.dma_start(raw[:, s, :], panels[bass.ds(i * SLOTS + (MOD_SPARE * SLOTS + s), 1)].rearrange("a p n -> p (a n)")
                                 ).then_inc(landed[s], 16)
            for q in range(4):
                sp.wait_ge(S["fin_ok"], q + 1)
                sp.dma_start(out[:, 2 * q:2 * q + 2, :], tmp_a[:, 2 * q:2 * q + 2, :]).then_inc(S["stored"], 16)
            sp.wait_ge(S["stored"], 4 * 16)

        def need(eng, s, value):
            if not isinstance(value, int) or value > 0:
                eng.wait_ge(s, value)

        def settle(eng):
            eng.sem_inc(S["settled"], 1)

        def flat(ap):
            return ap.rearrange("p a b -> p (a b)")

        @block.gpsimd
        def _(pool):
            step = Steps(pool, S["pool_step"])
            for dst, src in ((square, square_d), (wdt, wdt_d)):
                pool.dma_start(dst[:], src).then_inc(S["early_in"], 16)
            for k in range(1, KT):
                pool.wait_ge(S["scaled_ok"], k + 1)
                ins = nc.gpsimd.tensor_tensor(out=mod_pool[:], in0=mod_scaled[:, 0] if k == 1 else mod_pool[:], in1=mod_scaled[:, k],
                                              op=ALU.add)
                if k < KT - 1:
                    step(ins)
            ins.then_inc(S["pool_sum"], 1)
            pool.wait_ge(landed[3], (RAW_FIRST + 1) * 16)
            for dst, src in ((wst, ws_t), (bs_sb, bs_rows)):
                pool.dma_start(dst[:], src).then_inc(S["sgu_in"], 16)
            pool.wait_ge(S["early_in"], 32)
            pool.wait_ge(S["sgu_in"], 32)
            nc.gpsimd.affine_select(out=wst[:], in_=wst[:], pattern=[[0, GROUPS_SGU], [1, P]], base=0,
                                    channel_multiplier=-1, compare_op=ALU.is_ge, fill=0.0).then_inc(S["ws_masked"], 1)

            def two_taps(dst, src, taps, scale, bias, conv_t, done):
                nc.gpsimd.tensor_scalar(out=dst, in0=src[:, taps - 1:taps - 1 + T], scalar1=scale(taps - 1), scalar2=bias,
                                        op0=ALU.mult, op1=ALU.add)
                step(nc.gpsimd.tensor_scalar(out=conv_t, in0=src[:, taps - 2:taps - 2 + T], scalar1=scale(taps - 2),
                                             scalar2=0.0, op0=ALU.mult, op1=ALU.add))
                nc.gpsimd.tensor_tensor(out=dst, in0=dst, in1=conv_t, op=ALU.add).then_inc(done, 1)

            def chunk_taps(c, name, taps):
                for at_col, where, width in ((0, name + "_w", NT * taps), (16, name + "_b", NT)):
                    src = cols[:, bass.ds(c * width + COL[where], width)] if not isinstance(c, int) else col(where, c * width, width)
                    settle(pool)
                    last = nc.gpsimd.tensor_copy(taps_sb[:, at_col:at_col + width], src)
                step(last)
                settle(pool)

            def conv_chunk(c, par, tiles=NT):
                pool.wait_ge(evac_act, EVAC_XBC + c + 1)
                need(pool, S["xbc_done"], c)
                need(pool, S["conv_pool"], c * NT)
                chunk_taps(c, "conv", 4)
                for nt in range(tiles):
                    two_taps(conv_acc[:, par, nt], conv_in[:, par, nt], 4,
                             lambda j: taps_sb[:, 4 * nt + j:4 * nt + j + 1], taps_sb[:, 16 + nt:17 + nt], conv_t[:, nt], S["conv_pool"])

            per = NT + 1
            conv_chunk(0, 0)
            with step.loop(3, 2 * per) as i:
                conv_chunk(i * 2 + 1, 1)
                conv_chunk(i * 2 + 2, 0)
            conv_chunk(7, 1, tiles=2)

            def ssd_side(g, par, first=False):
                pool.wait_ge(S["y_ok"], g + 1)
                settle(pool)
                nc.gpsimd.tensor_copy(stg[:, par, 0:2], xbc[:, bass.ds(g * 2, 2), :])
                nc.gpsimd.tensor_copy(stg[:, par, 2:3], xbc[:, bass.ds(g + 16, 1), :])
                nc.gpsimd.tensor_copy(stg[:, par, 3:4], xbc[:, bass.ds(g + 24, 1), :]).then_inc(S["stg_ok"], 1)
                for c in range(2):
                    pool.wait_ge(S["seg_mm"], g * 2 + (c + 1))
                    if c == 1:
                        pool.wait_ge(S["cum_mm"], g + 1)
                    settle(pool)
                    nc.gpsimd.tensor_tensor(out=a_upto_hi[:, c], in0=spread(a_hi[:, c, bass.ds(g * HPG, HPG)].bitcast(F32), 2, P),
                                            in1=spread(upto, 1, HPG), op=ALU.mult)
                    nc.gpsimd.tensor_tensor(out=a_upto_lo[:, c], in0=spread(a_lo[:, c, bass.ds(g * HPG, HPG)].bitcast(F32), 2, P),
                                            in1=spread(upto, 1, HPG), op=ALU.mult).then_inc(S["upto_ok"], 1)
                if not first:
                    pool.wait_ge(S["g2_ok"], g)
                    nc.gpsimd.tensor_tensor(out=g_sq[:, 0], in0=g_sq[:, 0], in1=g_sq[:, 1], op=ALU.add).then_inc(S["gsq_ok"], 1)
                pool.wait_ge(S["xdt_ok"], g + 1)
                settle(pool)
                nc.gpsimd.tensor_tensor(out=xw[:].rearrange("p (h d) -> p h d", h=HPG),
                                        in0=xdt[:, 0].rearrange("p (h d) -> p h d", h=HPG),
                                        in1=spread(dts[:, 2, 0, bass.ds(g * HPG, HPG)], 2, 64),
                                        op=ALU.mult).then_inc(S["xw_ok"], 1)
                pool.wait_ge(S["ecum_ok"], g + 2)
                nc.gpsimd.tensor_tensor(out=c_in[:], in0=c_in[:], in1=spread(stg[:, par, 3, P:T], 1, HPG),
                                        op=ALU.mult).then_inc(S["cin_ok"], 1)

            pool.wait_ge(S["xbc_done"], 7 + 1)
            pool.wait_ge(S["a_parts_ok"], 1)
            pool.wait_ge(S["sgu_done"], 1)
            pool.wait_ge(S["wend_ok"], 1)
            ssd_side(0, 0, first=True)
            pool.wait_ge(S["xbc_done"], 8 + 1)
            with pool.Fori(0, 3) as i:
                ssd_side(i * 2 + 1, 1)
                ssd_side(i * 2 + 2, 0)
            ssd_side(7, 1)


            for q in range(1, 4):
                pool.wait_ge(S["yb_h"], q + 1)
                nc.gpsimd.tensor_tensor(out=yb_lo[:, 4 * q:4 * q + 4], in0=xbc[:, 4 * q:4 * q + 4],
                                        in1=yb_hi[:, 4 * q:4 * q + 4].bitcast(F32), op=ALU.subtract).then_inc(S["yb_ok"], 1)

            def sum_squares(n, weighted=False):
                for sq, done, summed in ((tmp_b, "sq_done", "sq_sum"), (tmp_a, "sqw_done", "sqw_sum"))[:1 + weighted]:
                    pool.wait_ge(S[done], (KT * n if sq is tmp_b else 0) + 4)
                    step(nc.gpsimd.tensor_tensor(out=sq[:, 0:2], in0=sq[:, 0:2], in1=sq[:, 2:4], op=ALU.add))
                    nc.gpsimd.tensor_tensor(out=sq[:, 0], in0=sq[:, 0], in1=sq[:, 1], op=ALU.add).then_inc(S[summed], 1)

            sum_squares(1)
            sum_squares(2, True)
            pool.wait_ge(S["late_in"], 80)
            q_all = flat(gqk[:, 0:2])
            k_all = flat(gqk[:, 2:4])
            for e, m in enumerate(LEVELS + [P]):
                halves = lambda ap: ap.rearrange("p (n m) -> p n m", m=2 * m)
                pool.wait_ge(S["lev_e"], e + 1)
                if e >= 2:
                    pool.wait_ge(S["lev_mm"], e)
                nc.gpsimd.tensor_tensor(out=halves(gx[:, e % 2])[:, :, m:2 * m], in0=halves(q_all)[:, :, m:2 * m],
                                        in1=halves(gd[:, e % 2])[:, :, m:2 * m], op=ALU.mult)
                nc.gpsimd.tensor_tensor(out=halves(gx[:, e % 2])[:, :, 0:m], in0=halves(k_all)[:, :, 0:m],
                                        in1=halves(gd[:, e % 2])[:, :, 0:m], op=ALU.mult).then_inc(S["lev_x"], 1)

            for w, x in enumerate((q_sb, k_sb)):
                pool.wait_ge(evac_act, EVAC_IN2 + 2 + w)
                nc.gpsimd.tensor_tensor(out=rope_c[:, w], in0=x[:], in1=spread(rope_sb[:, 0], 1, NT), op=ALU.mult
                                        ).then_inc(S["cos_ok"], 1)

            sum_squares(3)
            def fconv_chunk(c, par):
                pool.wait_ge(evac_act, EVAC_UP + c + 1)
                need(pool, S["glu_f"], c)
                need(pool, S["fc_pool"], c * NT)
                chunk_taps(c, "fconv", 3)
                for nt in range(NT):
                    two_taps(fconv_acc[:, par, nt], fconv_in[:, par, nt], 3,
                             lambda j: taps_sb[:, 3 * nt + j:3 * nt + j + 1], taps_sb[:, 16 + nt:17 + nt], conv_t[:, nt], S["fc_pool"])

            fconv_chunk(0, 0)
            with step.loop(5, 2 * per) as i:
                fconv_chunk(i * 2 + 1, 1)
                fconv_chunk(i * 2 + 2, 0)
            sum_squares(4)

        @block.scalar
        def _(act):
            def split_hi(g, s, rg=None):
                rg = landed_group(g) if rg is None else rg
                act.wait_ge(landed[s], rg * 16 + 16)
                need(act, used, g * SLOTS + (s + 1 - SLOTS))
                nc.scalar.copy(w_hi[:, s, :], raw[:, s, :]).then_inc(hi_done, 1)

            def split_all(g, rg=None):
                for s in range(SLOTS):
                    split_hi(g, s, rg)

            def evac(dst, g, par, func=ACT.Copy):
                act.wait_ge(used, g * SLOTS + SLOTS)
                if not isinstance(g, int):
                    settle(act)
                src = proj_ps[:, par].rearrange("p (n t) -> p n t", n=dst.shape[1])
                if func == ACT.Copy:
                    return nc.scalar.copy(dst, src).then_inc(evac_act, 1)
                return nc.scalar.activation(dst, src, func).then_inc(evac_act, 1)

            def squares(j, res=None, weight=None):
                for k in range(4 * j, 4 * j + 4):
                    if res is not None:
                        act.wait_ge(S["res_ok"], res + k + 1)
                    nc.scalar.activation(tmp_b[:, k], xres[:, k], ACT.Square).then_inc(S["sq_done"], 1)
                    if weight:
                        nc.scalar.activation(tmp_a[:, k], xres[:, k], ACT.Square, scale=weight(k)).then_inc(S["sqw_done"], 1)

            def root(n, src=None):
                if src is None:
                    act.wait_ge(S["ms_mm"], n + 1)
                nc.scalar.activation(stat[:, 0], aux[:, 2, 0:TT] if src is None else src, ACT.Sqrt, bias=eps[:]
                                     ).then_inc(S["rt_done"], 1)

            def norm_hi(a, shift, beside):
                for k in range(KT):
                    act.wait_ge(S["nrm_t"], KT * a + k + 1)
                    nc.scalar.activation(act_hi[:, k], tmp_a[:, k], ACT.Identity, bias=shift(k)).then_inc(S["nrm_hi"], 1)
                    beside(k)

            def ahead(g):
                return lambda k: split_hi(g, SLOTS - 1) if k == 3 else None

            act.wait_ge(S["cols_in"], 16)
            act.wait_ge(S["ready"], N_READY)
            nc.scalar.activation(silu_c[:], col("c", 0, 8), ACT.Silu).then_inc(S["c_ready"], 1)
            nc.scalar.activation(exp_a[:], col("a_log", 0, HEADS), ACT.Exp).then_inc(S["exp_a_ok"], 1)
            act.wait_ge(S["x_in"], 16)
            for j in range(2):
                squares(j)
            act.wait_ge(S["c_ready"], 1)
            for k in range(KT):
                act.wait_ge(spare_in[k // 2], 16)
                nc.scalar.activation(mod_scaled[:, k], spare[0][:, k // 2, 512 * (k % 2):512 * (k % 2) + 512], ACT.Identity,
                                     bias=zero8[:, 0:1], scale=silu_c[:, k:k + 1]).then_inc(S["scaled_ok"], 1)
            act.wait_ge(S["ready"], N_READY)
            root(0)
            act.wait_ge(S["early_in"], 32)
            nc.scalar.copy(wdt_hi[:], wdt[:]).then_inc(S["narrow_hi_ok"], 1)
            norm_hi(0, lambda k: modc[:, k:k + 1], lambda k: split_hi(0, k // 2) if k % 2 else None)
            for j in range(2):
                split_all(GROUP["v"] + j + 1)
                evac(v_sb[:, :, 512 * j:512 * j + 512], GROUP["v"] + j, j, ACT.Gelu_apprx_tanh)
            act.wait_ge(evac_act, 2)
            for t in range(TT):
                nc.scalar.activation(flat(tmp_b[:, 4 * t:4 * t + 4]), v_sb[:, t], ACT.Square,
                                     accum_out=small[:, t:t + 1]).then_inc(S["v_ss"], 1)
            act.wait_ge(S["v_ss"], 2)
            nc.scalar.activation(small[:, 2:4], small[:, 0:2], ACT.Sqrt, bias=eps[:], scale=1.0 / D).then_inc(S["v_rt"], 1)
            for s in range(SLOTS):
                split_hi(GROUP["u"] + 1, s)
                if s == 0:
                    act.wait_ge(S["dt_abs"], 1)
                    nc.scalar.activation(dts[:, 5], dts[:, 4], ACT.Exp, scale=-1.0).then_inc(S["dt_exp"], 1)
                if s == 1:
                    act.wait_ge(S["dt_u"], 1)
                    nc.scalar.activation(dts[:, 7], dts[:, 6], ACT.Ln).then_inc(S["dt_ln"], 1)
            evac(u_sb[:, 0:4], GROUP["u"], 0, ACT.Gelu_apprx_tanh)
            act.wait_ge(S["dt_ok"], 1)
            nc.scalar.copy(a_hi[:], dts[:, 1]).then_inc(S["a_hi_ok"], 1)
            act.wait_ge(S["wend_mm"], 1)
            nc.scalar.activation(dts[:, 2, 0], aux[:, 1, 0:HEADS], ACT.Exp).then_inc(S["wend_ok"], 1)
            split_all(GROUP["u"] + 2)
            evac(u_sb[:, 4:8], GROUP["u"] + 1, 1, ACT.Gelu_apprx_tanh)
            act.wait_ge(S["padded"], 1)

            def conv_silu(c, par, fixed):
                act.wait_ge(S["conv_done"], c * NT + (NT + NT))
                dst = xbc[:, 4 * c:4 * c + 4] if fixed else xbc[:, bass.ds(c * NT, NT), :]
                settle(act)
                nc.scalar.activation(dst, conv_acc[:, par], ACT.Silu).then_inc(S["xbc_done"], 1)

            def conv_step(c, par, silu=True):
                for s in range(SLOTS):
                    split_hi(c + (GROUP["xbc"] + 1), s, c + (landed_group(GROUP["xbc"]) + 1))
                    if silu and s == 1:
                        conv_silu(c - 2, par, False)
                if isinstance(c, int) and c == 0:
                    act.wait_ge(S["sgu_y"], 2)
                    nc.scalar.copy(ya_hi[:], u_sb[:]).then_inc(S["sgu_hi"], 1)
                need(act, S["conv_done"], c * NT)
                evac(conv_in[:, par, :, 3:3 + T], c + GROUP["xbc"], par)

            conv_step(0, 0, silu=False)
            conv_step(1, 1, silu=False)
            with act.Fori(0, 3) as i:
                conv_step(i * 2 + 2, 0)
                conv_step(i * 2 + 3, 1)
            conv_silu(6, 0, True)
            act.wait_ge(S["sgu_done"], 1)
            nc.scalar.copy(after_r[:], after)
            nc.scalar.copy(ones_r[:], ones[:]).then_inc(S["sums_ok"], 1)
            zg0 = landed_group(GROUP["zg"])
            for s in range(SLOTS):
                split_hi(GROUP["zg"] + 1, s)
                if s == 0:
                    conv_silu(7, 1, True)
            evac(zg[:, 0:4], GROUP["zg"], 0)

            def gate_silu(g):
                z = zg[:, bass.ds(g * 2, 2), :]
                settle(act)
                nc.scalar.activation(z, z, ACT.Silu).then_inc(S["silu_z"], 1)

            def gated_square(g):
                act.wait_ge(S["g_ok"], g + 1)
                act.wait_ge(S["gs_mm"], g + 1)
                settle(act)
                nc.scalar.activation(g_sq[:], xbc[:, bass.ds(g * 2, 2), :], ACT.Square).then_inc(S["g2_ok"], 1)

            def group_mean(g):
                act.wait_ge(S["gs_mm"], g + 2)
                settle(act)
                nc.scalar.copy(g_stat[:, 0, bass.ds(g, 1)].rearrange("p a t -> p (a t)"), aux[:, 1, 3 * P:3 * P + TT]
                                      ).then_inc(S["gs_ok"], 1)

            def ssd_act(g, par, first=False, last=False):
                act.wait_ge(S["cb_mm"], g + 1)
                nc.scalar.copy(b_tok[:], aux[:, 1, T:T + P]).then_inc(S["btok_ok"], 1)
                for c in range(2):
                    act.wait_ge(S["seg_mm"], g * 2 + (c + 3))
                    nc.scalar.activation(flat(decay[:, c]), aux[:, 2 + c], ACT.Exp).then_inc(S["decay_ok"], 1)
                nxt = g + (GROUP["zg"] + 2)
                landed_nxt = landed_group(nxt) if last else g * 2 + (zg0 + 3)
                split_hi(nxt, 0, landed_nxt)
                act.wait_ge(S["cum_mm"], g + 2)
                nc.scalar.activation(flat(c_in[:]), aux[:, 0], ACT.Exp).then_inc(S["ecum_ok"], 1)
                split_hi(nxt, 1, landed_nxt)
                act.wait_ge(S["st_mm"], g + 1)
                if not first:
                    group_mean(g - 1)
                nc.scalar.copy(state[:], aux[:, 1, 0:T]).then_inc(S["state_ok"], 1)
                split_hi(nxt, 2, landed_nxt)
                split_hi(nxt, 3, landed_nxt)
                if not last:
                    evac(zg[:, bass.ds(g * NT + NT, NT), :], g + (GROUP["zg"] + 1), 1 - par)
                gate_silu(g)
                gated_square(g)

            ssd_act(0, 0, first=True)
            with act.Fori(0, 3) as i:
                ssd_act(i * 2 + 1, 1)
                ssd_act(i * 2 + 2, 0)
            ssd_act(7, 1, last=True)
            act.wait_ge(S["narrow_ok"], 1)
            for dst, src in ((rope_sb, rope_d), (level_sb, levels_d), (neg_sb, neg_d), (wgu, wgu_d), (wglr, wglr_d)):
                act.dma_start(dst[:], src).then_inc(S["late_in"], 16)
            group_mean(7)
            act.wait_ge(S["gs_ok"], SSD_GROUPS + 1)
            nc.scalar.activation(g_stat[:, 1], g_stat[:, 0], ACT.Sqrt, bias=eps[:]).then_inc(S["grt_ok"], 1)
            nc.scalar.activation(zg[:, 16:24], zg[:, 16:24], ACT.Sigmoid).then_inc(S["sig_ok"], 1)
            split_hi(GROUP["ssm"], 0)
            split_hi(GROUP["ssm"], 1)
            nc.scalar.activation(zg[:, 24:32], zg[:, 24:32], ACT.Sigmoid).then_inc(S["sig_ok"], 1)
            for q in range(4):
                act.wait_ge(S["yb_f"], q + 1)
                nc.scalar.copy(yb_hi[:, 4 * q:4 * q + 4], xbc[:, 4 * q:4 * q + 4]).then_inc(S["yb_h"], 1)
                if q < 2:
                    split_hi(GROUP["ssm"], q + 2)
            for j in range(2):
                split_all(GROUP["ssm"] + 2 * j + 1)
                split_all(GROUP["ssm"] + 2 * j + 2)
                act.wait_ge(S["mix_f"], j + 1)
                nc.scalar.copy(act_hi[:, 4 * j:4 * j + 4], zg[:, 16 + 4 * j:20 + 4 * j]).then_inc(S["mix_h"], 1)
            split_all(GROUP["out"] + 1)
            squares(0, RES_OUT)
            for s in range(SLOTS - 1):
                split_hi(GROUP["ff1"], s)
            squares(1, RES_OUT)
            root(1)
            norm_hi(1, lambda k: modc[:, 24 + k:25 + k], ahead(GROUP["ff1"]))
            def ff1_step(c, par):
                split_all(c + (GROUP["ff1"] + 1), c + (landed_group(GROUP["ff1"]) + 1))
                evac(relu_sb[:, par].rearrange("p (n t) -> p n t", n=NT), c + GROUP["ff1"], par, ACT.Relu)
                act.wait_ge(S["sq_ok"], c + 1)
                settle(act)
                nc.scalar.copy(ff_hi[:, bass.ds(c * NT, NT), :], sq_sb[:, par].rearrange("p (n t) -> p n t", n=NT)
                               ).then_inc(S["ffhi_ok"], 1)

            with act.Fori(0, 4) as i:
                ff1_step(i * 2, 0)
                ff1_step(i * 2 + 1, 1)
            final_w = lambda k: col("final_norm_w", k)
            for g in range(4):
                split_all(GROUP["ff2"] + g + 1)
            squares(0, RES_FF2, final_w)
            for g in range(4, 7):
                split_all(GROUP["ff2"] + g + 1)
            for s in range(SLOTS - 1):
                split_hi(GROUP["in2"], s)
            squares(1, RES_FF2, final_w)
            root(2)
            act.wait_ge(S["ratio_ok"], 1)
            root(3, stat[:, 3])
            norm_hi(2, lambda k: zero8[:, k:k + 1], ahead(GROUP["in2"]))
            act.wait_ge(S["late_in"], 80)
            nc.scalar.copy(wglr_hi[:], wglr[:]).then_inc(S["narrow_hi_ok"], 1)

            i2 = GROUP["in2"]

            def level_exp(e):
                m = (LEVELS + [P])[e]
                view = gd[:, e % 2].rearrange("p (n m) -> p n m", m=2 * m)
                act.wait_ge(S["lev_d"], e + 1)
                nc.scalar.activation(view[:, :, m:2 * m], view[:, :, m:2 * m], ACT.Exp)
                nc.scalar.activation(view[:, :, 0:m], view[:, :, 0:m], ACT.Exp, scale=-1.0).then_inc(S["lev_e"], 1)

            split_all(i2 + 1)
            act.wait_ge(used, i2 * SLOTS + SLOTS)
            nc.scalar.activation(gqk[:, 0:2], proj_ps[:, 0, 0:2 * T].rearrange("p (n t) -> p n t", n=2), ACT.Copy, scale=0.125)
            nc.scalar.copy(gqk[:, 2:4], proj_ps[:, 0, 2 * T:].rearrange("p (n t) -> p n t", n=2)).then_inc(evac_act, 1)
            act.wait_ge(S["glr_mm"], 1)
            nc.scalar.copy(glr_sb[:], aux[0:16, 0, 0:T]).then_inc(S["glr_ok"], 1)
            split_hi(i2 + 2, 0)
            act.wait_ge(S["gx_abs"], 1)
            nc.scalar.activation(gt[:, 1], gt[:, 0], ACT.Exp, scale=-1.0).then_inc(S["gx_exp"], 1)
            split_hi(i2 + 2, 1)
            act.wait_ge(S["gx_u"], 1)
            nc.scalar.activation(glog[:], gt[:, 2], ACT.Ln).then_inc(S["gx_ln"], 1)
            act.wait_ge(S["gx_ln"], 1)
            nc.scalar.activation(og2[:, 0:2], glog[:], ACT.Exp, scale=-1.0).then_inc(S["gx_inv"], 1)
            split_hi(i2 + 2, 2)
            split_hi(i2 + 2, 3)
            evac(q_sb[:], i2 + 1, 1)
            for s in range(SLOTS):
                level_exp(s)
                split_hi(i2 + 3, s)
            evac(k_sb[:], i2 + 2, 0)
            for s in range(SLOTS):
                level_exp(4 + s)
                split_hi(i2 + 4, s)
            evac(gr_sb[:], i2 + 3, 1, ACT.Silu)
            split_all(i2 + 5)
            evac(gv_sb[:], i2 + 4, 0)

            def moba_exp(w):
                act.wait_ge(S["max_ok"], w + 1)
                n = 4 if w < 2 else 2
                for h in range(n):
                    part = prob[:, w, h * (512 // n):(h + 1) * (512 // n)]
                    last = nc.scalar.activation(part, part, ACT.Exp, bias=small[:, 32 + 4 * w + h:33 + 4 * w + h], scale=0.125,
                                                accum_out=small[:, 64 + 4 * w + h:65 + 4 * w + h])
                last.then_inc(S["exp_ok"], 1)

            def moba_keys(w):
                act.wait_ge(S["pt_mm"], w + 1)
                nc.scalar.copy(prob_t[:, w], aux[:, 1]).then_inc(S["pt_ok"], 1)

            def moba_high(half):
                act.wait_ge(S["ym_mm"], half + 1)
                nc.scalar.copy(flat(mix_hi[:, 4 + 2 * half:6 + 2 * half]), aux[:, 2 + half]).then_inc(S["ym_h"], 1)

            for w in range(2 * SLOTS):
                split_hi(i2 + 6 + w // SLOTS, w % SLOTS)
                if w == 3:
                    evac(mv_sb[:], i2 + 5, 1)
                if w == 0:
                    act.wait_ge(S["og_mm"], 1)
                    nc.scalar.copy(og[:], proj_ps[:, 0].rearrange("p (n t) -> p n t", n=GLA_HEADS))
                    nc.scalar.activation(og2[:], proj_ps[:, 0].rearrange("p (n t) -> p n t", n=GLA_HEADS), ACT.Square
                                         ).then_inc(S["og_sq"], 1)
                if w == 1:
                    act.wait_ge(S["og_ms"], 1)
                    nc.scalar.activation(og_stat[:, 0], proj_ps[:, 0, 0:GLA_HEADS * TT], ACT.Sqrt, bias=eps[:]).then_inc(S["og_rt"], 1)
                if w < UNITS:
                    moba_exp(w)
                if 1 <= w <= UNITS:
                    moba_keys(w - 1)
                if w == 2:
                    act.wait_ge(S["gla_f"], 1)
                    nc.scalar.copy(mix_hi[:, 0:4], og[:]).then_inc(S["gla_h"], 1)
                if w == 6:
                    moba_high(0)
            moba_high(1)
            squares(0, RES_OUT2)
            for s in range(SLOTS - 1):
                split_hi(GROUP["up"], s)
            squares(1, RES_OUT2)
            root(3)
            norm_hi(3, lambda k: zero8[:, k:k + 1], ahead(GROUP["up"]))
            act.wait_ge(S["fpadded"], 1)

            def gate_silu(c, par):
                act.wait_ge(S["fc_done"], c * NT + (NT + NT))
                nc.scalar.activation(fconv_acc[:, par, 0:2], fconv_acc[:, par, 0:2], ACT.Silu).then_inc(S["fc_silu"], 1)

            def glu_high(c, par, fixed=False):
                act.wait_ge(S["glu_f"], c + 2)
                settle(act)
                dst = glu_hi[:, 2 * c:2 * c + 2] if fixed else glu_hi[:, bass.ds(c * 2, 2), :]
                nc.scalar.copy(dst, glu_sb[:, par]).then_inc(S["glu_h"], 1)

            def up_step(c, par, silu=True, glu=True, fixed=False):
                for s in range(SLOTS):
                    split_hi(c + (GROUP["up"] + 1), s, c + (landed_group(GROUP["up"]) + 1))
                    if glu and s == 1:
                        glu_high(c - 2, par, fixed)
                need(act, S["fc_done"], c * NT)
                evac(fconv_in[:, par, :, 2:2 + T], c + GROUP["up"], par)
                if silu:
                    gate_silu(c - 1, 1 - par)

            up_step(0, 0, silu=False, glu=False)
            up_step(1, 1, glu=False)
            with act.Fori(0, 4) as i:
                up_step(i * 2 + 2, 0)
                up_step(i * 2 + 3, 1)
            up_step(10, 0, fixed=True)
            for s in range(SLOTS):
                split_hi(GROUP["down"] + 1, s)
                if s == 1:
                    glu_high(9, 1, True)
            gate_silu(10, 0)
            glu_high(10, 0, True)
            for j in range(2):
                for g in range(1 - j, 3 - j):
                    split_all(GROUP["down"] + 3 * j + g + 1)
                squares(j, RES_DOWN)
            root(4)

        @block.vector
        def _(dve):
            step = Steps(dve, S["dve_step"])
            tt, ts, stt = nc.vector.tensor_tensor, nc.vector.tensor_scalar, nc.vector.scalar_tensor_tensor

            def split_lo(g, s):
                dve.wait_ge(hi_done, g * SLOTS + (s + 1))
                tt(out=w_lo[:, s, :], in0=raw[:, s, :], in1=w_hi[:, s, :].bitcast(F32), op=ALU.subtract).then_inc(taken, 1)

            def split_all(g):
                for s in range(SLOTS):
                    split_lo(g, s)

            def mod_panel(src, par, s, done, count):
                acc = mod_acc[:, par]
                for k in range(2):
                    half, c_k = src[:, 512 * k:512 * k + 512], silu_c[:, 2 * s + k:2 * s + k + 1]
                    if s == 0 and k == 0:
                        step(ts(out=acc, in0=half, scalar1=c_k, scalar2=0.0, op0=ALU.mult, op1=ALU.add))
                    elif k == 0:
                        step(stt(out=acc, in0=half, scalar=c_k, in1=acc, op0=ALU.mult, op1=ALU.add))
                    else:
                        stt(out=acc, in0=half, scalar=c_k, in1=acc, op0=ALU.mult, op1=ALU.add).then_inc(done, 1)
                        dve.wait_ge(done, count)

            def mod_raw_panel(rg, par, s):
                dve.wait_ge(landed[s], rg * 16 + 16)
                mod_panel(raw[:, s], par, s, taken, rg * SLOTS + (s + 1))

            def mod_evac(m):
                dve.wait_ge(S["mod_mm"], m + 1)
                tt(out=modc[:, bass.ds(m * 4, 4)], in0=aux[:, 3, 0:4], in1=cols[:, bass.ds(m * 4 + COL["b_mod"], 4)],
                   op=ALU.add).then_inc(S["mod_done"], 1)

            def inverse(n, dst):
                dve.wait_ge(S["rt_done"], n + 1)
                step(nc.vector.reciprocal(dst, stat[:, 0]))

            def broadcast(n, src, wait=True):
                tt(out=diag[:], in0=spread(ident, 1, TT), in1=spread(src, 2, P), op=ALU.mult).then_inc(S["rs_done"], 1)
                if wait:
                    dve.wait_ge(S["rs_mm"], n + 1)

            rs_ps = aux[:, 3, 0:T]

            def norm_apply(a, scale, shift, beside):
                for pair in range(0, KT, 2):
                    for k in (pair, pair + 1):
                        stt(out=tmp_a[:, k], in0=xres[:, k], scalar=scale(k), in1=rs_ps, op0=ALU.mult,
                            op1=ALU.mult).then_inc(S["nrm_t"], 1)
                    for k in (pair, pair + 1):
                        dve.wait_ge(S["nrm_hi"], KT * a + k + 1)
                        dve.wait_ge(S["nrm_t"], KT * a + k + 1)
                        stt(out=act_lo[:, k], in0=tmp_a[:, k], scalar=shift(k), in1=act_hi[:, k].bitcast(F32),
                            op0=ALU.add, op1=ALU.subtract).then_inc(S["nrm_lo"], 1)
                        beside(k)

            def ahead(g):
                return lambda k: split_lo(g, SLOTS - 1) if k == KT - 1 else None

            def softplus_lost(e, u, small_part):
                step(stt(out=small_part, in0=u, scalar=1.0, in1=e, op0=ALU.subtract, op1=ALU.subtract))

            def softplus_add(inverse_u, ln, small_part):
                step(stt(out=small_part, in0=small_part, scalar=-1.0, in1=inverse_u, op0=ALU.mult, op1=ALU.mult))
                step(tt(out=ln, in0=ln, in1=small_part, op=ALU.add))

            def add_residual(j, par, gate=None):
                for nt in range(NT):
                    k = 4 * j + nt
                    src = proj_ps[:, par, nt * T:nt * T + T]
                    if gate is None:
                        last = tt(out=xres[:, k], in0=xres[:, k], in1=src, op=ALU.add)
                    else:
                        last = stt(out=xres[:, k], in0=src, scalar=modc[:, gate + k:gate + k + 1], in1=xres[:, k],
                                   op0=ALU.mult, op1=ALU.add)
                    last.then_inc(S["res_ok"], 1)

            nc.vector.memset(ones[:], 1.0).then_inc(S["ready"], 1)
            nc.vector.memset(avg_d[:], 1.0 / D).then_inc(S["ready"], 1)
            nc.vector.memset(avg_g[:], 1.0 / 256).then_inc(S["ready"], 1)
            nc.vector.memset(avg_v[:], 1.0 / P).then_inc(S["ready"], 1)
            nc.vector.memset(eps[:], EPS).then_inc(S["ready"], 1)
            nc.vector.memset(zero8[:], 0.0).then_inc(S["ready"], 1)
            for n, (name, credit) in enumerate((("conv_done", NT), ("xbc_done", 1), ("seg_mm", 2), ("cum_mm", 1), ("ecum_ok", 1),
                                                ("state_ok", 1), ("y_ok", 2), ("gs_mm", 1), ("gs_ok", 1), ("fc_done", NT), ("glu_f", 1))):
                nc.vector.memset(junk[:, n:n + 1], 0.0).then_inc(S[name], credit)
            dve.wait_ge(S["cols_in"], 16)
            dve.wait_ge(S["c_ready"], 1)
            for s in range(SLOTS):
                mod_raw_panel(0, 0, s)
            for s in range(SLOTS):
                dve.wait_ge(spare_in[SLOTS + s], 16)
                mod_panel(spare[1][:, s], 1, s, S["spare_used"], s + 1)
            inverse(0, stat[:, 1])
            dve.wait_ge(S["early_in"], 32)
            broadcast(0, stat[:, 1], wait=False)
            dve.wait_ge(S["mod_mm"], 1)
            for s in range(SLOTS):
                dve.wait_ge(spare_in[2 * SLOTS + s], 16)
                mod_panel(spare[2][:, s], 0, s, S["spare_used"], SLOTS + s + 1)
            dve.wait_ge(S["mod_mm"], MOD_FIRST)
            dve.wait_ge(S["rs_mm"], 1)
            tt(out=modc[:, 0:16], in0=aux[:, 1, 0:16], in1=col("b_mod", 0, 16), op=ALU.add).then_inc(S["mod_done"], MOD_FIRST)
            dve.wait_ge(S["mod_done"], MOD_FIRST)
            step(ts(out=modc[:, 8:16], in0=modc[:, 8:16], scalar1=1.0, scalar2=None, op0=ALU.add))
            norm_apply(0, lambda k: modc[:, 8 + k:9 + k], lambda k: modc[:, k:k + 1],
                       lambda k: split_lo(0, k // 2) if k % 2 else None)
            dve.wait_ge(S["narrow_hi_ok"], 1)
            tt(out=wdt_lo[:], in0=wdt[:], in1=wdt_hi[:].bitcast(F32), op=ALU.subtract).then_inc(S["narrow_ok"], 1)
            for g in range(1, GROUP["u"] + 1):
                split_all(g)
            u1 = GROUP["u"] + 1
            dve.wait_ge(S["dt_mm"], 1)
            step(tt(out=dts[:, 3], in0=aux[:, 0, 0:TT * HEADS].rearrange("p (t h) -> p t h", t=TT),
                    in1=spread(col("dt_bias", 0, HEADS), 1, TT), op=ALU.add))
            stt(out=dts[:, 4], in0=dts[:, 3], scalar=-1.0, in1=dts[:, 3], op0=ALU.mult, op1=ALU.max).then_inc(S["dt_abs"], 1)
            split_lo(u1, 0)
            dve.wait_ge(S["dt_exp"], 1)
            ts(out=dts[:, 6], in0=dts[:, 5], scalar1=1.0, scalar2=None, op0=ALU.add).then_inc(S["dt_u"], 1)
            split_lo(u1, 1)
            dve.wait_ge(S["dt_ln"], 1)
            softplus_lost(dts[:, 5], dts[:, 6], dts[:, 4])
            step(nc.vector.reciprocal(dts[:, 6], dts[:, 6]))
            softplus_add(dts[:, 6], dts[:, 7], dts[:, 4])
            step(stt(out=dts[:, 0], in0=dts[:, 3], scalar=0.0, in1=dts[:, 7], op0=ALU.max, op1=ALU.add))
            dve.wait_ge(S["exp_a_ok"], 1)
            stt(out=dts[:, 1], in0=dts[:, 0], scalar=-1.0, in1=spread(exp_a[:], 1, TT), op0=ALU.mult,
                op1=ALU.mult).then_inc(S["dt_ok"], 1)
            split_lo(u1, 2)
            dve.wait_ge(S["v_rt"], 1)
            step(nc.vector.reciprocal(small[:, 4:6], small[:, 2:4]))
            for t in range(TT):
                ts(out=v_sb[:, t], in0=v_sb[:, t], scalar1=small[:, 4 + t:5 + t], scalar2=None,
                   op0=ALU.mult).then_inc(S["v_ready"], 1)
            split_lo(u1, 3)
            dve.wait_ge(S["a_hi_ok"], 1)
            tt(out=a_lo[:], in0=dts[:, 1], in1=a_hi[:].bitcast(F32), op=ALU.subtract).then_inc(S["a_parts_ok"], 1)
            nc.vector.memset(conv_in[:, :, :, 0:3], 0.0).then_inc(S["padded"], 1)
            split_all(GROUP["xbc"])
            dve.wait_ge(S["sgu_in"], 32)
            dve.wait_ge(evac_act, EVAC_XBC)
            for g in range(GROUPS_SGU):
                if g % 2 == 0:
                    dve.wait_ge(S["sgu_mm"], g // 2 + 1)
                last = stt(out=sgu_t[:, g].rearrange("p (c i) -> p c i", c=TT),
                           in0=aux[:, g // 2, (g % 2) * T:(g % 2) * T + T].rearrange("p (c i) -> p c i", c=TT),
                           scalar=col("gm_norm_w", g), in1=spread(bs_sb[:, g], 1, TT), op0=ALU.mult, op1=ALU.add)
            last.then_inc(S["sgu_y"], 1)
            dve.wait_ge(S["sgu_y"], 1)
            tt(out=u_sb[:], in0=u_sb[:], in1=sgu_t[:], op=ALU.mult).then_inc(S["sgu_y"], 1)
            def last_taps(c, par, nt):
                dve.wait_ge(S["conv_pool"], c * NT + (nt + 1))
                acc, src = conv_acc[:, par, nt], conv_in[:, par, nt]
                w = c * (NT * 4) + nt * 4
                step(stt(out=acc, in0=src[:, 1:1 + T], scalar=col_at("conv_w", w + 1), in1=acc, op0=ALU.mult, op1=ALU.add))
                stt(out=acc, in0=src[:, 0:T], scalar=col_at("conv_w", w), in1=acc, op0=ALU.mult,
                    op1=ALU.add).then_inc(S["conv_done"], 1)

            def all_taps(c, par, nt):
                dve.wait_ge(evac_act, EVAC_XBC + c + 1)
                acc, src = conv_acc[:, par, nt], conv_in[:, par, nt]
                w = [col("conv_w", 4 * (NT * c + nt) + j) for j in range(4)]
                step(ts(out=acc, in0=src[:, 3:3 + T], scalar1=w[3], scalar2=col("conv_b", NT * c + nt), op0=ALU.mult, op1=ALU.add))
                step(stt(out=acc, in0=src[:, 2:2 + T], scalar=w[2], in1=acc, op0=ALU.mult, op1=ALU.add))
                step(stt(out=acc, in0=src[:, 1:1 + T], scalar=w[1], in1=acc, op0=ALU.mult, op1=ALU.add))
                stt(out=acc, in0=src[:, 0:T], scalar=w[0], in1=acc, op0=ALU.mult, op1=ALU.add).then_inc(S["conv_done"], 1)

            def conv_step(c, par, first=False, last=False):
                for s in range(SLOTS):
                    if not last:
                        split_lo(c + (GROUP["xbc"] + 1), s)
                    if not first:
                        last_taps(c - 1, 1 - par, s)

            conv_step(0, 0, first=True)
            dve.wait_ge(S["sgu_hi"], 1)
            dve.wait_ge(S["sgu_y"], 2)
            tt(out=ya_lo[:], in0=u_sb[:], in1=ya_hi[:].bitcast(F32), op=ALU.subtract).then_inc(S["sgu_done"], 1)
            conv_step(1, 1)
            with step.loop(3, 2 * NT) as i:
                conv_step(i * 2 + 2, 0)
                conv_step(i * 2 + 3, 1)
            zg0 = landed_group(GROUP["zg"])
            all_taps(7, 1, 2)
            all_taps(7, 1, 3)
            last_taps(7, 1, 0)
            last_taps(7, 1, 1)
            split_all(GROUP["zg"] + 1)

            def ssd_dve(g, par):
                mod_panel_of = lambda s: mod_raw_panel(g * 2 + (zg0 + 2), par, s)
                dve.wait_ge(S["mod_mm"], g + (MOD_FIRST - 1))
                mod_panel_of(0)
                dve.wait_ge(S["t_mm"], g + 1)
                tt(out=xdt[:].rearrange("p c (h d) -> p c h d", h=HPG),
                   in0=aux[:, 0].rearrange("p (c h d) -> p c h d", c=2, h=HPG),
                   in1=spread(dts[:, 0, :, bass.ds(g * HPG, HPG)], 3, 64), op=ALU.mult).then_inc(S["xdt_ok"], 1)
                dve.wait_ge(S["btok_ok"], g + 1)
                tt(out=cbm[:], in0=aux[:, 1, 0:2 * P].rearrange("p (c i) -> p c i", c=2), in1=spread(upto, 1, 2),
                   op=ALU.mult).then_inc(S["cbm_ok"], 1)
                mod_panel_of(1)
                for c in range(2):
                    mod_panel_of(2 + c)
                    dve.wait_ge(S["decay_ok"], g * 2 + (c + 1))
                    dve.wait_ge(S["cbm_ok"], g + 1)
                    tt(out=decay[:, c], in0=decay[:, c], in1=spread(cbm[:, c], 1, HPG), op=ALU.mult).then_inc(S["m_ok"], 1)
                for s in range(SLOTS):
                    split_lo(g + (GROUP["zg"] + 2), s)
                dve.wait_ge(S["y_mm"], g + 1)
                for pair in range(2):
                    last_y = stt(out=xbc[:, bass.ds(g * 2 + pair, 1), :].rearrange("p a t -> p (a t)"), in0=stg[:, par, pair],
                                 scalar=col_at("d_skip", g * 2 + pair), in1=aux[:, 2, pair * T:pair * T + T],
                                 op0=ALU.mult, op1=ALU.add)
                last_y.then_inc(S["y_ok"], 1)
                mod_evac(g + MOD_FIRST)
                dve.wait_ge(S["silu_z"], g + 1)
                dve.wait_ge(S["y_ok"], g + 3)
                y = xbc[:, bass.ds(g * 2, 2), :]
                tt(out=y, in0=y, in1=zg[:, bass.ds(g * 2, 2), :], op=ALU.mult).then_inc(S["g_ok"], 1)

            ssd_dve(0, 0)
            with step.loop(3, 2 * SLOTS) as i:
                ssd_dve(i * 2 + 1, 1)
                ssd_dve(i * 2 + 2, 0)
            ssd_dve(7, 1)
            dve.wait_ge(S["mod_done"], 12)
            step(ts(out=modc[:, 32:40], in0=modc[:, 32:40], scalar1=1.0, scalar2=None, op0=ALU.add))

            def branch_gm(j):
                dve.wait_ge(S["sig_ok"], 1)
                dve.wait_ge(used, (GROUP["gm"] + j + 1) * SLOTS)
                tt(out=zg[:, 16 + 4 * j:20 + 4 * j], in0=zg[:, 16 + 4 * j:20 + 4 * j],
                   in1=proj_ps[:, j].rearrange("p (n t) -> p n t", n=NT), op=ALU.mult).then_inc(evac_dve, 1)

            dve.wait_ge(S["grt_ok"], 1)
            step(nc.vector.reciprocal(g_stat[:, 1], g_stat[:, 1]))
            for q in range(4):
                tt(out=g_diag[:, q], in0=spread(ident, 1, 4), in1=spread(g_stat[:, 1, 2 * q:2 * q + 2].rearrange("p g t -> p (g t)"), 2, P),
                   op=ALU.mult).then_inc(S["gdiag_ok"], 1)
            branch_gm(0)
            split_lo(GROUP["ssm"], 0)
            for q in range(4):
                dve.wait_ge(S["grow_mm"], q + 1)
                for k in range(4 * q, 4 * q + 4):
                    last = stt(out=xbc[:, k], in0=xbc[:, k], scalar=col("ssm_norm_w", k),
                               in1=aux[:, q, (k // 2 % 2) * T:(k // 2 % 2) * T + T], op0=ALU.mult, op1=ALU.mult)
                last.then_inc(S["yb_f"], 1)
                if q == 0:
                    dve.wait_ge(S["yb_h"], 1)
                    tt(out=yb_lo[:, 0:4], in0=xbc[:, 0:4], in1=yb_hi[:, 0:4].bitcast(F32), op=ALU.subtract).then_inc(S["yb0_ok"], 1)
                if q < 3:
                    split_lo(GROUP["ssm"], q + 1)
            branch_gm(1)
            for j in range(2):
                split_all(GROUP["ssm"] + 2 * j + 1)
                for s in range(SLOTS - 1):
                    split_lo(GROUP["ssm"] + 2 * j + 2, s)
                ga, gb = zg[:, 16 + 4 * j:20 + 4 * j], zg[:, 24 + 4 * j:28 + 4 * j]
                dve.wait_ge(S["sig_ok"], 2)
                dve.wait_ge(used, (GROUP["ssm"] + 2 * j + 2) * SLOTS)
                tt(out=gb, in0=gb, in1=proj_ps[:, j].rearrange("p (n t) -> p n t", n=NT), op=ALU.mult).then_inc(evac_dve, 1)
                dve.wait_ge(evac_dve, 3 + j)
                tt(out=ga, in0=ga, in1=gb, op=ALU.add).then_inc(S["mix_f"], 1)
                split_lo(GROUP["ssm"] + 2 * j + 2, SLOTS - 1)
                dve.wait_ge(S["mix_h"], j + 1)
                dve.wait_ge(S["mix_f"], j + 1)
                tt(out=act_lo[:, 4 * j:4 * j + 4], in0=ga, in1=act_hi[:, 4 * j:4 * j + 4].bitcast(F32),
                   op=ALU.subtract).then_inc(S["mix_ok"], 1)
            for j in range(2):
                for s in range(SLOTS - j):
                    split_lo(GROUP["out"] + j + 1, s)
                dve.wait_ge(used, (GROUP["out"] + j + 1) * SLOTS)
                add_residual(j, j, 16)
            dve.wait_ge(S["res_ok"], RES_OUT + KT)
            inverse(1, stat[:, 1])
            broadcast(1, stat[:, 1])
            norm_apply(1, lambda k: modc[:, 32 + k:33 + k], lambda k: modc[:, 24 + k:25 + k], ahead(GROUP["ff1"]))

            def ff1_step(c, par):
                split_all(c + (GROUP["ff1"] + 1))
                dve.wait_ge(evac_act, c + (EVAC_FF1 + 1))
                tt(out=sq_sb[:, par], in0=relu_sb[:, par], in1=relu_sb[:, par], op=ALU.mult).then_inc(S["sq_ok"], 1)
                dve.wait_ge(S["ffhi_ok"], c + 1)
                tt(out=ff_lo[:, bass.ds(c * NT, NT), :], in0=sq_sb[:, par].rearrange("p (n t) -> p n t", n=NT),
                   in1=ff_hi[:, bass.ds(c * NT, NT), :].bitcast(F32), op=ALU.subtract).then_inc(S["ff_ok"], 1)

            with dve.Fori(0, 4) as i:
                ff1_step(i * 2, 0)
                ff1_step(i * 2 + 1, 1)
            step(tt(out=small[:, 88:96], in0=col("final_norm_w", 0, KT), in1=col("attn_g", 0, KT), op=ALU.mult))
            for j in range(2):
                for g in range(4):
                    for s in range(SLOTS - (j == 1 and g == 3)):
                        split_lo(GROUP["ff2"] + 4 * j + g + 1, s)
                dve.wait_ge(used, (GROUP["ff2"] + 4 * j + 4) * SLOTS)
                add_residual(j, j, 40)
            dve.wait_ge(S["res_ok"], RES_FF2 + KT)
            inverse(2, stat[:, 2])
            step(tt(out=stat[:, 3], in0=stat[:, 2], in1=aux[:, 2, TT:2 * TT], op=ALU.mult))
            tt(out=stat[:, 3], in0=stat[:, 3], in1=stat[:, 2], op=ALU.mult).then_inc(S["ratio_ok"], 1)
            inverse(3, stat[:, 1])
            step(tt(out=stat[:, 1], in0=stat[:, 1], in1=stat[:, 2], op=ALU.mult))
            broadcast(2, stat[:, 1])
            norm_apply(2, lambda k: small[:, 88 + k:89 + k], lambda k: zero8[:, k:k + 1], ahead(GROUP["in2"]))
            dve.wait_ge(S["narrow_hi_ok"], 2)
            tt(out=wglr_lo[:], in0=wglr[:], in1=wglr_hi[:].bitcast(F32), op=ALU.subtract).then_inc(S["narrow_ok"], 1)
            step(nc.vector.memset(scores_t[:], 0.0))
            i2 = GROUP["in2"]
            split_all(i2 + 1)
            dve.wait_ge(S["nrm_t"], 3 * KT)
            broadcast(3, stat[:, 2], wait=False)

            def first_output(ks):
                for k in ks:
                    last = stt(out=xres[:, k], in0=xres[:, k], scalar=col("final_norm_w", k), in1=rs_ps, op0=ALU.mult, op1=ALU.mult)
                step(last)

            dve.wait_ge(S["gate_mm"], 1)
            for t in range(2):
                last = ts(out=og[:, t], in0=aux[:, 1, t * T:t * T + T], scalar1=col("b_gate", t), scalar2=None, op0=ALU.add)
            step(last)
            stt(out=gt[:, 0], in0=og[:, 0:2], scalar=-1.0, in1=og[:, 0:2], op0=ALU.mult, op1=ALU.max).then_inc(S["gx_abs"], 1)
            split_lo(i2 + 2, 0)
            dve.wait_ge(S["rs_mm"], 4)
            first_output(range(4))
            dve.wait_ge(S["gx_exp"], 1)
            ts(out=gt[:, 2], in0=gt[:, 1], scalar1=1.0, scalar2=None, op0=ALU.add).then_inc(S["gx_u"], 1)
            split_lo(i2 + 2, 1)
            first_output(range(4, KT))
            softplus_lost(gt[:, 1], gt[:, 2], gt[:, 0])
            dve.wait_ge(S["gx_inv"], 1)
            softplus_add(og2[:, 0:2], glog[:], gt[:, 0])
            step(stt(out=gt[:, 0], in0=og[:, 0:2], scalar=0.0, in1=glog[:], op0=ALU.min, op1=ALU.subtract))
            split_lo(i2 + 2, 2)
            step(ts(out=gt[:, 0], in0=gt[:, 0], scalar1=1.0 / 16, scalar2=None, op0=ALU.mult))
            step(nc.vector.memset(gt[:, 1], 1.0))
            for t in range(2):
                last = nc.vector.tensor_tensor_scan(out=glog[:, t], data0=gt[:, 1, t], data1=gt[:, 0, t], initial=0.0,
                                                    op0=ALU.mult, op1=ALU.add)
            step(last)

            def level_diff(e):
                m = (LEVELS + [P])[e]
                view = flat(glog[:]).rearrange("p (n m) -> p n m", m=2 * m)
                if e >= 2:
                    dve.wait_ge(S["lev_x"], e - 1)
                tt(out=gd[:, e % 2].rearrange("p (n m) -> p n m", m=2 * m), in0=view,
                   in1=view[:, :, m - 1:m].broadcast_to(list(view.shape)), op=ALU.subtract).then_inc(S["lev_d"], 1)

            def level_pick(l):
                dve.wait_ge(S["lev_mm"], l + 1)
                bank = 2 * (l % 2)
                if l == 8:
                    nc.vector.tensor_copy(scores_t[:, 2].rearrange("p (a b) i -> p a (b i)", a=2), aux[:, bank:bank + 2, 0:2 * P]
                                          ).then_inc(S["lev_ok"], 1)
                    return
                if l > 0:
                    dve.wait_ge(S["lev_ok"], l)
                for t in range(TT):
                    last = nc.vector.copy_predicated(
                        scores_t[:, t].rearrange("p (a b) i -> p a b i", a=2),
                        spread(spread(level_sb[:, l].bitcast(U32), 1, 2), 1, 2),
                        aux[:, bank:bank + 2, 2 * t * P:2 * t * P + 2 * P].rearrange("p a (b i) -> p a b i", b=2))
                last.then_inc(S["lev_ok"], 1)

            level_diff(0)
            split_lo(i2 + 2, 3)
            for c in range(2):
                for s in range(SLOTS):
                    l = 4 * c + s
                    if l + 1 < 8:
                        level_diff(l + 1)
                    split_lo(i2 + 3 + c, s)
                    level_pick(l)

            def rope(w, x):
                dve.wait_ge(S["turn_mm"], w + 1)
                bank = 2 - 2 * w
                step(tt(out=rope_s[:].rearrange("p (b n) t -> p b n t", b=2),
                        in0=aux[:, bank:bank + 2].rearrange("p b (n t) -> p b n t", n=2),
                        in1=spread(spread(rope_sb[:, 1], 1, 2), 1, 2), op=ALU.mult))
                dve.wait_ge(S["cos_ok"], w + 1)
                tt(out=x[:], in0=rope_c[:, w], in1=rope_s[:], op=ALU.add).then_inc(S["rope_ok"], 1)
                dve.wait_ge(S["rope_ok"], w + 1)

            split_lo(i2 + 5, 0)
            level_pick(8)
            rope(0, q_sb)
            split_lo(i2 + 5, 1)
            rope(1, k_sb)
            split_lo(i2 + 5, 2)
            split_lo(i2 + 5, 3)

            def moba_max(w):
                n = 4 if w < 2 else 2
                dve.wait_ge(S["sc_mm"], w + 1)
                mask = neg_sb[:, 1] if w < 2 else flat(neg_sb[:, 0:2])
                part = prob[:, w].rearrange("p (h k) -> p h k", h=n)
                step(tt(out=part, in0=aux[:, 0].rearrange("p (h k) -> p h k", h=n), in1=spread(mask, 1, n), op=ALU.add))
                step(nc.vector.reduce_max(small[:, 4 * w:4 * w + n], part, AX_X))
                ts(out=small[:, 32 + 4 * w:32 + 4 * w + n], in0=small[:, 4 * w:4 * w + n], scalar1=-0.125, scalar2=None,
                   op0=ALU.mult).then_inc(S["max_ok"], 1)

            def moba_normalise(w):
                n = 4 if w < 2 else 2
                at_sum = 64 + 4 * w
                dve.wait_ge(S["exp_ok"], w + 1)
                step(nc.vector.reciprocal(small[:, at_sum:at_sum + n], small[:, at_sum:at_sum + n]))
                part = prob[:, w].rearrange("p (h k) -> p h k", h=n)
                tt(out=part, in0=part, in1=spread(small[:, at_sum:at_sum + n], 2, 512 // n), op=ALU.mult).then_inc(S["p_ok"], 1)

            def moba_low(half):
                dve.wait_ge(S["ym_h"], half + 1)
                tiles = slice(4 + 2 * half, 6 + 2 * half)
                tt(out=flat(mix_lo[:, tiles]), in0=aux[:, 2 + half], in1=flat(mix_hi[:, tiles]).bitcast(F32), op=ALU.subtract
                   ).then_inc(S["ym_ok"], 1)

            for w in range(2 * SLOTS):
                if w == 2:
                    dve.wait_ge(S["og_row"], 1)
                    step(tt(out=og[:], in0=og[:], in1=proj_ps[:, 0].rearrange("p (n t) -> p n t", n=GLA_HEADS), op=ALU.mult))
                    for h in range(GLA_HEADS):
                        last = stt(out=og[:, h], in0=og[:, h], scalar=col("gla_g", h), in1=gr_sb[:, h], op0=ALU.mult, op1=ALU.mult)
                    last.then_inc(S["gla_f"], 1)
                if w == 3:
                    dve.wait_ge(S["gla_f"], 1)
                    dve.wait_ge(S["gla_h"], 1)
                    tt(out=mix_lo[:, 0:4], in0=og[:], in1=mix_hi[:, 0:4].bitcast(F32), op=ALU.subtract).then_inc(S["gla_ok"], 1)
                if w < UNITS:
                    moba_max(w)
                split_lo(i2 + 6 + w // SLOTS, w % SLOTS)
                if w == 1:
                    dve.wait_ge(S["og_rt"], 1)
                    step(nc.vector.reciprocal(og_stat[:, 1], og_stat[:, 0]))
                    tt(out=og2[:].rearrange("p h (t i) -> p (h t) i", t=TT), in0=spread(ident, 1, GLA_HEADS * TT),
                       in1=spread(og_stat[:, 1], 2, P), op=ALU.mult).then_inc(S["og_diag"], 1)
                if w < UNITS:
                    moba_normalise(w)
                if w == 6:
                    moba_low(0)
            moba_low(1)
            for j in range(2):
                dve.wait_ge(used, GROUP["out2"] * SLOTS + 6 + 2 * j)
                add_residual(j, j)
                if j == 0:
                    for s in range(SLOTS - 1):
                        split_lo(GROUP["up"], s)
            dve.wait_ge(S["res_ok"], RES_OUT2 + KT)
            inverse(4, stat[:, 1])
            broadcast(4, stat[:, 1])
            norm_apply(3, lambda k: col("ffn_g", k), lambda k: zero8[:, k:k + 1], ahead(GROUP["up"]))
            nc.vector.memset(fconv_in[:, :, :, 0:2], 0.0).then_inc(S["fpadded"], 1)

            def glu_product(c, par):
                dve.wait_ge(S["fc_silu"], c + 1)
                tt(out=glu_sb[:, par], in0=fconv_acc[:, par, 0:2], in1=fconv_acc[:, par, 2:4], op=ALU.mult).then_inc(S["glu_f"], 1)

            def glu_low(c, par, fixed=False):
                dve.wait_ge(S["glu_h"], c + 1)
                part = slice(2 * c, 2 * c + 2) if fixed else bass.ds(c * 2, 2)
                tt(out=glu_lo[:, part, :], in0=glu_sb[:, par], in1=glu_hi[:, part, :].bitcast(F32),
                   op=ALU.subtract).then_inc(S["glu_ok"], 1)

            def first_tap(c, par, nt):
                dve.wait_ge(S["fc_pool"], c * NT + (nt + 1))
                acc = fconv_acc[:, par, nt]
                stt(out=acc, in0=fconv_in[:, par, nt, 0:T], scalar=col_at("fconv_w", c * (NT * 3) + nt * 3), in1=acc,
                    op0=ALU.mult, op1=ALU.add).then_inc(S["fc_done"], 1)

            def up_step(c, par, taps=True, glu=True, fixed=False):
                if glu:
                    glu_product(c - 2, par)
                for s in range(SLOTS):
                    split_lo(c + (GROUP["up"] + 1), s)
                    if taps:
                        first_tap(c - 1, 1 - par, s)
                    if glu and s == 2:
                        glu_low(c - 2, par, fixed)

            up_step(0, 0, taps=False, glu=False)
            up_step(1, 1, glu=False)
            with dve.Fori(0, 4) as i:
                up_step(i * 2 + 2, 0)
                up_step(i * 2 + 3, 1)
            up_step(10, 0, fixed=True)
            glu_product(9, 1)
            for s in range(SLOTS):
                split_lo(GROUP["down"] + 1, s)
                first_tap(10, 0, s)
                if s == 2:
                    glu_low(9, 1, True)
            glu_product(10, 0)
            glu_low(10, 0, True)
            for j in range(2):
                for g in range(1 - j, 3 - j):
                    split_all(GROUP["down"] + 3 * j + g + 1)
                dve.wait_ge(used, (GROUP["down"] + 3 * j + 3) * SLOTS)
                add_residual(j, (j + 1) % 2)
            dve.wait_ge(S["res_ok"], RES_DOWN + KT)
            inverse(5, stat[:, 1])
            broadcast(5, stat[:, 1])
            for k in range(KT):
                last = stt(out=tmp_a[:, k], in0=xres[:, k], scalar=col("final_g", k), in1=rs_ps, op0=ALU.mult, op1=ALU.mult)
                if k % 2:
                    last.then_inc(S["fin_ok"], 1)

        @block.tensor
        def _(pe):
            mm = nc.tensor.matmul

            def panel(g, s, par, x_hi, x_lo, k0=0, first=False, last=False, rg=None, ks=2, release=1):
                rg = landed_group(g) if rg is None else rg
                pe.wait_ge(taken, rg * SLOTS + (s + 1))
                for nt in range(NT):
                    dst = proj_ps[:, par, nt * T:nt * T + T]
                    for k in range(ks):
                        hi = w_hi[:, s, k * 512 + nt * P:k * 512 + nt * P + P]
                        lo = w_lo[:, s, k * 512 + nt * P:k * 512 + nt * P + P]
                        xh, xl = x_hi[:, k0 + k], x_lo[:, k0 + k]
                        mm(dst, hi, xh, start=first and k == 0 and nt % 2 == 0, stop=False, skip_group_check=True)
                        mm(dst, hi, xl, start=False, stop=False, skip_group_check=True)
                        ins = mm(dst, lo, xh, start=False, stop=last and k == ks - 1, skip_group_check=True)
                ins.then_inc(used, release)

            def chunk(g, par, rg=None, x_ready=None):
                for s in range(SLOTS):
                    if x_ready:
                        pe.wait_ge(x_ready[0], x_ready[1] + 2 * s + 2)
                    panel(g, s, par, act_hi, act_lo, 2 * s, s == 0, s == SLOTS - 1, rg)

            def token_panel(g, s, par):
                pe.wait_ge(taken, landed_group(g) * SLOTS + (s + 1))
                for t in range(TT):
                    dst = proj_ps[:, par, t * 512:t * 512 + 512]
                    for k in range(2):
                        wh, wl = w_hi[:, s, k * 512:k * 512 + 512], w_lo[:, s, k * 512:k * 512 + 512]
                        xh, xl = (a[:, 2 * s + k, t * P:t * P + P] for a in (act_hi, act_lo))
                        mm(dst, xh, wh, start=s == 0 and k == 0, stop=False)
                        mm(dst, xh, wl, start=False, stop=False)
                        ins = mm(dst, xl, wh, start=False, stop=s == SLOTS - 1 and k == 1)
                ins.then_inc(used, 1)

            def chunk_tokens(g, par, x_ready=None):
                for s in range(SLOTS):
                    if x_ready:
                        pe.wait_ge(x_ready[0], x_ready[1] + 2 * s + 2)
                    token_panel(g, s, par)

            def mean_square(n, ks, weighted=False):
                for k in ks:
                    for w, (sq, done, summed) in enumerate(((tmp_b, "sq_done", "sq_sum"), (tmp_a, "sqw_done", "sqw_sum"))[:1 + weighted]):
                        if n > 0 and k == 0:
                            pe.wait_ge(S[summed], 1 if w else n)
                        else:
                            pe.wait_ge(S[done], (0 if w else KT * n) + k + 1)
                        for t in range(TT):
                            ins = mm(aux[:, 2, w * TT + t:w * TT + t + 1], sq[:, k, t * P:t * P + P], avg_d[:, 0:1],
                                     start=k + w + t == 0, stop=k == KT - 1, skip_group_check=True)
                if KT - 1 in ks:
                    ins.then_inc(S["ms_mm"], 1)

            def row_of(n):
                pe.wait_ge(S["rs_done"], n + 1)
                mm(aux[:, 3, 0:T], ones[:], flat(diag[:]), start=True, stop=True).then_inc(S["rs_mm"], 1)

            def mod_sum(dst, acc):
                for nt in range(NT):
                    ins = mm(dst[:, nt:nt + 1], acc[:, nt * P:nt * P + P], ones[:, 0:1], start=True, stop=True)
                ins.then_inc(S["mod_mm"], 1)

            pe.wait_ge(S["ready"], N_READY)
            pe.wait_ge(taken, SLOTS)
            mod_sum(aux[:, 1, 0:4], mod_acc[:, 0])
            mean_square(0, range(KT))
            pe.wait_ge(S["pool_sum"], 1)
            mod_sum(aux[:, 1, 4:8], mod_pool[:])
            pe.wait_ge(S["spare_used"], SLOTS)
            mod_sum(aux[:, 1, 8:12], mod_acc[:, 1])
            row_of(0)
            pe.wait_ge(S["spare_used"], 2 * SLOTS)
            mod_sum(aux[:, 1, 12:16], mod_acc[:, 0])
            for j in range(2):
                chunk_tokens(GROUP["v"] + j, j, (S["nrm_lo"], 0))
            pe.wait_ge(S["narrow_ok"], 1)
            for t in range(TT):
                for k in range(KT):
                    xh, xl = (a[:, k, t * P:t * P + P] for a in (act_hi, act_lo))
                    dst = aux[:, 0, t * HEADS:t * HEADS + HEADS]
                    mm(dst, xh, wdt_hi[:, k], start=k == 0, stop=False)
                    mm(dst, xh, wdt_lo[:, k], start=False, stop=False)
                    ins = mm(dst, xl, wdt_hi[:, k], start=False, stop=k == KT - 1)
            ins.then_inc(S["dt_mm"], 1)
            pe.wait_ge(evac_act, 1)
            chunk(GROUP["u"], 0)
            pe.wait_ge(S["dt_ok"], 1)
            pe.wait_ge(S["early_in"], 32)
            mm(aux[:, 1, 0:HEADS], after, dts[:, 1, 0], start=True, stop=True).then_inc(S["wend_mm"], 1)
            pe.wait_ge(evac_act, 2)
            chunk(GROUP["u"] + 1, 1)
            pe.wait_ge(S["v_ready"], 2)
            pe.wait_ge(S["ws_masked"], 1)
            pe.wait_ge(S["wend_ok"], 1)
            for g in range(GROUPS_SGU):
                for c in range(TT):
                    ins = mm(aux[:, g // 2, (g % 2) * T + c * P:(g % 2) * T + c * P + P], v_sb[:, c, g * P:g * P + P],
                             wst[:, g], start=True, stop=True)
                if g % 2:
                    ins.then_inc(S["sgu_mm"], 1)
            with pe.Fori(0, 4) as i:
                for par in range(2):
                    c = i * 2 + par
                    pe.wait_ge(evac_act, c + (EVAC_XBC - 1))
                    chunk(c + GROUP["xbc"], par, c + landed_group(GROUP["xbc"]))
            zg0 = landed_group(GROUP["zg"])
            pe.wait_ge(evac_act, EVAC_ZG - 1)
            chunk(GROUP["zg"], 0)
            pe.wait_ge(S["sgu_y"], 1)

            def group_sum(g):
                last = isinstance(g, int) and g == SSD_GROUPS - 1
                if last:
                    pe.wait_ge(S["g2_ok"], g + 1)
                else:
                    pe.wait_ge(S["gsq_ok"], g + 1)
                pe.wait_ge(S["gs_ok"], g + 1)
                for k in range(1 + last):
                    for t in range(TT):
                        ins = mm(aux[:, 1, 3 * P + t:3 * P + t + 1], g_sq[:, k, t * P:t * P + P], avg_g[:, 0:1],
                                 start=k + t == 0, stop=k == last, skip_group_check=True)
                ins.then_inc(S["gs_mm"], 1)

            def ssd(g, par, first=False, last=False):
                x_hi, x_lo = (ya_hi, ya_lo) if last else (act_hi, act_lo)
                zg_panel = lambda s: panel(g + (GROUP["zg"] + 1), s, 1 - par, x_hi, x_lo, 2 * s, s == 0, s == SLOTS - 1,
                                           g * 2 + (zg0 + 1))
                x, b, c_t = stg[:, par, 0:2], stg[:, par, 2], stg[:, par, 3]
                pe.wait_ge(evac_act, g + EVAC_ZG)
                if last:
                    pe.wait_ge(S["sgu_done"], 1)
                zg_panel(0)
                pe.wait_ge(S["stg_ok"], g + 1)
                pe.wait_ge(S["ecum_ok"], g + 1)
                for c in range(2):
                    for pair in range(2):
                        ins = nc.tensor.transpose(aux[:, 0, c * T + pair * P:c * T + pair * P + P], x[:, pair, c * P:c * P + P], ident)
                ins.then_inc(S["t_mm"], 1)
                pe.wait_ge(S["state_ok"], g + 1)
                nc.tensor.transpose(aux[:, 1, T:T + P], b[:, 0:P], ident)
                for c in range(2):
                    ins = mm(aux[:, 1, c * P:c * P + P], b[:, c * P:c * P + P], c_t[:, c * P:c * P + P], start=True, stop=True)
                ins.then_inc(S["cb_mm"], 1)
                for c in range(2):
                    pe.wait_ge(S["upto_ok"], g * 2 + (c + 1))
                    if c == 0:
                        pe.wait_ge(S["y_ok"], g + 2)
                    else:
                        pe.wait_ge(S["mod_done"], g + MOD_FIRST)
                    mm(aux[:, 2 + c], after_r[:], flat(a_upto_hi[:, c]), start=True, stop=False)
                    mm(aux[:, 2 + c], after_r[:], flat(a_upto_lo[:, c]), start=False, stop=True).then_inc(S["seg_mm"], 1)
                zg_panel(1)
                pe.wait_ge(S["xdt_ok"], g + 1)
                mm(aux[:, 0], ones_r[:], flat(a_upto_hi[:, 1]), start=True, stop=False)
                mm(aux[:, 0], ones_r[:], flat(a_upto_lo[:, 1]), start=False, stop=True).then_inc(S["cum_mm"], 1)
                zg_panel(2)
                pe.wait_ge(S["xw_ok"], g + 1)
                pe.wait_ge(S["btok_ok"], g + 1)
                pe.wait_ge(S["cbm_ok"], g + 1)
                if not first:
                    group_sum(g - 1)
                mm(aux[:, 1, 0:T], b_tok[:], xw[:], start=True, stop=True).then_inc(S["st_mm"], 1)
                y = lambda h, c: aux[64 * (h % 2):64 * (h % 2) + 64, 2, (h // 2) * T + c * P:(h // 2) * T + c * P + P]
                pe.wait_ge(S["m_ok"], g * 2 + 1)
                for h in range(HPG):
                    mm(y(h, 0), xdt[:, 0, 64 * h:64 * h + 64], decay[:, 0, h], start=True, stop=True)
                zg_panel(3)
                pe.wait_ge(S["m_ok"], g * 2 + 2)
                pe.wait_ge(S["state_ok"], g + 2)
                pe.wait_ge(S["cin_ok"], g + 1)
                for h in range(HPG):
                    mm(y(h, 1), xdt[:, 1, 64 * h:64 * h + 64], decay[:, 1, h], start=True, stop=False)
                    ins = mm(y(h, 1), state[:, 64 * h:64 * h + 64], c_in[:, h], start=False, stop=True)
                ins.then_inc(S["y_mm"], 1)
                pe.wait_ge(taken, g * (2 * SLOTS) + (zg0 + 3) * SLOTS)
                mod_sum(aux[:, 3, 0:4], mod_acc[:, par])

            pe.wait_ge(S["sums_ok"], 1)
            ssd(0, 0, first=True)
            with pe.Fori(0, 3) as i:
                ssd(i * 2 + 1, 1)
                ssd(i * 2 + 2, 0)
            ssd(7, 1, last=True)
            pe.wait_ge(evac_act, EVAC_ZG + 8)
            for s in range(SLOTS):
                panel(GROUP["gm"] + 1, s, 1, ya_hi, ya_lo, 2 * s, s == 0, s == SLOTS - 1)
                if s == 0:
                    group_sum(7)
                for q in ((), (), (0, 1), (2, 3))[s]:
                    pe.wait_ge(S["gdiag_ok"], q + 1)
                    pe.wait_ge(*((S["ecum_ok"], 9), (S["gs_ok"], 9), (S["y_ok"], 10), (S["mod_done"], 12))[q])
                    mm(aux[:, q], ones[:], flat(g_diag[:, q]), start=True, stop=True).then_inc(S["grow_mm"], 1)
            for j in range(2):
                pe.wait_ge(evac_dve, j + 1)
                for g in range(2):
                    for s in range(SLOTS):
                        q = (8 * g + 2 * s) // 4
                        if q == 0:
                            pe.wait_ge(S["yb0_ok"], 1)
                        else:
                            pe.wait_ge(S["yb_ok"], q)
                        panel(GROUP["ssm"] + 2 * j + g, s, j, yb_hi, yb_lo, 8 * g + 2 * s, g == 0 and s == 0, g == 1 and s == 3)
            for j in range(2):
                pe.wait_ge(evac_dve, 3 + j)
                for s in range(SLOTS):
                    pe.wait_ge(S["mix_ok"], s // 2 + 1)
                    panel(GROUP["out"] + j, s, j, act_hi, act_lo, 2 * s, s == 0, s == 3)
            mean_square(1, (0, 4, 5, 6, 7))
            row_of(1)
            pe.wait_ge(S["res_ok"], RES_OUT + KT)
            with pe.Fori(0, 4) as i:
                for par in range(2):
                    c = i * 2 + par
                    pe.wait_ge(evac_act, c + (EVAC_FF1 - 1))
                    chunk(c + GROUP["ff1"], par, c + landed_group(GROUP["ff1"]), (S["nrm_lo"], KT))
            for j in range(2):
                pe.wait_ge(evac_act, EVAC_FF1 + 7 + j)
                for g in range(4):
                    for s in range(SLOTS):
                        pe.wait_ge(S["ff_ok"], (8 * g + 2 * s) // 4 + 1)
                        panel(GROUP["ff2"] + 4 * j + g, s, j, ff_hi, ff_lo, 8 * g + 2 * s, g == 0 and s == 0, g == 3 and s == 3)
                        if (j, g, s) == (1, 1, 0):
                            mean_square(2, (0,), True)
            mean_square(2, (4, 5, 6, 7), True)
            row_of(2)
            i2 = GROUP["in2"]
            pe.wait_ge(S["res_ok"], RES_FF2 + KT)
            ready2 = (S["nrm_lo"], 2 * KT)
            chunk(i2, 0, x_ready=ready2)
            pe.wait_ge(S["narrow_ok"], 2)
            for k in range(KT):
                dst = aux[0:16, 0, 0:T]
                mm(dst, wglr_hi[:, k], act_hi[:, k], start=k == 0, stop=False)
                mm(dst, wglr_hi[:, k], act_lo[:, k], start=False, stop=False)
                ins = mm(dst, wglr_lo[:, k], act_hi[:, k], start=False, stop=k == KT - 1)
            ins.then_inc(S["glr_mm"], 1)
            row_of(3)
            panel(i2 + 1, 0, 1, act_hi, act_lo, 0, True)
            pe.wait_ge(S["glr_ok"], 1)
            pe.wait_ge(S["late_in"], 80)
            for t in range(2):
                ins = mm(aux[:, 1, t * T:t * T + T], wgu[:, t * P:t * P + P], glr_sb[:], start=True, stop=True)
            ins.then_inc(S["gate_mm"], 1)
            for s in range(1, SLOTS):
                panel(i2 + 1, s, 1, act_hi, act_lo, 2 * s, False, s == 3)

            def level_mm(l):
                if l == 0:
                    pe.wait_ge(S["gx_abs"], 1)
                else:
                    pe.wait_ge(S["lev_x"], l)
                if l >= 2:
                    pe.wait_ge(S["lev_ok"], l - 1)
                bank = 2 * (l % 2)
                for t in range(1 if l == 8 else TT):
                    for h in range(GLA_HEADS):
                        rows, pair = slice(64 * (h % 2), 64 * (h % 2) + 64), h // 2
                        if l == 0:
                            keys, queries = (gqk[rows, a + pair, t * P:t * P + P] for a in (2, 0))
                        elif l == 8:
                            keys, queries = (gx[rows, (l - 1) % 2, pair * T + a * P:pair * T + a * P + P] for a in (0, 1))
                        else:
                            keys = queries = gx[rows, (l - 1) % 2, pair * T + t * P:pair * T + t * P + P]
                        at_col = (2 * t + pair) * P
                        ins = mm(aux[:, bank + h % 2, at_col:at_col + P], keys, queries, start=True, stop=True)
                ins.then_inc(S["lev_mm"], 1)

            for c in range(2):
                pe.wait_ge(evac_act, EVAC_IN2 + 1 + c)
                for s in range(SLOTS):
                    panel(i2 + 2 + c, s, c, act_hi, act_lo, 2 * s, s == 0, s == 3)
                    level_mm(4 * c + s)
            pe.wait_ge(evac_act, EVAC_IN2 + 3)
            for s in range(SLOTS):
                token_panel(i2 + 4, s, 0)
                if s == 0:
                    level_mm(8)
                if s < 2:
                    pe.wait_ge(S["lev_ok"], 8 + s)
                    for nt in range(NT):
                        ins = mm(aux[:, 2 - 2 * s + nt // 2, (nt % 2) * T:(nt % 2) * T + T], turn, (q_sb, k_sb)[s][:, nt],
                                 start=True, stop=True)
                    ins.then_inc(S["turn_mm"], 1)

            def unit(w):
                return (0, range(w, MOBA_HEADS, 2)) if w < 2 else (1, range(w % 2 + 4 * (w // 2 - 1), 4 * (w // 2), 2))

            def moba_scores(w):
                tile, heads = unit(w)
                if w == 0:
                    pe.wait_ge(S["rope_ok"], 2)
                else:
                    pe.wait_ge(S["max_ok"], w)
                for i, h in enumerate(heads):
                    rows = slice(64 * (h % 2), 64 * (h % 2) + 64)
                    n = P * (tile + 1)
                    ins = mm(aux[:, 0, i * n:i * n + n], q_sb[rows, h // 2, tile * P:tile * P + P],
                             k_sb[rows, h // 2, 0:n], start=True, stop=True)
                ins.then_inc(S["sc_mm"], 1)

            def moba_turn(w):
                pe.wait_ge(S["p_ok"], w + 1)
                need(pe, S["pt_ok"], w)
                for b in range(4):
                    ins = nc.tensor.transpose(aux[:, 1, b * P:b * P + P], prob[:, w, b * P:b * P + P], ident)
                ins.then_inc(S["pt_mm"], 1)

            def moba_values(w):
                tile, heads = unit(w)
                pe.wait_ge(S["pt_ok"], w + 1)
                b = 0
                for h in heads:
                    at_h = (h // 2 % 2) * T + tile * P
                    for kt in range(tile + 1):
                        ins = mm(aux[64 * (h % 2):64 * (h % 2) + 64, 2 + h // 4, at_h:at_h + P],
                                 mv_sb[:, kt, 64 * h:64 * h + 64], prob_t[:, w, b * P:b * P + P],
                                 start=kt == 0, stop=kt == tile)
                        b += 1
                if w in (3, 5):
                    ins.then_inc(S["ym_mm"], 1)

            o2 = GROUP["out2"]

            def out2_panel(n):
                j, k0 = OUT2_PANELS[n]
                panel(o2 + n // SLOTS, n % SLOTS, j, mix_hi, mix_lo, k0, k0 == 0, k0 == 6)

            pe.wait_ge(evac_act, EVAC_IN2 + 4)
            for w in range(2 * SLOTS):
                if w < SLOTS:
                    token_panel(i2 + 5, w, 1)
                else:
                    if w == SLOTS:
                        pe.wait_ge(S["gla_ok"], 1)
                        pe.wait_ge(evac_act, EVAC_IN2 + 6)
                    out2_panel(w - SLOTS)
                if w == 2:
                    pe.wait_ge(S["og_diag"], 1)
                    for b in range(2):
                        ins = mm(proj_ps[:, 0, b * 512:b * 512 + 512], ones[:], flat(og2[:, 2 * b:2 * b + 2]), start=True, stop=True)
                    ins.then_inc(S["og_row"], 1)
                if w < UNITS:
                    moba_scores(w)
                if w == 0:
                    pe.wait_ge(evac_act, EVAC_IN2 + 5)
                    pe.wait_ge(S["lev_ok"], 9)
                    for h in range(GLA_HEADS):
                        dst = proj_ps[:, 0, h * T:h * T + T]
                        at_h = (h % 2) * 2 + h // 2
                        mm(dst[:, 0:P], gv_sb[:, 0, h * P:h * P + P], scores_t[:, 0, at_h], start=True, stop=True)
                        mm(dst[:, P:T], gv_sb[:, 1, h * P:h * P + P], scores_t[:, 1, at_h], start=True, stop=False)
                        ins = mm(dst[:, P:T], gv_sb[:, 0, h * P:h * P + P], scores_t[:, 2, at_h], start=False, stop=True)
                    ins.then_inc(S["og_mm"], 1)
                if w == 1:
                    pe.wait_ge(S["og_sq"], 1)
                    for h in range(GLA_HEADS):
                        for t in range(TT):
                            ins = mm(proj_ps[:, 0, h * TT + t:h * TT + t + 1], og2[:, h, t * P:t * P + P], avg_v[:, 0:1],
                                     start=True, stop=True)
                    ins.then_inc(S["og_ms"], 1)
                if 1 <= w <= UNITS:
                    moba_turn(w - 1)
                for v in ((), (), (), (), (0, 1), (2, 3), (4,), (5,))[w]:
                    moba_values(v)
            for n in range(4, 8):
                pe.wait_ge(S["ym_ok"], n % 2 + 1)
                out2_panel(n)
            mean_square(3, (0, 4, 5, 6, 7))
            row_of(4)
            pe.wait_ge(S["res_ok"], RES_OUT2 + KT)

            def up_chunk(c, par):
                pe.wait_ge(evac_act, c + (EVAC_UP - 1))
                chunk(c + GROUP["up"], par, c + landed_group(GROUP["up"]), (S["nrm_lo"], 3 * KT))

            up_chunk(0, 0)
            with pe.Fori(0, 5) as i:
                up_chunk(i * 2 + 1, 1)
                up_chunk(i * 2 + 2, 0)
            for j in range(2):
                par = (j + 1) % 2
                pe.wait_ge(evac_act, EVAC_UP + 10 + j)
                for g in range(3):
                    for s in range(SLOTS):
                        n = g * SLOTS + s
                        if n == 11:
                            continue
                        pe.wait_ge(S["glu_ok"], n + 1)
                        panel(GROUP["down"] + 3 * j + g, s, par, glu_hi, glu_lo, 2 * n, n == 0, n == 10, release=1 + (n == 10))
                        if (j, n) == (1, 4):
                            mean_square(4, (0,))
            mean_square(4, (4, 5, 6, 7))
            row_of(5)



def kernel(**inputs):
    import numpy as np
    import concourse.bacc as bacc
    from concourse.bass_utils import run_bass_kernel_spmd

    w = {k: np.asarray(v) for k, v in inputs.items()}

    def panels_of(m):
        rows, n = m.shape
        return m.reshape(rows // 256, 2, P, n // 512, 512).transpose(3, 0, 2, 1, 4).reshape(-1, P, 1024)

    w_in, w_mod = w["w_in"][0], panels_of(w["w_mod"][0])
    u0, v0, z0, x0, dt0, g0 = 0, 1024, 2048, 4096, 8192, 8224
    z_gates = panels_of(np.concatenate([w_in[:, z0:x0], w_in[:, g0:g0 + 2048]], 1)).reshape(8, 4, P, 1024)
    gm_in, mod_in = panels_of(w["w_branch_gm"][0]), w_mod[16:].reshape(8, 4, P, 1024)
    beside_mod = np.concatenate([z_gates[1:], gm_in[None, :4]], 0)
    alternate = np.stack([beside_mod, mod_in], 1).reshape(-1, P, 1024)
    w2 = w["w_in_2"][0]
    in2 = np.concatenate([w2[:, 1536:2048], w2[:, 0:512], w2[:, 512:1024], w2[:, 2560:3072], w2[:, 2048:2560],
                          w2[:, 1024:1536]], 1)
    out2 = np.concatenate([w["w_out_2"][0][512:], w["w_out_2"][0][:512]], 0)
    half = GLU_TILES * P

    def glu_order(a):
        lead = a.shape[:-1]
        return np.moveaxis(a.reshape(lead + (2, GLU_TILES // 2, 2 * P)), -3, -2).reshape(lead + (2 * half,))

    down = np.concatenate([w["w_ffn_down_2"][0], np.zeros((256, D), np.float32)], 0)
    stream = np.concatenate([
        w_mod[:16], panels_of(w_in[:, v0:z0]), panels_of(w_in[:, u0:v0]), panels_of(w_in[:, x0:dt0]), z_gates[0], alternate,
        gm_in[4:], panels_of(w["w_branch_ssm"][0]), panels_of(w["w_out"][0]),
        panels_of(w["w_ff1"][0]), panels_of(w["w_ff2"][0]), panels_of(in2), panels_of(out2)[[4 * j + k // 2 for j, k in OUT2_PANELS]],
        panels_of(glu_order(w["w_ffn_up_2"][0])), panels_of(down)], 0)

    def tiles(v):
        return np.ascontiguousarray(v.reshape(-1, P).T)

    def taps(m):
        return m.reshape(m.shape[0], -1, P).transpose(2, 1, 0).reshape(P, -1)

    parts = {
        "b_mod": tiles(w["b_mod"][0]), "conv_w": taps(w["conv_w"][0]), "conv_b": tiles(w["conv_b"][0]),
        "gm_norm_w": tiles(w["gm_norm_w"][0]), "ssm_norm_w": tiles(w["ssm_norm_w"][0]),
        "d_skip": tiles(np.repeat(w["d_skip"][0], 64)), "final_norm_w": tiles(w["final_norm_w"]), "c": tiles(w["c"][0]),
        "attn_g": tiles(w["attn_norm_g_2"][0]), "b_gate": tiles(w["b_gate_2"][0]), "gla_g": tiles(w["gla_norm_g_2"][0].reshape(-1)),
        "ffn_g": tiles(w["ffn_norm_g_2"][0]), "fconv_w": taps(glu_order(w["conv_w_2"][0])),
        "fconv_b": tiles(glu_order(w["conv_b_2"][0])), "final_g": tiles(w["final_norm_g_2"]),
        "dt_bias": np.broadcast_to(w["dt_bias"][0], (P, HEADS)), "a_log": np.broadcast_to(w["a_log"][0], (P, HEADS)),
    }
    table = np.concatenate([parts[n] for n, _ in _WIDTHS], 1)

    r = np.arange(P)
    turn = np.zeros((P, P), np.float32)
    lower = r % 64 < 32
    turn[r[lower] + 32, r[lower]] = -1.0
    turn[r[~lower] - 32, r[~lower]] = 1.0
    square = np.stack([(r[:, None] <= r[None, :]), (r[:, None] > r[None, :]), np.eye(P), turn], 1).astype(np.float32)
    inv_freq = (1.0 / (np.float32(10000.0) ** (np.arange(0, 64, 2, dtype=np.float32) / np.float32(64)))).astype(np.float32)
    angle = np.arange(T, dtype=np.float32)[None, :] * inv_freq[r % 32][:, None]
    rope = np.stack([np.cos(angle), np.sin(angle)], 1).astype(np.float32)
    levels = [r[:, None] == r[None, :]]
    for m in LEVELS:
        levels.append((r[:, None] // (2 * m) == r[None, :] // (2 * m)) & (r[:, None] % (2 * m) < m) & (r[None, :] % (2 * m) >= m))
    levels = np.stack(levels, 1).astype(np.float32)
    neg = np.zeros((P, 2, P), np.float32)
    neg[:, 1] = np.where(r[None, :] <= r[:, None], 0.0, NEG)

    def by_row_tile(m):
        return m.reshape(KT, P, -1).transpose(1, 0, 2)

    arrays = {
        "panels": stream, "x_t": by_row_tile(w["x"][0].T), "cols": table, "square": square,
        "ws_t": w["gm_ws"][0].transpose(2, 0, 1), "bs_rows": np.broadcast_to(w["gm_bs"][0], (P, GROUPS_SGU, P)),
        "wdt": by_row_tile(w_in[:, dt0:g0]), "wglr": by_row_tile(w2[:, 3072:3088]), "wgu": w["w_gate_up_2"][0],
        "rope": rope, "levels": levels, "neg": neg,
    }
    nc = bacc.Bacc("TRN2", target_bir_lowering=False, num_devices=1)
    arrays = {"in_" + n: np.ascontiguousarray(a) for n, a in arrays.items()}
    args = [nc.dram_tensor(n, a.shape, F32, kind="ExternalInput").ap() for n, a in arrays.items()]
    out = nc.dram_tensor("out_t", (P, KT, T), F32, kind="ExternalOutput").ap()
    two_blocks(nc, *args, out)
    got = run_bass_kernel_spmd(nc, [arrays], core_ids=[0]).results[0]["out_t"]
    return np.ascontiguousarray(np.asarray(got).transpose(1, 0, 2).reshape(D, T).T)[None]
```
